# Optimizing a Trainium2 kernel written in Bass

```python
import jax
import jax.numpy as jnp
from jax import lax
import numpy as np

D_MODEL = 2048
BATCH = 1
SEQ = 256
DEPTH = 1

EPS = 1e-6
ROPE_THETA = 10000.0
NEG = -1e30
BIG = 1e9

HG_HEADS = 8
HG_KDIM = 128
HG_VDIM = 128
HG_QK = HG_HEADS * HG_KDIM
HG_WIDTH = HG_HEADS * HG_VDIM
HG_CHUNK = 64

NSA_HEADS = 16
NSA_KV_GROUPS = 4
NSA_HEAD_DIM = 64
NSA_WIDTH = NSA_HEADS * NSA_HEAD_DIM
NSA_KV = NSA_KV_GROUPS * NSA_HEAD_DIM
CMP_BLOCK = 32
CMP_STRIDE = 16
CMP_HIDDEN = 256
SLC_BLOCK = 64
SLC_TOPK = 16
SLC_LOCAL = 2
WIN = 512
NSA_Q_BLOCK = 64

D_MIX = HG_WIDTH + NSA_WIDTH
IN_SIZES = (HG_QK, HG_QK, HG_WIDTH, HG_WIDTH, NSA_WIDTH, NSA_KV, NSA_KV, NSA_KV, NSA_KV, NSA_KV, NSA_KV, 3 * NSA_HEADS)
IN_COLS = sum(IN_SIZES)

MOE_GROUPS = 4
MOE_EXPERTS_PER_GROUP = 8
N_EXPERTS = MOE_GROUPS * MOE_EXPERTS_PER_GROUP
MOE_TOPK = 2
EXPERT_FF = 512
MOE_BLOCK = 128

kernel_name = 'hymba_hgrn2_nsa_hier_moe'

def rmsnorm(x, gain):
    xf = x.astype(jnp.float32)
    y = xf * lax.rsqrt(jnp.mean(xf * xf, axis=-1, keepdims=True) + EPS)
    return (y * gain.astype(jnp.float32)).astype(x.dtype)

def rope_tables(seq, dim):
    inv = 1.0 / (ROPE_THETA ** (jnp.arange(0, dim, 2, dtype=jnp.float32) / dim))
    ang = jnp.arange(seq, dtype=jnp.float32)[:, None] * inv[None, :]
    return jnp.cos(ang), jnp.sin(ang)

def apply_rope(x, cos, sin):
    x1, x2 = jnp.split(x.astype(jnp.float32), 2, axis=-1)
    c, s = cos[None, :, None, :], sin[None, :, None, :]
    return jnp.concatenate([x1 * c - x2 * s, x2 * c + x1 * s], axis=-1).astype(x.dtype)

def hgrn2_mixer(q, f_raw, i, g, lb, out_gain):
    B, S, _ = q.shape
    C = HG_CHUNK
    nc = S // C
    f = lb + (1.0 - lb) * jax.nn.sigmoid(f_raw.astype(jnp.float32))
    log_f = jnp.log(f)
    k = 1.0 - f

    def chunks(t, d):
        return t.astype(jnp.float32).reshape(B, nc, C, HG_HEADS, d).transpose(1, 0, 3, 2, 4)

    xs = (chunks(q, HG_KDIM) * HG_KDIM ** -0.5, chunks(k, HG_KDIM), chunks(i, HG_VDIM), chunks(log_f, HG_KDIM))
    causal = jnp.tril(jnp.ones((C, C), dtype=bool))[:, :, None]

    def step(state, inp):
        qb, kb, vb, lfb = inp
        bcum = jnp.cumsum(lfb, axis=2)
        diff = bcum[:, :, :, None, :] - bcum[:, :, None, :, :]
        decay = jnp.exp(jnp.where(causal, diff, -jnp.inf))
        scores = jnp.einsum('bhtk,bhtsk->bhts', qb, decay * kb[:, :, None, :, :])
        o = jnp.einsum('bhts,bhsv->bhtv', scores, vb) + jnp.einsum('bhtk,bhkv->bhtv', qb * jnp.exp(bcum), state)
        blast = bcum[:, :, -1:, :]
        state = jnp.exp(blast[:, :, 0, :])[..., None] * state + jnp.einsum('bhsk,bhsv->bhkv', kb * jnp.exp(blast - bcum), vb)
        return state, o

    s0 = jnp.zeros((B, HG_HEADS, HG_KDIM, HG_VDIM), jnp.float32)
    _, ys = lax.scan(step, s0, xs)
    o = ys.transpose(1, 0, 3, 2, 4).reshape(B, S, HG_HEADS, HG_VDIM)
    gate = jax.nn.silu(g.astype(jnp.float32)).reshape(B, S, HG_HEADS, HG_VDIM)
    o = rmsnorm(o, out_gain) * gate
    return o.reshape(B, S, HG_WIDTH).astype(q.dtype)

def compress_blocks(kv, pos, w1, w2):
    B, S, G, dk = kv.shape
    n_cmp = (S - CMP_BLOCK) // CMP_STRIDE + 1
    idx = np.arange(n_cmp)[:, None] * CMP_STRIDE + np.arange(CMP_BLOCK)[None, :]
    blk = kv[:, idx] + pos[None, None, :, None, :]
    flat = blk.transpose(0, 1, 3, 2, 4).reshape(B, n_cmp, G, CMP_BLOCK * dk)
    return jax.nn.gelu(flat @ w1) @ w2

def nsa_mixer(q, k_cmp, v_cmp, k_slc, v_slc, k_win, v_win, gate_raw,
              cmp_pos_k, cmp_w1_k, cmp_w2_k, cmp_pos_v, cmp_w1_v, cmp_w2_v, cos, sin):
    B, S, _ = q.shape
    H, G, dk = NSA_HEADS, NSA_KV_GROUPS, NSA_HEAD_DIM
    R = H // G
    Qb = NSA_Q_BLOCK
    scale = dk ** -0.5
    q = q.reshape(B, S, H, dk)
    q_rot = apply_rope(q, cos, sin)
    k_cmp, v_cmp, v_slc, v_win = [t.reshape(B, S, G, dk) for t in (k_cmp, v_cmp, v_slc, v_win)]
    k_slc = apply_rope(k_slc.reshape(B, S, G, dk), cos, sin)
    k_win = apply_rope(k_win.reshape(B, S, G, dk), cos, sin)

    kc = compress_blocks(k_cmp, cmp_pos_k, cmp_w1_k, cmp_w2_k)
    vc = compress_blocks(v_cmp, cmp_pos_v, cmp_w1_v, cmp_w2_v)
    n_cmp = kc.shape[1]
    cmp_end = jnp.arange(n_cmp) * CMP_STRIDE + CMP_BLOCK - 1

    n_slc = S // SLC_BLOCK
    topk = min(SLC_TOPK, n_slc)
    ci = np.arange(n_cmp)[:, None]
    sj = np.arange(n_slc)[None, :]
    overlap = (ci * CMP_STRIDE < (sj + 1) * SLC_BLOCK) & (ci * CMP_STRIDE + CMP_BLOCK > sj * SLC_BLOCK)
    agg = jnp.asarray(overlap, jnp.float32)
    kb = k_slc.reshape(B, n_slc, SLC_BLOCK, G, dk).transpose(0, 3, 1, 2, 4)
    vb = v_slc.reshape(B, n_slc, SLC_BLOCK, G, dk).transpose(0, 3, 1, 2, 4)
    blk_j = jnp.arange(n_slc)
    b_ix = jnp.arange(B)[:, None, None, None]
    g_ix = jnp.arange(G)[None, :, None, None]

    kw = jnp.pad(k_win, ((0, 0), (WIN, 0), (0, 0), (0, 0)))
    vw = jnp.pad(v_win, ((0, 0), (WIN, 0), (0, 0), (0, 0)))
    gates = jax.nn.sigmoid(gate_raw.astype(jnp.float32)).reshape(B, S, H, 3)

    def heads_by_group(t):
        return t.reshape(B, Qb, G, R, t.shape[-1]).transpose(0, 2, 3, 1, 4)

    def block(qs):
        t = qs + jnp.arange(Qb)
        qr = heads_by_group(lax.dynamic_slice_in_dim(q, qs, Qb, 1)).astype(jnp.float32)
        qo = heads_by_group(lax.dynamic_slice_in_dim(q_rot, qs, Qb, 1)).astype(jnp.float32)

        m_c = cmp_end[None, :] <= t[:, None]
        s_c = jnp.einsum('bgrqd,bcgd->bgrqc', qr, kc) * scale
        p_c = jax.nn.softmax(jnp.where(m_c, s_c, NEG), axis=-1) * m_c
        o_c = jnp.einsum('bgrqc,bcgd->bgrqd', p_c, vc)

        imp = jnp.einsum('bgrqc,cj->bgqj', p_c, agg)
        cur = t // SLC_BLOCK
        dj = cur[:, None] - blk_j[None, :]
        forced = (blk_j[None, :] == 0) | ((dj >= 0) & (dj < SLC_LOCAL))
        causal_blk = blk_j[None, :] * SLC_BLOCK <= t[:, None]
        imp = jnp.where(forced, BIG, jnp.where(causal_blk, imp, -BIG))
        _, idx = lax.top_k(imp, topk)
        kg = kb[b_ix, g_ix, idx]
        vg = vb[b_ix, g_ix, idx]
        pos = idx[..., None] * SLC_BLOCK + jnp.arange(SLC_BLOCK)
        m_s = (pos <= t[None, None, :, None, None])[:, :, None]
        s_s = jnp.einsum('bgrqd,bgqnld->bgrqnl', qo, kg) * scale
        s_s = jnp.where(m_s, s_s, NEG).reshape(B, G, R, Qb, topk * SLC_BLOCK)
        p_s = jax.nn.softmax(s_s, axis=-1).reshape(B, G, R, Qb, topk, SLC_BLOCK)
        o_s = jnp.einsum('bgrqnl,bgqnld->bgrqd', p_s, vg)

        kwin = lax.dynamic_slice_in_dim(kw, qs, WIN + Qb, 1)
        vwin = lax.dynamic_slice_in_dim(vw, qs, WIN + Qb, 1)
        kpos = qs - WIN + jnp.arange(WIN + Qb)
        dlt = t[:, None] - kpos[None, :]
        m_w = (dlt >= 0) & (dlt < WIN) & (kpos[None, :] >= 0)
        s_w = jnp.einsum('bgrqd,bkgd->bgrqk', qo, kwin) * scale
        p_w = jax.nn.softmax(jnp.where(m_w, s_w, NEG), axis=-1)
        o_w = jnp.einsum('bgrqk,bkgd->bgrqd', p_w, vwin)

        gq = heads_by_group(lax.dynamic_slice_in_dim(gates, qs, Qb, 1))
        o = gq[..., 0:1] * o_c + gq[..., 1:2] * o_s + gq[..., 2:3] * o_w
        return o.transpose(0, 3, 1, 2, 4).reshape(B, Qb, H * dk)

    out = lax.map(block, jnp.arange(S // Qb) * Qb)
    return out.transpose(1, 0, 2, 3).reshape(B, S, NSA_WIDTH).astype(q.dtype)

def hier_moe(x, w_group, b_group, w_router, b_router, w_gate, w_up, w_down):
    B, S, D = x.shape
    n_tok = B * S
    xt = x.reshape(n_tok, D)
    g_prob = jax.nn.softmax((xt @ w_group).astype(jnp.float32) + b_group.astype(jnp.float32), axis=-1)
    g_sel = jnp.argmax(g_prob, axis=-1)
    g_w = jnp.take_along_axis(g_prob, g_sel[:, None], axis=-1)
    e_logits = ((xt @ w_router).astype(jnp.float32) + b_router.astype(jnp.float32)).reshape(n_tok, MOE_GROUPS, MOE_EXPERTS_PER_GROUP)
    e_in = jnp.take_along_axis(e_logits, g_sel[:, None, None], axis=1)[:, 0]
    e_val, e_loc = lax.top_k(e_in, MOE_TOPK)
    e_w = jax.nn.softmax(e_val, axis=-1) * g_w
    e_id = g_sel[:, None] * MOE_EXPERTS_PER_GROUP + e_loc

    n_asg = n_tok * MOE_TOPK
    flat_e = e_id.reshape(n_asg).astype(jnp.int32)
    flat_t = jnp.repeat(jnp.arange(n_tok, dtype=jnp.int32), MOE_TOPK)
    flat_w = e_w.reshape(n_asg)
    order = jnp.argsort(flat_e)
    se, st, sw = flat_e[order], flat_t[order], flat_w[order]
    counts = jnp.bincount(flat_e, length=N_EXPERTS)
    start = jnp.cumsum(counts) - counts
    padded = (counts + MOE_BLOCK - 1) // MOE_BLOCK * MOE_BLOCK
    pend = jnp.cumsum(padded)
    pstart = pend - padded
    dest = pstart[se] + (jnp.arange(n_asg) - start[se])
    n_blocks = (n_asg + MOE_BLOCK - 1) // MOE_BLOCK + N_EXPERTS
    buf_tok = jnp.zeros((n_blocks * MOE_BLOCK,), jnp.int32).at[dest].set(st)
    buf_w = jnp.zeros((n_blocks * MOE_BLOCK,), jnp.float32).at[dest].set(sw)
    block_e = jnp.minimum(jnp.searchsorted(pend, jnp.arange(n_blocks) * MOE_BLOCK, side='right'), N_EXPERTS - 1)

    def expert_block(args):
        tok, w, e = args
        xb = xt[tok]
        hid = jax.nn.silu(xb @ w_gate[e]) * (xb @ w_up[e])
        return (hid @ w_down[e]) * w[:, None].astype(xb.dtype)

    ys = lax.map(expert_block, (buf_tok.reshape(n_blocks, MOE_BLOCK), buf_w.reshape(n_blocks, MOE_BLOCK), block_e))
    out = jnp.zeros((n_tok, D), x.dtype).at[buf_tok].add(ys.reshape(-1, D))
    return out.reshape(B, S, D)

def setup_inputs(seed: int = 0) -> dict:
    key = jax.random.key(seed)
    ks = jax.random.split(key, 24)
    L = DEPTH

    def nrm(k, shape, scale):
        return jax.random.normal(k, shape, jnp.float32) * scale

    return {
        'x': nrm(ks[0], (BATCH, SEQ, D_MODEL), 1.0),
        'attn_norm': 1.0 + nrm(ks[1], (L, D_MODEL), 0.02),
        'w_in': nrm(ks[2], (L, D_MODEL, IN_COLS), D_MODEL ** -0.5),
        'hg_lb_logits': nrm(ks[3], (L + 1, HG_QK), 0.5),
        'hg_out_norm': 1.0 + nrm(ks[4], (L, HG_VDIM), 0.02),
        'cmp_pos_k': nrm(ks[5], (L, CMP_BLOCK, NSA_HEAD_DIM), 0.1),
        'cmp_w1_k': nrm(ks[6], (L, CMP_BLOCK * NSA_HEAD_DIM, CMP_HIDDEN), (CMP_BLOCK * NSA_HEAD_DIM) ** -0.5),
        'cmp_w2_k': nrm(ks[7], (L, CMP_HIDDEN, NSA_HEAD_DIM), CMP_HIDDEN ** -0.5),
        'cmp_pos_v': nrm(ks[8], (L, CMP_BLOCK, NSA_HEAD_DIM), 0.1),
        'cmp_w1_v': nrm(ks[9], (L, CMP_BLOCK * NSA_HEAD_DIM, CMP_HIDDEN), (CMP_BLOCK * NSA_HEAD_DIM) ** -0.5),
        'cmp_w2_v': nrm(ks[10], (L, CMP_HIDDEN, NSA_HEAD_DIM), CMP_HIDDEN ** -0.5),
        'nsa_out_norm': 1.0 + nrm(ks[11], (L, NSA_WIDTH), 0.02),
        'w_out': nrm(ks[12], (L, D_MIX, D_MODEL), D_MIX ** -0.5),
        'ffn_norm': 1.0 + nrm(ks[13], (L, D_MODEL), 0.02),
        'moe_w_group': nrm(ks[14], (L, D_MODEL, MOE_GROUPS), D_MODEL ** -0.5),
        'moe_b_group': nrm(ks[15], (L, MOE_GROUPS), 0.01),
        'moe_w_router': nrm(ks[16], (L, D_MODEL, N_EXPERTS), D_MODEL ** -0.5),
        'moe_b_router': nrm(ks[17], (L, N_EXPERTS), 0.01),
        'moe_w_gate': nrm(ks[18], (L, N_EXPERTS, D_MODEL, EXPERT_FF), D_MODEL ** -0.5),
        'moe_w_up': nrm(ks[19], (L, N_EXPERTS, D_MODEL, EXPERT_FF), D_MODEL ** -0.5),
        'moe_w_down': nrm(ks[20], (L, N_EXPERTS, EXPERT_FF, D_MODEL), EXPERT_FF ** -0.5),
        'final_norm': 1.0 + nrm(ks[21], (D_MODEL,), 0.02),
    }

def reference(x, attn_norm, w_in, hg_lb_logits, hg_out_norm, cmp_pos_k, cmp_w1_k, cmp_w2_k,
              cmp_pos_v, cmp_w1_v, cmp_w2_v, nsa_out_norm, w_out, ffn_norm, moe_w_group, moe_b_group,
              moe_w_router, moe_b_router, moe_w_gate, moe_w_up, moe_w_down, final_norm):
    S = x.shape[1]
    cos, sin = rope_tables(S, NSA_HEAD_DIM)
    lower_bounds = jnp.cumsum(jax.nn.softmax(hg_lb_logits.astype(jnp.float32), axis=0), axis=0)
    split_at = [int(v) for v in np.cumsum(IN_SIZES)[:-1]]
    for l in range(DEPTH):
        h = rmsnorm(x, attn_norm[l])
        proj = jnp.einsum('bsd,de->bse', h, w_in[l])
        hq, hf, hi, hg, nq, kc, vc, ksl, vsl, kwn, vwn, gr = jnp.split(proj, split_at, axis=-1)
        y_hg = hgrn2_mixer(hq, hf, hi, hg, lower_bounds[l], hg_out_norm[l])
        y_nsa = nsa_mixer(nq, kc, vc, ksl, vsl, kwn, vwn, gr, cmp_pos_k[l], cmp_w1_k[l], cmp_w2_k[l],
                          cmp_pos_v[l], cmp_w1_v[l], cmp_w2_v[l], cos, sin)
        y_nsa = rmsnorm(y_nsa, nsa_out_norm[l])
        y = jnp.concatenate([y_hg.astype(x.dtype), y_nsa.astype(x.dtype)], axis=-1)
        x = x + jnp.einsum('bse,ed->bsd', y, w_out[l])
        x = x + hier_moe(rmsnorm(x, ffn_norm[l]), moe_w_group[l], moe_b_group[l], moe_w_router[l],
                         moe_b_router[l], moe_w_gate[l], moe_w_up[l], moe_w_down[l])
    return rmsnorm(x, final_norm)


_drawn_inputs = setup_inputs


def setup_inputs(seed=0):
    import zlib

    import numpy as np

    out = dict(_drawn_inputs(seed))
    spreads = {}
    factors = {'hg_out_norm': 19.241,
     'nsa_out_norm': 10.019,
     'moe_b_group': 64.0,
     'moe_b_router': 28.532,
     'final_norm': 7.646,
     'cmp_pos_k': 3.205,
     'ffn_norm': 4.994}
    for name, (base, spread) in spreads.items():
        noise = np.random.default_rng([zlib.crc32(name.encode()), seed]).standard_normal(out[name].shape)
        drawn = base * np.exp(spread * noise) if base else spread * noise
        out[name] = jnp.asarray(drawn.astype(out[name].dtype))
    for name, factor in factors.items():
        out[name] = (out[name] * factor).astype(out[name].dtype)
    return out
```

```python
from contextlib import ExitStack

import concourse.bass as bass
from concourse import mybir
import numpy as np

F32 = mybir.dt.float32
BF16 = mybir.dt.bfloat16
I32 = mybir.dt.int32
ALU = mybir.AluOpType
ACT = mybir.ActivationFunctionType
AX = mybir.AxisListType.X

P = 128
SEQ = 256
D = 2048
T = SEQ // P
KC = D // P
HG = 1024
HH = 8
NH, NG, DK = 16, 4, 64
NCMP = 15
IN_COLS = 4 * HG + NH * DK + 6 * NG * DK + 3 * NH
HQ0, HF0, HI0, HG0, NQ0 = 0, HG, 2 * HG, 3 * HG, 4 * HG
KC0 = NQ0 + NH * DK
VC0, KS0, VS0, KW0, VW0, GR0 = (KC0 + n * NG * DK for n in range(1, 7))
NCH = 512
IN_CH = GR0 // NCH
OUT_CH = D // NCH
PIECE = 2048
RING_SLOTS = 12
PP = D * NCH // (P * PIECE)
NE, FF = 32, 512
SLOTS = 64
ROUNDS = SEQ // SLOTS
EP = 12
LEVELS = [64, 32, 16, 8, 4, 2, 1]
NL = len(LEVELS)
EPS = 1e-6
NEG = 1e30

C_ID = 0
C_LT = C_ID + 128
C_M = C_LT + 128
C_COS = C_M + (NL + 2) * 128
C_SIN = C_COS + T * 32
C_CM = C_SIN + T * 32
C_CN = C_CM + T * 16
C_NV = C_CN + T * 16
C_BD = C_NV + T
C_IOTA = C_BD + 8
C_REV = C_IOTA + SLOTS
C_N = C_REV + 36
B_ID = 0
B_CAUSAL = 128
B_GM = B_CAUSAL + 512
B_N = B_GM + (NL + 1) * 128


def tables():
    c = np.zeros((P, C_N), np.float32)
    b = np.zeros((P, B_N), np.float32)
    s, t = np.arange(P)[:, None], np.arange(P)[None, :]
    c[:, C_ID:C_ID + 128] = s == t
    c[:, C_LT:C_LT + 128] = s < t
    for n, h in enumerate(LEVELS):
        start = t // (2 * h) * (2 * h)
        right = t % (2 * h) >= h
        c[:, C_M + n * 128:C_M + n * 128 + 128] = np.where(
            right, (s >= start + h) & (s <= t), (s > t) & (s < start + h))
        b[:, B_GM + n * 128:B_GM + n * 128 + 128] = (s // (2 * h) == t // (2 * h)) & (s % (2 * h) < h) & right
    c[:, C_M + NL * 128:C_M + NL * 128 + 128] = s <= t
    c[:, C_M + (NL + 1) * 128:C_M + (NL + 2) * 128] = s > t
    b[:, B_GM + NL * 128:] = s == t
    b[:, B_ID:B_ID + 128] = s == t
    b[:, B_CAUSAL:B_CAUSAL + 512] = np.concatenate([np.zeros((P, 128)), np.where(t <= s, 0, -NEG)] * 2, 1)
    inv = (1.0 / (np.float32(10000.0) ** (np.arange(0, DK, 2, dtype=np.float32) / np.float32(DK)))).astype(np.float32)
    ang = np.arange(SEQ, dtype=np.float32)[:, None] * inv[None, :]
    for tau in range(T):
        rows = np.arange(P) + tau * P
        c[:, C_COS + tau * 32:C_COS + tau * 32 + 32] = np.cos(ang[rows])
        c[:, C_SIN + tau * 32:C_SIN + tau * 32 + 32] = np.sin(ang[rows])
        m = (np.arange(16)[None, :] * 16 + 31 <= rows[:, None]) & (np.arange(16)[None, :] < NCMP)
        c[:, C_CM + tau * 16:C_CM + tau * 16 + 16] = m
        c[:, C_CN + tau * 16:C_CN + tau * 16 + 16] = (m - 1.0) * NEG
        c[:, C_NV + tau] = ~m.any(1)
    c[:, C_BD:C_BD + 8] = s // 16 == np.arange(8)[None, :]
    c[:, C_IOTA:C_IOTA + SLOTS] = np.arange(SLOTS)
    c[:, C_REV:C_REV + 4] = 4 - np.arange(4)
    c[:, C_REV + 4:C_REV + 36] = 32 - np.arange(32)
    return c, b


def hybrid_block(nc, x, attn_norm, w_in, hg_lb_logits, hg_out_norm, cmp_pos_k, cmp_w1_k, cmp_w2_k,
                 cmp_pos_v, cmp_w1_v, cmp_w2_v, nsa_out_norm, w_out, ffn_norm, moe_w_group, moe_b_group,
                 moe_w_router, moe_b_router, moe_w_gate, moe_w_up, moe_w_down, final_norm, consts, consts_bf, out):
    with ExitStack() as ctx:
        def sb(name, cols, dt=F32):
            return ctx.enter_context(nc.sbuf_tensor(name, [P, cols], dt))

        def sem(name):
            return ctx.enter_context(nc.semaphore(name))

        ctx.enter_context(nc.allow_non_contiguous_dma(reason="small transposed gains and position tables"))

        ring = sb("ring", RING_SLOTS * PIECE)
        proj = sb("proj", T * IN_COLS)
        xt = sb("xt", KC * SEQ)
        scr = sb("scr", 8192)
        cst = sb("cst", C_N)
        cbf = sb("cbf", B_N, BF16)
        stat = sb("stat", 128)
        gain = sb("gain", 3 * KC)
        cnt_i = sb("cnt_i", 2, I32)
        bank = [ctx.enter_context(nc.psum_tensor(f"bank{n}", [P, 512], F32)) for n in range(8)]

        PJ = proj[:, :].rearrange("p (t c) -> p t c", t=T)
        XT = xt[:, :].rearrange("p (c t) -> p c t", c=KC)
        ident = cst[:, C_ID:C_ID + 128]

        def slot(n, inner):
            n = n % RING_SLOTS
            return ring[:, n * PIECE:(n + 1) * PIECE].rearrange("p (a b) -> p a b", b=inner)

        XN = scr[:, 0:T * D].rearrange("p (t c) -> p t c", t=T)
        WGATE = scr[:, 4096:4096 + KC * 48].rearrange("p (c n) -> p c n", c=KC)

        cst_loaded = sem("cst_loaded")
        x_loaded = sem("x_loaded")
        slot_loaded = [sem(f"slot_loaded{n}") for n in range(RING_SLOTS)]
        piece_used = sem("piece_used")
        small_loaded = sem("small_loaded")
        lb_loaded = sem("lb_loaded")
        w2_loaded = sem("w2_loaded")
        route_loaded = sem("route_loaded")
        fin_loaded = sem("fin_loaded")
        stored = sem("stored")
        sq_ready = sem("sq_ready")
        ms_ready = sem("ms_ready")
        root_ready = sem("root_ready")
        nat_ready = sem("nat_ready")
        turned = sem("turned")
        turned_used = sem("turned_used")
        gate_cols_done = sem("gate_cols_done")
        proj_saved = sem("proj_saved")
        dve_chain = sem("dve_chain")
        act_chain = sem("act_chain")
        pool_chain = sem("pool_chain")

        chain_value = {"dve": 0, "act": 0, "pool": 0}
        chain_sem = {"dve": dve_chain, "act": act_chain, "pool": pool_chain}

        def link(eng, name, ins):
            chain_value[name] += 1
            ins.then_inc(chain_sem[name], 1)
            eng.wait_ge(chain_sem[name], chain_value[name])

        lb_exp = sem("lb_exp")
        lb_in = sem("lb_in")
        sig_ready = sem("sig_ready")
        f_ready = sem("f_ready")
        lf_ready = sem("lf_ready")
        qk_turned = sem("qk_turned")
        qk_saved = sem("qk_saved")
        expo_done = sem("expo_done")
        decay_ready = sem("decay_ready")
        pair_ready = sem("pair_ready")
        gram_done = sem("gram_done")
        gram_used = sem("gram_used")
        part_added = sem("part_added")
        hg_out = sem("hg_out")
        hg_saved = sem("hg_saved")
        hg_sq = sem("hg_sq")
        hg_copied = sem("hg_copied")
        hg_ms = sem("hg_ms")
        hg_root = sem("hg_root")
        silu_ready = sem("silu_ready")

        def rms_dve(dve, n, ss, width, rstd):
            dve.wait_ge(sq_ready, n + 1)
            dve.tensor_scalar(rstd, ss, 1.0 / width, EPS, ALU.mult, ALU.add).then_inc(ms_ready, 1)
            dve.wait_ge(root_ready, n + 1)
            link(dve, "dve", dve.reciprocal(rstd, rstd))

        def rms_act(act, n, rstd):
            act.wait_ge(ms_ready, n + 1)
            act.activation(rstd, rstd, ACT.Sqrt).then_inc(root_ready, 1)

        def turn_pe(pe, use, src):
            for k in range(8):
                tau, cg = k // 4, k % 4
                pe.wait_ge(nat_ready, 2 * use + tau + 1)
                if use or k >= 4:
                    pe.wait_ge(turned_used, 8 * use + k - 3)
                for j in range(4):
                    c = 4 * cg + j
                    last = pe.transpose(bank[k % 4][:, j * 128:(j + 1) * 128],
                                        src[:, tau, c:c + 127 * KC + 1:KC], ident)
                last.then_inc(turned, 1)

        def turn_dve(dve, use, dst, g):
            for k in range(8):
                tau, cg = k // 4, k % 4
                dve.wait_ge(turned, 8 * use + k + 1)
                dve.tensor_tensor(dst[:, 4 * cg:4 * cg + 4, tau * P:(tau + 1) * P],
                                  bank[k % 4][:, :].rearrange("p (c t) -> p c t", c=4),
                                  gain[:, g * KC + 4 * cg:g * KC + 4 * cg + 4].unsqueeze(2).to_broadcast([P, 4, P]),
                                  ALU.mult).then_inc(turned_used, 1)

        qT = xt[:, 0:1024].rearrange("p (h t) -> p h t", h=4)
        kT = xt[:, 1024:2048].rearrange("p (h t) -> p h t", h=4)
        att = [xt[:, 2048 + 512 * n:2560 + 512 * n] for n in range(3)]
        lbl = xt[:, 2048:4096].rearrange("p (a c) -> p a c", a=2)
        LF = scr[:, 0:2048].rearrange("p (t c) -> p t c", t=T)
        decay = [scr[:, 2048 + 512 * n:2560 + 512 * n] for n in range(2)]
        pair = [scr[:, 3072 + 512 * n:3584 + 512 * n] for n in range(2)]
        part = [scr[:, 4096 + 512 * n:4608 + 512 * n] for n in range(2)]
        sqt = scr[:, 7168:7680]
        LB = scr[:, 5120:6144]
        OMLB = scr[:, 6144:7168]
        rst = stat[:, 16:32]
        STEPS = [("level", tau, n) for tau in range(T) for n in range(NL)] + [("diag", 0, 0), ("diag", 1, 0), ("cross", 0, 0)]
        ADDS = T * NL
        ktmp = sb("ktmp", 128)
        sums = sb("sums", 16)
        nmx = sb("nmx", 8)


        def decays_upto(hg, n):
            return hg * (T * NL + 2) + sum({"level": 1, "diag": 0, "cross": 2}[s[0]] for s in STEPS[:n + 1])

        def pairs_upto(hg, n):
            return hg * (2 * T * NL + 2) + sum({"level": 2, "diag": 0, "cross": 2}[s[0]] for s in STEPS[:n + 1])

        qUT = xt[:, 0:2048].rearrange("p (a t) -> p a t", a=8)
        qRT = xt[:, 2048:4096].rearrange("p (a t) -> p a t", a=8)
        kRT = scr[:, 0:2048].rearrange("p (b g t) -> p b g t", b=2, g=4)
        kvT = [scr[:, 2048 + 1024 * n:3072 + 1024 * n].rearrange("p (g t) -> p g t", g=4) for n in range(2)]
        prob = scr[:, 2048:3072].rearrange("p (h s) -> p h s", h=4)
        probT = scr[:, 3072:4096].rearrange("p (h s) -> p h s", s=128)
        flat = scr[:, 4096:5056].rearrange("p (m g n) -> p m g n", m=16, g=4)
        hid = scr[:, 5056:5312]
        hidT = [scr[:, 5312 + 128 * n:5440 + 128 * n].rearrange("p (f m) -> p f m", f=2) for n in range(2)]
        hrep = scr[:, 5568:6080].rearrange("p (o f g r n) -> p o f g r n", o=2, f=2, g=2, r=4)
        kcT = scr[:, 6080:6144]
        vbd = scr[:, 6144:7168].rearrange("p (o h d) -> p o h d", o=2, h=8)
        sc = scr[:, 7168:7680].rearrange("p (t h n) -> p t h n", t=T, h=NH)
        pcT = scr[:, 5056:5568].rearrange("p (t o q) -> p t o q", t=T, o=2)
        tmp = scr[:, 7680:8192]
        QR = PJ[:, :, HF0:HF0 + HG]
        KR = PJ[:, :, HI0:HI0 + HG].rearrange("p t (b g u d) -> p t b g u d", b=2, g=4, u=2)
        YN = PJ[:, :, HF0:HF0 + HG]
        w2k = cst[:, C_M:C_M + 256].rearrange("p (f u d) -> p f u d", f=2, u=2)
        w2v = cst[:, C_M + 256:C_M + 384].rearrange("p (f d) -> p f d", f=2)
        posn = cst[0:16, C_M + 384:C_M + 640].rearrange("p (n x) -> p n x", n=2)
        posT = cst[:, C_M + 640:C_M + 672].rearrange("p (n m) -> p n m", n=2)

        q_turned = sem("q_turned")
        q_saved = sem("q_saved")
        rope_done = sem("rope_done")
        kv_turned = sem("kv_turned")
        kv_saved = sem("kv_saved")
        flat_ready = sem("flat_ready")
        hid_done = sem("hid_done")
        hid_ready = sem("hid_ready")
        hidT_done = sem("hidT_done")
        hidT_ready = sem("hidT_ready")
        cmp_done = sem("cmp_done")
        cmp_ready = sem("cmp_ready")
        sc_done = sem("sc_done")
        sc_in = sem("sc_in")
        sc_exp = sem("sc_exp")
        pc_ready = sem("pc_ready")
        pcT_done = sem("pcT_done")
        pcT_ready = sem("pcT_ready")
        oc_done = sem("oc_done")
        oc_used = sem("oc_used")
        gates_ready = sem("gates_ready")
        s_done = sem("s_done")
        s_max = sem("s_max")
        p_ready = sem("p_ready")
        pT_done = sem("pT_done")
        pT_ready = sem("pT_ready")
        o_done = sem("o_done")
        o_used = sem("o_used")
        YALL = PJ[:, :, 0:D]
        pT_ready_b = sem("pT_ready_b")
        UNITS = [(br, g, tau) for br in range(2) for g in range(NG) for tau in range(T)]
        gates = stat[:, 32:128].rearrange("p (t h b) -> p t h b", t=T, h=NH)

        X2 = proj[:, 0:T * D].rearrange("p (t c) -> p t c", t=T)
        XS = proj[:, T * D:2 * T * D].rearrange("p (t c) -> p t c", t=T)
        mo = 2 * T * D
        WR = proj[:, mo:mo + KC * 36].rearrange("p (c n) -> p c n", c=KC)
        rbias = proj[:, mo + 576:mo + 612]
        fgain = proj[:, mo + 640:mo + 640 + D]
        LG = scr[:, 0:72].rearrange("p (t n) -> p t n", t=T)
        sel = scr[:, 72:136].rearrange("p (t n) -> p t n", t=T)
        wt = scr[:, 640:640 + T * (NE + 1)].rearrange("p (t n) -> p t n", t=T)
        posm = scr[:, 720:720 + T * (NE + 1)].rearrange("p (t n) -> p t n", t=T)
        ones = scr[:, 264:392]
        r8 = scr[:, 392:512]
        disp = scr[:, 1024:1152].rearrange("p (t s) -> p t s", t=T)
        dispw = scr[:, 1152:1408].rearrange("p (t u s) -> p t u s", t=T, u=2)
        dispT = scr[:, 1408:1664].rearrange("p (t q) -> p t q", t=T)
        xg = scr[:, 2048:3072].rearrange("p (c s) -> p c s", c=KC)
        hs = scr[:, 3072:3584]
        hv = scr[:, 3584:4096]
        hT = scr[:, 4096:4352].rearrange("p (c s) -> p c s", c=4)
        yb = scr[:, 4608:5632].rearrange("p (a n) -> p a n", a=2)

        out_done = sem("out_done")
        out_saved = sem("out_saved")
        res_loaded = sem("res_loaded")
        logit_done = sem("logit_done")
        r_in = sem("r_in")
        r_exp = sem("r_exp")
        sel_ready = sem("sel_ready")
        pos_done = sem("pos_done")
        pos_ready = sem("pos_ready")
        disp_ready = sem("disp_ready")
        disp_hot = sem("disp_hot")
        gath_done = sem("gath_done")
        gath_saved = sem("gath_saved")
        dT_done = sem("dT_done")
        dT_saved = sem("dT_saved")
        gu_done = sem("gu_done")
        silu_done = sem("silu_done")
        h_ready = sem("h_ready")
        hT_done = sem("hT_done")
        hT_saved = sem("hT_saved")
        down_done = sem("down_done")
        y_saved_a = sem("y_saved_a")
        y_saved_d = sem("y_saved_d")
        scat_done = sem("scat_done")
        scat_used = sem("scat_used")
        final_ready = sem("final_ready")
        experts_done = sem("experts_done")

        x_v = x.rearrange("b (t p) d -> (b p) t d", p=P)
        out_v = out.rearrange("b (t p) d -> (b p) t d", p=P)
        win_v = w_in[0].rearrange("(p c) n -> p c n", p=P)
        wout_v = w_out[0].rearrange("(p c) n -> p c n", p=P)
        gate_v = moe_w_gate[0].rearrange("e (p c) n -> e p (c n)", p=P)
        up_v = moe_w_up[0].rearrange("e (p c) n -> e p (c n)", p=P)
        down_v = moe_w_down[0].rearrange("e (p c) n -> e p (c n)", p=P)

        CST_LOADS = 16 * 13
        CMP_PIECE = IN_CH * PP
        OUT_PIECE = CMP_PIECE + 4
        MOE_PIECE = OUT_PIECE + OUT_CH * PP
        assert MOE_PIECE % RING_SLOTS == 0 and RING_SLOTS == EP

        def piece_ready(eng, n):
            eng.wait_ge(slot_loaded[n % RING_SLOTS], 16 * (n // RING_SLOTS + 1))

        moe_turn = MOE_PIECE // RING_SLOTS

        block = ctx.enter_context(nc.Block())

        @block.sync
        def _(sp):
            for tau in range(T):
                sp.dma_start(XN[:, tau, :], x_v[:, tau, :]).then_inc(x_loaded, 16)

            def load(n, src, inner):
                if n >= RING_SLOTS:
                    sp.wait_ge(piece_used, n - RING_SLOTS + 1)
                sp.dma_start(slot(n, inner), src).then_inc(slot_loaded[n % RING_SLOTS], 16)

            for ch in range(IN_CH):
                for i in range(PP):
                    load(ch * PP + i, win_v[:, 4 * i:4 * i + 4, ch * NCH:(ch + 1) * NCH], NCH)
            for n, w in enumerate((cmp_w1_k, cmp_w1_v)):
                v = w[0].rearrange("(m p) n -> p m n", p=P)
                for i in range(2):
                    load(CMP_PIECE + 2 * n + i, v[:, 8 * i:8 * i + 8, :], 256)
            for ch in range(OUT_CH):
                for i in range(PP):
                    load(OUT_PIECE + ch * PP + i, wout_v[:, 4 * i:4 * i + 4, ch * NCH:(ch + 1) * NCH], NCH)

            def expert_loads(e, done):
                k = 0
                for j in range(4):
                    for w in (gate_v, up_v):
                        sp.wait_ge(piece_used, done * EP + (MOE_PIECE - RING_SLOTS + k + 1))
                        sp.dma_start(ring[:, k * PIECE:(k + 1) * PIECE],
                                     w[bass.ds(e, 1), :, j * PIECE:(j + 1) * PIECE].rearrange("e p n -> (e p) n")
                                     ).then_inc(slot_loaded[k], 16)
                        k += 1
                for j in range(4):
                    sp.wait_ge(piece_used, done * EP + (MOE_PIECE - RING_SLOTS + k + 1))
                    sp.dma_start(ring[:, k * PIECE:(k + 1) * PIECE],
                                 down_v[bass.ds(e, 1), :, j * PIECE:(j + 1) * PIECE].rearrange("e p n -> (e p) n")
                                 ).then_inc(slot_loaded[k], 16)
                    k += 1

            with sp.Fori(0, NE) as e:
                expert_loads(e, e)
            sp.wait_ge(pos_ready, 2)
            most = sp.value_load(cnt_i[0:1, 0:1], min_val=0, max_val=SEQ)
            with sp.If(most > SLOTS):
                for r in range(1, ROUNDS):
                    with sp.Fori(0, NE) as e:
                        expert_loads(e, e + r * NE)
            sp.wait_ge(final_ready, 2)
            sp.dma_start(out_v, XS).then_inc(stored, 16)
            sp.wait_ge(stored, 16)

        @block.gpsimd
        def _(pool):

            pool.dma_start(WGATE, win_v[:, :, GR0:IN_COLS]).then_inc(small_loaded, 16)

            pool.wait_ge(gate_cols_done, 1)
            pool.dma_start(lbl, hg_lb_logits.rearrange("(o a) c -> o a c", o=1).to_broadcast([P, 2, HG])
                           ).then_inc(lb_loaded, 16)
            k = 0
            for hg in range(2):
                for n, (kind, tau, lv) in enumerate(STEPS):
                    if kind == "cross" or (kind == "level" and lv == 0):
                        continue
                    pool.wait_ge(gram_used, hg * len(STEPS) + n + 1)
                    if k:
                        pool.wait_ge(part_added, k)
                    pool.tensor_tensor(att[tau], att[tau], part[n % 2], ALU.add).then_inc(part_added, 1)
                    k += 1

            pool.wait_ge(expo_done, 2 * (T * NL + 2))
            pool.dma_start(w2v[:, :, :], cmp_w2_v[0].rearrange("(f p) d -> p f d", p=P)).then_inc(w2_loaded, 16)
            for u in range(2):
                pool.dma_start(w2k[:, :, u, :], cmp_w2_k[0].rearrange("(f p) d -> p f d", p=P)).then_inc(w2_loaded, 16)
            for n, w in enumerate((cmp_pos_k, cmp_pos_v)):
                pool.dma_start(posn[:, n, :], w[0].rearrange("(m a) d -> m (a d)", a=2)).then_inc(w2_loaded, 16)
            pool.wait_ge(hg_out, 4)
            for tau in range(T):
                cos = cst[:, C_COS + tau * 32:C_COS + tau * 32 + 32].unsqueeze(1).to_broadcast([P, NG, 32])
                sin = cst[:, C_SIN + tau * 32:C_SIN + tau * 32 + 32].unsqueeze(1).to_broadcast([P, NG, 32])
                kt = ktmp[:, :].rearrange("p (g d) -> p g d", g=NG)
                for br, col in enumerate((KS0, KW0)):
                    src = PJ[:, tau, col:col + 256].rearrange("p (g a d) -> p g a d", g=NG, a=2)
                    for half, op in ((0, ALU.subtract), (1, ALU.add)):
                        dst = KR[:, tau, br, :, 0, 32 * half:32 * half + 32]
                        link(pool, "pool", pool.tensor_tensor(dst, src[:, :, half, :], cos, ALU.mult))
                        link(pool, "pool", pool.tensor_tensor(kt, src[:, :, 1 - half, :], sin, ALU.mult))
                        link(pool, "pool", pool.tensor_tensor(dst, dst, kt, op))
                    last = pool.tensor_copy(KR[:, tau, br, :, 1, :], KR[:, tau, br, :, 0, :])
                    if tau == T - 1 and br == 1:
                        last.then_inc(rope_done, 1)
                    else:
                        link(pool, "pool", last)

            pool.wait_ge(turned, 16)
            for tau in range(T):
                pool.dma_start(X2[:, tau, :], x_v[:, tau, :]).then_inc(res_loaded, 16)
            pool.dma_start(WR[:, :, 0:4], moe_w_group[0].rearrange("(p c) n -> p c n", p=P)).then_inc(route_loaded, 16)
            pool.dma_start(WR[:, :, 4:36], moe_w_router[0].rearrange("(p c) n -> p c n", p=P)).then_inc(route_loaded, 16)
            pool.dma_start(rbias[:, 0:4], moe_b_group.to_broadcast([P, 4])).then_inc(route_loaded, 16)
            pool.dma_start(rbias[:, 4:36], moe_b_router.to_broadcast([P, NE])).then_inc(route_loaded, 16)
            pool.dma_start(fgain, final_norm.rearrange("(o d) -> o d", o=1).to_broadcast([P, D])).then_inc(fin_loaded, 16)

        @block.tensor
        def _(pe):
            pe.wait_ge(cst_loaded, CST_LOADS)
            turn_pe(pe, 0, XN)
            for ch in range(IN_CH + 1):
                if ch == 0:
                    pe.wait_ge(turned_used, 8)
                if ch >= 2:
                    pe.wait_ge(proj_saved, ch - 1)
                width = NCH if ch < IN_CH else 48
                if ch == IN_CH:
                    pe.wait_ge(small_loaded, 16)
                for i in range(PP):
                    if ch < IN_CH:
                        piece_ready(pe, ch * PP + i)
                    for tau in range(T):
                        for cc in range(4):
                            c = 4 * i + cc
                            rhs = slot(ch * PP + i, NCH)[:, cc, :] if ch < IN_CH else WGATE[:, c, :]
                            last = pe.matmul(bank[2 * (ch % 2) + tau][:, 0:width], XT[:, c, tau * P:(tau + 1) * P], rhs,
                                             start=c == 0, stop=c == KC - 1)
                    if ch < IN_CH:
                        last.then_inc(piece_used, 1)
                if ch == IN_CH:
                    last.then_inc(gate_cols_done, 1)

            pe.wait_ge(lf_ready, 2)
            k = 0
            for hg in range(2):
                for n in range(4):
                    what, tau = n // 2, n % 2
                    if hg:
                        pe.wait_ge(qk_saved, 4)
                    if n == 0 and hg == 0:
                        pe.wait_ge(proj_saved, IN_CH + 1)
                    if n == 0 and hg:
                        pe.wait_ge(hg_saved, 2)
                    for j in range(4):
                        h = 4 * hg + j
                        col = (HQ0, HF0)[what] + h * 128
                        last = pe.transpose(bank[n][:, j * 128:(j + 1) * 128], PJ[:, tau, col:col + 128], ident)
                    last.then_inc(qk_turned, 1)
                pe.wait_ge(qk_saved, 4 * (hg + 1))

                def exponents(n):
                    kind, tau, lv = STEPS[n]
                    g = hg * len(STEPS) + n
                    if kind == "diag":
                        return
                    b = bank[4 + n % 2]
                    if kind == "level":
                        if n >= 2:
                            pe.wait_ge(decay_ready, decays_upto(hg, n - 2))
                        for j in range(4):
                            h = 4 * hg + j
                            last = pe.matmul(b[:, j * 128:(j + 1) * 128], LF[:, tau, h * 128:(h + 1) * 128],
                                             cst[:, C_M + lv * 128:C_M + lv * 128 + 128], start=True, stop=True)
                        last.then_inc(expo_done, 1)
                    else:
                        pe.wait_ge(decay_ready, decays_upto(hg, n - 1))
                        for u in range(2):
                            for j in range(4):
                                h = 4 * hg + j
                                m = C_M + (NL + u) * 128
                                last = pe.matmul(bank[4 + u][:, j * 128:(j + 1) * 128],
                                                 LF[:, 1 - u, h * 128:(h + 1) * 128],
                                                 cst[:, m:m + 128], start=True, stop=True)
                            last.then_inc(expo_done, 1)

                def products(n):
                    kind, tau, lv = STEPS[n]
                    g = hg * len(STEPS) + n
                    if g >= 2:
                        pe.wait_ge(gram_used, g - 1)
                    if kind != "diag":
                        pe.wait_ge(pair_ready, pairs_upto(hg, n))
                    b = bank[6 + g % 2]
                    for j in range(4):
                        sl = slice(j * 128, (j + 1) * 128)
                        if kind == "level":
                            l = r = pair[n % 2][:, sl]
                        elif kind == "diag":
                            l, r = kT[:, j, tau * P:(tau + 1) * P], qT[:, j, tau * P:(tau + 1) * P]
                        else:
                            l, r = pair[1][:, sl], pair[0][:, sl]
                        last = pe.matmul(b[:, sl], l, r, start=True, stop=True)
                    last.then_inc(gram_done, 1)

                exponents(0)
                for n in range(len(STEPS)):
                    if n + 1 < len(STEPS):
                        exponents(n + 1)
                    products(n)
                pe.wait_ge(gram_used, len(STEPS) * (hg + 1))
                pe.wait_ge(part_added, ADDS * (hg + 1))
                for tau in range(T):
                    for j in range(4):
                        h = 4 * hg + j
                        sl = slice(j * 128, (j + 1) * 128)
                        v = [PJ[:, t, HI0 + h * 128:HI0 + h * 128 + 128] for t in range(T)]
                        if tau == 0:
                            last = pe.matmul(bank[0][:, sl], att[0][:, sl], v[0], start=True, stop=True)
                        else:
                            pe.matmul(bank[1][:, sl], att[2][:, sl], v[0], start=True, stop=False)
                            last = pe.matmul(bank[1][:, sl], att[1][:, sl], v[1], start=False, stop=True)
                    last.then_inc(hg_out, 1)

            pe.wait_ge(hg_saved, 4)
            pe.wait_ge(w2_loaded, 80)
            for n in range(2):
                last = pe.transpose(bank[0][:, n * 16:(n + 1) * 16], posn[:, n, :], ident[0:16, 0:16])
            last.then_inc(kv_turned, 1)
            for n in range(4):
                if n >= 2:
                    pe.wait_ge(q_saved, n - 1)
                for j in range(4):
                    i = 4 * n + j
                    tau, a = i // 8, i % 8
                    last = pe.transpose(bank[1 + n % 2][:, j * 128:(j + 1) * 128],
                                        PJ[:, tau, NQ0 + a * 128:NQ0 + a * 128 + 128], ident)
                last.then_inc(q_turned, 1)
            for n in range(2):
                for j in range(4):
                    a, tau = j // 2, j % 2
                    col = (KC0, VC0)[n] + a * 128
                    last = pe.transpose(bank[3 + n][:, j * 128:(j + 1) * 128], PJ[:, tau, col:col + 128], ident)
                last.then_inc(kv_turned, 1)
            pe.wait_ge(rope_done, 2)
            for n in range(4):
                pe.wait_ge(q_saved, 3 + n)
                for j in range(4):
                    i = 4 * n + j
                    tau, a = i // 8, i % 8
                    last = pe.transpose(bank[1 + n % 2][:, j * 128:(j + 1) * 128], QR[:, tau, a * 128:(a + 1) * 128], ident)
                last.then_inc(q_turned, 1)
            for n in range(4):
                br, tau = n // 2, n % 2
                if n >= 2:
                    pe.wait_ge(q_saved, 7 + n)
                for g in range(NG):
                    last = pe.transpose(bank[5 + n % 2][:, g * 128:(g + 1) * 128],
                                        PJ[:, tau, HI0 + (br * 4 + g) * 128:HI0 + (br * 4 + g + 1) * 128], ident)
                last.then_inc(q_turned, 1)
            for n in range(2):
                pe.wait_ge(flat_ready, n + 1)
                for i in range(2):
                    piece_ready(pe, CMP_PIECE + 2 * n + i)
                    for mm in range(8):
                        m = 8 * i + mm
                        last = pe.matmul(bank[7][0:60, 0:256], flat[:, m, :, :].rearrange("p g n -> p (g n)"),
                                         slot(CMP_PIECE + 2 * n + i, 256)[:, mm, :], start=m == 0, stop=m == 15)
                    last.then_inc(piece_used, 1)
                pe.wait_ge(hid_ready, n + 1)
                for f in range(2):
                    last = pe.transpose(bank[0][:, 64 * f:64 * f + 60], hid[0:60, f * 128:(f + 1) * 128], ident[0:60, 0:60])
                last.then_inc(hidT_done, 1)
                pe.wait_ge(hidT_ready, n + 1)
                if n == 0:
                    for f in range(2):
                        last = pe.matmul(bank[0][:, 256:316], w2k[:, f, :, :].rearrange("p u d -> p (u d)"),
                                         hidT[0][:, f, 0:60], start=f == 0, stop=f == 1)
                    last.then_inc(cmp_done, 1)
                else:
                    for o in range(2):
                        for f in range(2):
                            last = pe.matmul(bank[7][:, o * 64:o * 64 + 64],
                                             hrep[:, o, f, :, :, :].rearrange("p g r n -> p (g r n)"),
                                             w2v[:, f, :], start=f == 0, stop=f == 1)
                    last.then_inc(cmp_done, 1)
            pe.wait_ge(cmp_ready, 1)
            pe.wait_ge(q_saved, 12)
            for tau in range(T):
                for h in range(NH):
                    half = slice(64 * (h % 2), 64 * (h % 2) + 64)
                    col = tau * 128 + (h // 2) * 16
                    last = pe.matmul(bank[1 + h % 2][:, col:col + NCMP], qUT[half, h // 2, tau * P:(tau + 1) * P],
                                     kcT[half, (h // 4) * NCMP:(h // 4 + 1) * NCMP], start=True, stop=True)
            last.then_inc(sc_done, 1)
            pe.wait_ge(pc_ready, 1)
            for tau in range(T):
                for o in range(2):
                    last = pe.transpose(bank[3][:, (2 * tau + o) * 128:(2 * tau + o + 1) * 128],
                                        sc[:, tau, 8 * o:8 * o + 8, :].rearrange("p h n -> p (h n)"), ident)
            last.then_inc(pcT_done, 1)
            pe.wait_ge(pcT_ready, 1)
            pe.wait_ge(cmp_ready, 2)
            for tau in range(T):
                for o in range(2):
                    if 2 * tau + o >= 2:
                        pe.wait_ge(oc_used, 2 * tau + o - 1)
                    last = pe.matmul(bank[4 + o][:, :], pcT[:, tau, o, :], vbd[:, o, :, :].rearrange("p h d -> p (h d)"),
                                     start=True, stop=True)
                    last.then_inc(oc_done, 1)
            pe.wait_ge(oc_used, 4)

            def scores(u):
                br, g, tau = UNITS[u]
                if u >= 2:
                    pe.wait_ge(p_ready, 4 * (u - 1))
                n = 128 * (tau + 1)
                for half in range(2):
                    b = bank[2 * (u % 2) + half][:, 0:2 * n].rearrange("p (h s) -> p h s", h=2)
                    mask = cbf[:, B_CAUSAL:B_CAUSAL + 512].rearrange("p (h s) -> p h s", h=2)[:, :, 256 - n:256]
                    pe.matmul(b, cbf[:, B_ID:B_ID + 128], mask, start=True, stop=False, skip_group_check=True)
                for i in range(2):
                    for half in range(2):
                        a = 2 * g + i
                        rows = slice(64 * half, 64 * half + 64)
                        b = bank[2 * (u % 2) + half][:, i * n:(i + 1) * n]
                        last = pe.matmul(b, qRT[rows, a, tau * P:(tau + 1) * P], kRT[rows, br, g, 0:n],
                                         start=False, stop=True, skip_group_check=True)
                last.then_inc(s_done, 1)

            def values(u):
                br, g, tau = UNITS[u]
                pe.wait_ge(p_ready, 4 * (u + 1))
                for sb_ in range(tau + 1):
                    for h in range(4):
                        last = pe.transpose(bank[4 + sb_][:, h * 128:(h + 1) * 128],
                                            prob[:, h, sb_ * 128:(sb_ + 1) * 128], ident)
                last.then_inc(pT_done, 1)
                pe.wait_ge(pT_ready, u + 1)
                if tau:
                    pe.wait_ge(pT_ready_b, u // 2 + 1)
                if u >= 2:
                    pe.wait_ge(o_used, u - 1)
                v0 = (VS0, VW0)[br] + g * DK
                for h in range(4):
                    for sb_ in range(tau + 1):
                        last = pe.matmul(bank[6 + u % 2][:, h * DK:(h + 1) * DK], probT[:, 4 * sb_ + h, :],
                                         PJ[:, sb_, v0:v0 + DK], start=sb_ == 0, stop=sb_ == tau)
                last.then_inc(o_done, 1)

            scores(0)
            for u in range(len(UNITS)):
                if u + 1 < len(UNITS):
                    scores(u + 1)
                values(u)

            turn_pe(pe, 1, YALL)
            pe.wait_ge(turned_used, 16)
            for ch in range(OUT_CH):
                if ch >= 2:
                    pe.wait_ge(out_saved, 2 * (ch - 1))
                for i in range(PP):
                    n = OUT_PIECE + ch * PP + i
                    piece_ready(pe, n)
                    for tau in range(T):
                        for cc in range(4):
                            c = 4 * i + cc
                            last = pe.matmul(bank[2 * (ch % 2) + tau][:, :], XT[:, c, tau * P:(tau + 1) * P],
                                             slot(n, NCH)[:, cc, :], start=c == 0, stop=c == KC - 1)
                    last.then_inc(piece_used, 1)

            turn_pe(pe, 2, XS)
            pe.wait_ge(turned_used, 24)
            pe.wait_ge(route_loaded, 64)
            for tau in range(T):
                for c in range(KC):
                    last = pe.matmul(bank[4][:, tau * 36:tau * 36 + 36], XT[:, c, tau * P:(tau + 1) * P], WR[:, c, :],
                                     start=c == 0, stop=c == KC - 1)
            last.then_inc(logit_done, 1)
            pe.wait_ge(sel_ready, 1)
            lt = cst[:, C_LT:C_LT + 128]
            pe.matmul(bank[5][:, 0:32], lt, sel[:, 0, :], start=True, stop=True)
            pe.matmul(bank[5][:, 32:64], ones, sel[:, 0, :], start=True, stop=False)
            pe.matmul(bank[5][:, 32:64], lt, sel[:, 1, :], start=False, stop=True)
            pe.matmul(bank[5][:, 64:96], ones, sel[:, 0, :], start=True, stop=False)
            pe.matmul(bank[5][:, 64:96], ones, sel[:, 1, :], start=False, stop=True).then_inc(pos_done, 1)

            def expert(done, r):
                pe.wait_ge(disp_ready, 2 * done + (2 + 2 * r))
                pe.wait_ge(scat_used, 8 * done + 8)
                for half in range(2):
                    for cc in range(8):
                        c = 8 * half + cc
                        for tau in range(T):
                            last = pe.matmul(bank[half][:, cc * SLOTS:(cc + 1) * SLOTS], XS[:, tau, c:c + 127 * KC + 1:KC],
                                             disp[:, tau, :], start=tau == 0, stop=tau == T - 1)
                    last.then_inc(gath_done, 1)
                for tau in range(T):
                    last = pe.transpose(bank[2][:, tau * 128:(tau + 1) * 128],
                                        dispw[:, tau, :, :].rearrange("p u s -> p (u s)"), ident)
                last.then_inc(dT_done, 1)
                for j in range(4):
                    pe.wait_ge(slot_loaded[2 * j], 16 * done + 16 * (moe_turn + 1))
                    pe.wait_ge(slot_loaded[2 * j + 1], 16 * done + 16 * (moe_turn + 1))
                    if j % 2 == 0:
                        pe.wait_ge(gath_saved, 2 * done + (j // 2 + 1))
                    for cc in range(4):
                        c = 4 * j + cc
                        for u in range(2):
                            last = pe.matmul(bank[3][64 * u:64 * u + 64, :], xg[:, c, :],
                                             ring[:, (2 * j + u) * PIECE + cc * NCH:(2 * j + u) * PIECE + (cc + 1) * NCH],
                                             start=c == 0, stop=c == KC - 1)
                            if cc == 3:
                                last.then_inc(piece_used, 1)
                pe.wait_ge(dT_saved, done + 1)
                pe.wait_ge(h_ready, done + 1)
                for c in range(4):
                    last = pe.matmul(bank[2][:, 256 + c * 64:256 + c * 64 + 64], hv[64:128, c:c + 127 * 4 + 1:4],
                                     ident[64:128, 64:128], start=True, stop=True)
                last.then_inc(hT_done, 1)
                pe.wait_ge(hT_saved, done + 1)
                for c in range(4):
                    pe.wait_ge(slot_loaded[8 + c], 16 * done + 16 * (moe_turn + 1))
                    for n in range(4):
                        last = pe.matmul(bank[4 + n // 2][64 * (n % 2):64 * (n % 2) + 64, :], hT[:, c, :],
                                         ring[:, (8 + c) * PIECE + n * NCH:(8 + c) * PIECE + (n + 1) * NCH],
                                         start=c == 0, stop=c == 3)
                    last.then_inc(piece_used, 1)
                pe.wait_ge(y_saved_a, done + 1)
                pe.wait_ge(y_saved_d, done + 1)
                for tau in range(T):
                    for n in range(4):
                        if tau == 1:
                            pe.wait_ge(scat_used, 8 * done + (8 + n + 1))
                        rows = slice(64 * (n % 2), 64 * (n % 2) + 64)
                        pe.matmul(bank[(6, 7, 0, 1)[n]][:, :], dispT[rows, tau, :], yb[rows, n // 2, :],
                                  start=True, stop=True).then_inc(scat_done, 1)

            with pe.Fori(0, NE) as e:
                expert(e, 0)
            pe.wait_ge(pos_ready, 2)
            most = pe.value_load(cnt_i[0:1, 0:1], min_val=0, max_val=SEQ)
            with pe.If(most > SLOTS):
                for r in range(1, ROUNDS):
                    with pe.Fori(0, NE) as e:
                        expert(e + r * NE, r)

        @block.scalar
        def _(act):
            act.dma_start(cst[:, :], consts).then_inc(cst_loaded, 16)
            act.dma_start(cbf[:, :], consts_bf).then_inc(cst_loaded, 16)
            act.dma_start(gain[:, 0:KC], attn_norm[0].rearrange("(p c) -> p c", p=P)).then_inc(cst_loaded, 16)
            for h in range(8):
                act.dma_start(gain[8 * h:8 * h + 8, KC:2 * KC], hg_out_norm[0].rearrange("(p c) -> p c", c=KC)
                              ).then_inc(cst_loaded, 16)
            act.dma_start(gain[64:128, KC:2 * KC], nsa_out_norm[0].rearrange("(p c) -> p c", c=KC)).then_inc(cst_loaded, 16)
            act.dma_start(gain[:, 2 * KC:3 * KC], ffn_norm[0].rearrange("(p c) -> p c", p=P)).then_inc(cst_loaded, 16)

            def squares(src, n):
                link(act, "act", act.activation(XT[:, 0:8, :].rearrange("p c t -> p (c t)")[:, 0:src.shape[2]], src[:, 0, :],
                                                ACT.Square, accum_out=stat[:, 0:1]))
                act.activation(XT[:, 0:8, :].rearrange("p c t -> p (c t)")[:, 0:src.shape[2]], src[:, 1, :],
                               ACT.Square, accum_out=stat[:, 1:2]).then_inc(sq_ready, 1)

            act.wait_ge(x_loaded, 32)
            squares(XN, 0)
            rms_act(act, 0, stat[:, 0:2])
            for ch in range(IN_CH + 1):
                if ch < IN_CH:
                    act.wait_ge(piece_used, PP * (ch + 1))
                else:
                    act.wait_ge(gate_cols_done, 1)
                width = NCH if ch < IN_CH else 48
                for tau in range(T):
                    c = act.activation(PJ[:, tau, ch * NCH:ch * NCH + width], bank[2 * (ch % 2) + tau][:, 0:width], ACT.Copy)
                    if tau == 0:
                        c.then_inc(act_chain, 1)
                        chain_value["act"] += 1
                        act.wait_ge(act_chain, chain_value["act"])
                    else:
                        c.then_inc(proj_saved, 1)

            act.wait_ge(proj_saved, IN_CH + 1)
            for tau in range(T):
                act.activation(PJ[:, tau, HF0:HF0 + HG], PJ[:, tau, HF0:HF0 + HG], ACT.Sigmoid).then_inc(sig_ready, 1)
            act.activation(gates[:, :, :, :].rearrange("p t h b -> p t (h b)"), PJ[:, :, GR0:GR0 + 48],
                           ACT.Sigmoid).then_inc(gates_ready, 1)
            for tau in range(T):
                act.activation(PJ[:, tau, HG0:HG0 + HG], PJ[:, tau, HG0:HG0 + HG], ACT.Silu).then_inc(silu_ready, 1)
            act.wait_ge(lb_in, 1)
            act.activation(lbl, lbl, ACT.Exp).then_inc(lb_exp, 1)
            for tau in range(T):
                act.wait_ge(f_ready, tau + 1)
                act.activation(LF[:, tau, :], LF[:, tau, :], ACT.Ln).then_inc(lf_ready, 1)
            for hg in range(2):
                for tau in range(T):
                    act.wait_ge(qk_turned, 4 * hg + tau + 1)
                    if hg:
                        act.wait_ge(gram_done, len(STEPS))
                        act.wait_ge(pair_ready, pairs_upto(0, len(STEPS) - 1))
                    act.activation(qT[:, :, tau * P:(tau + 1) * P], bank[tau][:, :].rearrange("p (h t) -> p h t", h=4),
                                   ACT.Copy, scale=128.0 ** -0.5).then_inc(qk_saved, 1)
                for n, (kind, tau, lv) in enumerate(STEPS):
                    if kind == "diag":
                        continue
                    for u in range(2 if kind == "cross" else 1):
                        act.wait_ge(expo_done, decays_upto(hg, n) - (1 - u if kind == "cross" else 0))
                        b = u if kind == "cross" else n % 2
                        if hg or n >= 2:
                            act.wait_ge(pair_ready, pairs_upto(hg, n - 1) if kind == "cross" or n < 2 else pairs_upto(hg, n - 2))
                        act.activation(decay[b], bank[4 + b][:, :], ACT.Exp).then_inc(decay_ready, 1)
                for tau in range(T):
                    act.wait_ge(hg_copied, 2 * hg + tau + 1)
                    if 2 * hg + tau:
                        act.wait_ge(hg_saved, 2 * hg + tau)
                    act.activation(sqt, PJ[:, tau, HQ0 + 512 * hg:HQ0 + 512 * hg + 512], ACT.Square).then_inc(hg_sq, 1)
            act.wait_ge(hg_ms, 1)
            act.activation(rst, rst, ACT.Sqrt).then_inc(hg_root, 1)

            for n in range(12):
                act.wait_ge(q_turned, n + 1)
                if n < 8:
                    i = 4 * (n % 4)
                    tau, a = i // 8, i % 8
                    act.activation((qUT, qRT)[n // 4][:, a:a + 4, tau * P:(tau + 1) * P],
                                   bank[1 + n % 2][:, :].rearrange("p (a t) -> p a t", a=4),
                                   ACT.Copy, scale=DK ** -0.5).then_inc(q_saved, 1)
                else:
                    br, tau = (n - 8) // 2, n % 2
                    act.activation(kRT[:, br, :, tau * P:(tau + 1) * P],
                                   bank[5 + n % 2][:, :].rearrange("p (g t) -> p g t", g=4), ACT.Copy).then_inc(q_saved, 1)
            for n in range(2):
                act.wait_ge(piece_used, CMP_PIECE + 2 * (n + 1))
                if n:
                    act.wait_ge(hidT_done, n)
                act.activation(hid[0:60, :], bank[7][0:60, 0:256], ACT.Gelu_apprx_tanh).then_inc(hid_ready, 1)
            act.wait_ge(sc_in, 1)
            act.activation(sc, sc, ACT.Exp).then_inc(sc_exp, 1)
            for u, (br, g, tau) in enumerate(UNITS):
                act.wait_ge(s_max, u + 1)
                if u:
                    act.wait_ge(pT_done, u)
                if u >= 2:
                    act.wait_ge(o_used, u - 1)
                n = 128 * (tau + 1)
                for i in range(2):
                    for half in range(2):
                        h = 2 * i + half
                        act.activation(prob[:, h, 0:n], bank[2 * (u % 2) + half][:, i * n:(i + 1) * n], ACT.Exp,
                                       bias=nmx[:, 4 * (u % 2) + h:4 * (u % 2) + h + 1],
                                       accum_out=sums[:, 4 * (u % 2) + h:4 * (u % 2) + h + 1]).then_inc(p_ready, 1)
                if tau:
                    act.wait_ge(pT_done, u + 1)
                    act.wait_ge(o_done, u)
                    act.activation(probT[:, 4:8, :], bank[5][:, :].rearrange("p (h s) -> p h s", h=4),
                                   ACT.Copy).then_inc(pT_ready_b, 1)
            act.wait_ge(o_used, len(UNITS))
            squares(YN, 1)
            rms_act(act, 1, stat[:, 0:2])
            act.wait_ge(out_saved, 2 * OUT_CH)
            squares(X2, 2)
            rms_act(act, 2, stat[:, 0:2])
            act.wait_ge(r_in, 1)
            act.activation(r8[:, 0:8], r8[:, 0:8], ACT.Exp).then_inc(r_exp, 1)
            act.wait_ge(r_in, 2)
            act.activation(r8[:, 8:10], r8[:, 8:10], ACT.Exp).then_inc(r_exp, 1)

            def expert(done):
                act.wait_ge(dT_done, done + 1)
                act.activation(dispT.rearrange("p t q -> p (t q)"), bank[2][:, 0:256], ACT.Copy).then_inc(dT_saved, 1)
                act.wait_ge(piece_used, done * EP + (MOE_PIECE + 8))
                act.activation(hs[64:128, :], bank[3][0:64, :], ACT.Silu).then_inc(silu_done, 1)
                act.wait_ge(hT_done, done + 1)
                act.activation(hT.rearrange("p c s -> p (c s)"), bank[2][:, 256:512], ACT.Copy).then_inc(hT_saved, 1)
                act.wait_ge(piece_used, done * EP + (MOE_PIECE + EP))
                act.activation(yb[:, 0, :], bank[4][:, :], ACT.Copy).then_inc(y_saved_a, 1)

            with act.Fori(0, NE) as e:
                expert(e)
            act.wait_ge(pos_ready, 2)
            most = act.value_load(cnt_i[0:1, 0:1], min_val=0, max_val=SEQ)
            with act.If(most > SLOTS):
                for r in range(1, ROUNDS):
                    with act.Fori(0, NE) as e:
                        expert(e + r * NE)
            act.wait_ge(experts_done, 1)
            squares(X2, 3)
            rms_act(act, 3, stat[:, 0:2])

        @block.vector
        def _(dve):
            def run(ins):
                link(dve, "dve", ins)

            rstd = stat[:, 0:2]
            rms_dve(dve, 0, stat[:, 0:2], D, rstd)
            for tau in range(T):
                dve.tensor_scalar(XN[:, tau, :], XN[:, tau, :], rstd[:, tau:tau + 1], None, ALU.mult).then_inc(nat_ready, 1)
            dve.wait_ge(cst_loaded, CST_LOADS)
            turn_dve(dve, 0, XT, 0)

            dve.wait_ge(lb_loaded, 16)
            dve.wait_ge(small_loaded, 16)
            run(dve.tensor_tensor(LB, lbl[:, 0, :], lbl[:, 1, :], ALU.max))
            dve.tensor_tensor(lbl[:, 0, :], lbl[:, 0, :], LB, ALU.subtract).then_inc(dve_chain, 1)
            chain_value["dve"] += 1
            dve.tensor_tensor(lbl[:, 1, :], lbl[:, 1, :], LB, ALU.subtract).then_inc(lb_in, 1)
            dve.wait_ge(lb_exp, 1)
            run(dve.tensor_tensor(OMLB, lbl[:, 0, :], lbl[:, 1, :], ALU.add))
            run(dve.reciprocal(OMLB, OMLB))
            run(dve.tensor_tensor(LB, lbl[:, 0, :], OMLB, ALU.mult))
            run(dve.tensor_tensor(OMLB, lbl[:, 1, :], OMLB, ALU.mult))
            for tau in range(T):
                f = PJ[:, tau, HF0:HF0 + HG]
                dve.wait_ge(sig_ready, tau + 1)
                run(dve.tensor_tensor(LF[:, tau, :], f, OMLB, ALU.mult))
                run(dve.tensor_tensor(LF[:, tau, :], LF[:, tau, :], LB, ALU.add))
                dve.tensor_scalar(f, LF[:, tau, :], -1.0, 1.0, ALU.mult, ALU.add).then_inc(f_ready, 1)
            for hg in range(2):
                for tau in range(T):
                    dve.wait_ge(qk_turned, 4 * hg + 2 + tau + 1)
                    dve.tensor_copy(kT[:, :, tau * P:(tau + 1) * P],
                                    bank[2 + tau][:, :].rearrange("p (h t) -> p h t", h=4)).then_inc(qk_saved, 1)
                dve.wait_ge(qk_saved, 4 * (hg + 1))

                def decayed(n):
                    kind, tau, lv = STEPS[n]
                    if kind == "diag":
                        return
                    dve.wait_ge(decay_ready, decays_upto(hg, n))
                    if hg or n >= 2:
                        dve.wait_ge(gram_done, hg * len(STEPS) + max(n - 1, 0))
                    if kind == "cross":
                        v = [pair[i].rearrange("p (h t) -> p h t", h=4) for i in range(2)]
                        d = [decay[i].rearrange("p (h t) -> p h t", h=4) for i in range(2)]
                        dve.tensor_tensor(v[0], d[0], qT[:, :, P:2 * P], ALU.mult).then_inc(pair_ready, 1)
                        dve.tensor_tensor(v[1], d[1], kT[:, :, 0:P], ALU.mult).then_inc(pair_ready, 1)
                        return
                    w = LEVELS[lv]

                    def halves(a, side):
                        return a.rearrange("p (b two w) -> p b two w", two=2, w=w)[:, :, side, :]

                    for side, src in ((1, qT), (0, kT)):
                        if w == 64:
                            s_ = src[:, :, tau * P + 64 * side:tau * P + 64 * side + 64]
                            dve.tensor_tensor(halves(pair[n % 2], side), halves(decay[n % 2], side), s_,
                                              ALU.mult).then_inc(pair_ready, 1)
                        else:
                            s_ = src[:, :, tau * P:(tau + 1) * P].rearrange("p h (b two w) -> p h b two w", two=2, w=w)[:, :, :, side, :]
                            v, d = (a.rearrange("p (h b two w) -> p h b two w", h=4, two=2, w=w)[:, :, :, side, :]
                                    for a in (pair[n % 2], decay[n % 2]))
                            dve.tensor_tensor(v, d, s_, ALU.mult).then_inc(pair_ready, 1)

                def masked(n):
                    kind, tau, lv = STEPS[n]
                    g = hg * len(STEPS) + n
                    dve.wait_ge(gram_done, g + 1)
                    b = bank[6 + g % 2][:, :].rearrange("p (h t) -> p h t", h=4)
                    if kind == "cross":
                        dve.tensor_copy(att[2], bank[6 + g % 2][:, :]).then_inc(gram_used, 1)
                        return
                    m = B_GM + (lv if kind == "level" else NL) * 128
                    first = kind == "level" and lv == 0
                    if first and hg:
                        dve.wait_ge(hg_out, 2)
                    if not first:
                        adds = sum(1 for s in STEPS[:max(n - 1, 0)] if not (s[0] == "cross" or (s[0] == "level" and s[2] == 0)))
                        if hg * ADDS + adds:
                            dve.wait_ge(part_added, hg * ADDS + adds)
                    elif hg:
                        dve.wait_ge(part_added, hg * ADDS)
                    dst = (att[tau] if first else part[n % 2]).rearrange("p (h t) -> p h t", h=4)
                    dve.tensor_tensor(dst, b, cbf[:, m:m + 128].unsqueeze(1).to_broadcast([P, 4, P]),
                                      ALU.mult).then_inc(gram_used, 1)

                decayed(0)
                for n in range(len(STEPS)):
                    if n + 1 < len(STEPS):
                        decayed(n + 1)
                    masked(n)
                for tau in range(T):
                    dve.wait_ge(hg_out, 2 * hg + tau + 1)
                    dve.tensor_copy(PJ[:, tau, HQ0 + 512 * hg:HQ0 + 512 * hg + 512], bank[tau][:, :]).then_inc(hg_copied, 1)
                    dve.wait_ge(hg_sq, 2 * hg + tau + 1)
                    dve.tensor_reduce(rst[:, tau * 8 + 4 * hg:tau * 8 + 4 * hg + 4],
                                      sqt.rearrange("p (h v) -> p h v", h=4), AX, ALU.add).then_inc(hg_saved, 1)
            dve.wait_ge(hg_saved, 4)
            dve.tensor_scalar(rst, rst, 1.0 / 128, EPS, ALU.mult, ALU.add).then_inc(hg_ms, 1)
            for tau in range(T):
                cos = cst[:, C_COS + tau * 32:C_COS + tau * 32 + 32].unsqueeze(1).to_broadcast([P, NH, 32])
                sin = cst[:, C_SIN + tau * 32:C_SIN + tau * 32 + 32].unsqueeze(1).to_broadcast([P, NH, 32])
                src = PJ[:, tau, NQ0:NQ0 + NH * DK].rearrange("p (h a d) -> p h a d", h=NH, a=2)
                dq = QR[:, tau, :].rearrange("p (h a d) -> p h a d", h=NH, a=2)
                qt = tmp.rearrange("p (h d) -> p h d", h=NH)
                for half, op in ((0, ALU.subtract), (1, ALU.add)):
                    run(dve.tensor_tensor(dq[:, :, half, :], src[:, :, half, :], cos, ALU.mult))
                    run(dve.tensor_tensor(qt, src[:, :, 1 - half, :], sin, ALU.mult))
                    last = dve.tensor_tensor(dq[:, :, half, :], dq[:, :, half, :], qt, op)
                    if tau == T - 1 and half == 1:
                        last.then_inc(rope_done, 1)
                    else:
                        run(last)
            dve.wait_ge(hg_root, 1)
            run(dve.reciprocal(rst, rst))
            dve.wait_ge(silu_ready, 2)
            for tau in range(T):
                o = PJ[:, tau, 0:HG].rearrange("p (h v) -> p h v", h=HH)
                run(dve.tensor_tensor(o, o, rst[:, tau * 8:tau * 8 + 8].unsqueeze(2).to_broadcast([P, HH, 128]), ALU.mult))
                run(dve.tensor_tensor(PJ[:, tau, 0:HG], PJ[:, tau, 0:HG], PJ[:, tau, HG0:HG0 + HG], ALU.mult))

            dve.wait_ge(kv_turned, 1)
            run(dve.tensor_copy(posT[:, :, :].rearrange("p n m -> p (n m)"), bank[0][:, 0:32]))
            run(dve.memset(hrep, 0.0))
            run(dve.memset(sc, 0.0))
            for n in range(2):
                dve.wait_ge(kv_turned, n + 2)
                b = bank[3 + n][:, :].rearrange("p (a t) -> p a t", a=2)
                v = kvT[n].rearrange("p (a two) t -> p a two t", two=2)
                for two in range(2):
                    rows = slice(64 * two, 64 * two + 64)
                    run(dve.tensor_copy(v[0:64, :, two, :], b[rows, :, :]))
                    run(dve.tensor_copy(v[64:128, :, two, 0:SEQ - 1], b[rows, :, 1:SEQ]))
            for n in range(2):
                if n:
                    dve.wait_ge(piece_used, CMP_PIECE + 2)
                for i in range(2):
                    src = kvT[n].rearrange("p g (b m two) -> p m g b two", m=8, two=2)[:, :, :, i:i + NCMP, 0]
                    pos = posT[:, n, 8 * i:8 * i + 8].unsqueeze(2).unsqueeze(3).to_broadcast([P, 8, NG, NCMP])
                    for g in range(NG):
                        ins = dve.tensor_tensor(flat[:, 8 * i:8 * i + 8, g, :], src[:, :, g, :], pos[:, :, g, :], ALU.add)
                        if i == 1 and g == NG - 1:
                            ins.then_inc(flat_ready, 1)
                        else:
                            run(ins)
                dve.wait_ge(hidT_done, n + 1)
                hb = bank[0][:, 0:128].rearrange("p (f x) -> p f x", f=2)
                if n == 0:
                    dve.tensor_copy(hidT[0][:, :, 0:60], hb[:, :, 0:60]).then_inc(hidT_ready, 1)
                    dve.wait_ge(cmp_done, 1)
                    dve.tensor_copy(kcT[:, 0:60], bank[0][:, 256:316]).then_inc(cmp_ready, 1)
                else:
                    for o in range(2):
                        for f in range(2):
                            src = hb[:, f, 0:60].rearrange("p (g n) -> p g n", g=4)[:, 2 * o:2 * o + 2, :]
                            ins = dve.tensor_copy(hrep[:, o, f, :, :, 0:NCMP],
                                                  src.unsqueeze(2).to_broadcast([P, 2, 4, NCMP]))
                            if o and f:
                                ins.then_inc(hidT_ready, 1)
                            else:
                                run(ins)
                    dve.wait_ge(cmp_done, 2)
                    for o in range(2):
                        ins = dve.tensor_tensor(vbd[:, o, :, :],
                                                bank[7][:, o * 64:o * 64 + 64].unsqueeze(1).to_broadcast([P, 8, DK]),
                                                cst[:, C_BD:C_BD + 8].unsqueeze(2).to_broadcast([P, 8, DK]), ALU.mult)
                        if o:
                            ins.then_inc(cmp_ready, 1)
                        else:
                            run(ins)
            cm = cst[:, C_CM:C_CM + 32].rearrange("p (t n) -> p t n", t=T)
            cn = cst[:, C_CN:C_CN + 32].rearrange("p (t n) -> p t n", t=T)
            dve.wait_ge(sc_done, 1)
            for tau in range(T):
                sh = sc[:, tau, :, :].rearrange("p (a two) n -> p a two n", two=2)
                for half in range(2):
                    b = bank[1 + half][:, tau * 128:tau * 128 + 128].rearrange("p (a n) -> p a n", a=8)[:, :, 0:NCMP]
                    run(dve.tensor_tensor(sh[:, :, half, 0:NCMP], b,
                                          cm[:, tau, 0:NCMP].unsqueeze(1).to_broadcast([P, 8, NCMP]), ALU.mult))
                run(dve.tensor_tensor(sc[:, tau, :, 0:NCMP], sc[:, tau, :, 0:NCMP],
                                      cn[:, tau, 0:NCMP].unsqueeze(1).to_broadcast([P, NH, NCMP]), ALU.add))
            mx = tmp[:, 0:32].rearrange("p (t h) -> p t h", t=T)
            sm = tmp[:, 32:64].rearrange("p (t h) -> p t h", t=T)
            run(dve.tensor_reduce(mx, sc[:, :, :, 0:NCMP], AX, ALU.max))
            for tau in range(T):
                ins = dve.tensor_tensor(sc[:, tau, :, 0:NCMP], sc[:, tau, :, 0:NCMP],
                                        mx[:, tau, :].unsqueeze(2).to_broadcast([P, NH, NCMP]), ALU.subtract)
                if tau:
                    ins.then_inc(sc_in, 1)
                else:
                    run(ins)
            dve.wait_ge(sc_exp, 1)
            for tau in range(T):
                run(dve.tensor_tensor(sc[:, tau, :, :], sc[:, tau, :, :], cm[:, tau, :].unsqueeze(1).to_broadcast([P, NH, 16]), ALU.mult))
            run(dve.tensor_reduce(sm, sc, AX, ALU.add))
            for tau in range(T):
                run(dve.tensor_scalar(sm[:, tau, :], sm[:, tau, :], cst[:, C_NV + tau:C_NV + tau + 1], None, ALU.add))
            run(dve.reciprocal(sm, sm))
            for tau in range(T):
                ins = dve.tensor_tensor(sc[:, tau, :, :], sc[:, tau, :, :], sm[:, tau, :].unsqueeze(2).to_broadcast([P, NH, 16]), ALU.mult)
                if tau:
                    ins.then_inc(pc_ready, 1)
                else:
                    run(ins)
            dve.wait_ge(pcT_done, 1)
            dve.tensor_copy(pcT.rearrange("p t o q -> p (t o q)"), bank[3][:, :]).then_inc(pcT_ready, 1)
            dve.wait_ge(gates_ready, 1)
            dve.wait_ge(q_turned, 8)
            for tau in range(T):
                for o in range(2):
                    dve.wait_ge(oc_done, 2 * tau + o + 1)
                    dve.tensor_tensor(YN[:, tau, 512 * o:512 * o + 512].rearrange("p (h d) -> p h d", h=8),
                                      bank[4 + o][:, :].rearrange("p (h d) -> p h d", h=8),
                                      gates[:, tau, 8 * o:8 * o + 8, 0].unsqueeze(2).to_broadcast([P, 8, DK]),
                                      ALU.mult).then_inc(oc_used, 1)
            dve.wait_ge(oc_used, 4)

            def maxima(u):
                br, g, tau = UNITS[u]
                n = 128 * (tau + 1)
                dve.wait_ge(s_done, u + 1)
                if u >= 2:
                    dve.wait_ge(p_ready, 4 * (u - 1))
                m = nmx[:, 4 * (u % 2):4 * (u % 2) + 4].rearrange("p (i half) -> p i half", half=2)
                for half in range(2):
                    run(dve.tensor_reduce(m[:, :, half], bank[2 * (u % 2) + half][:, 0:2 * n].rearrange("p (i s) -> p i s", i=2),
                                          AX, ALU.max))
                dve.tensor_scalar(nmx[:, 4 * (u % 2):4 * (u % 2) + 4], nmx[:, 4 * (u % 2):4 * (u % 2) + 4], -1.0, None,
                                  ALU.mult).then_inc(s_max, 1)

            maxima(0)
            for u, (br, g, tau) in enumerate(UNITS):
                if u + 1 < len(UNITS):
                    maxima(u + 1)
                dve.wait_ge(pT_done, u + 1)
                if u:
                    dve.wait_ge(o_done, u)
                dve.tensor_copy(probT[:, 0:4, :], bank[4][:, :].rearrange("p (h s) -> p h s", h=4)).then_inc(pT_ready, 1)
                dve.wait_ge(p_ready, 4 * (u + 1))
                su = sums[:, 4 * (u % 2):4 * (u % 2) + 4]
                sg = sums[:, 8 + 4 * (u % 2):12 + 4 * (u % 2)]
                run(dve.reciprocal(sg, su))
                run(dve.tensor_tensor(sg, sg, gates[:, tau, 4 * g:4 * g + 4, 1 + br], ALU.mult))
                dve.wait_ge(o_done, u + 1)
                t4 = tmp[:, 0:256].rearrange("p (h d) -> p h d", h=4)
                run(dve.tensor_tensor(t4, bank[6 + u % 2][:, 0:256].rearrange("p (h d) -> p h d", h=4),
                                      sg.unsqueeze(2).to_broadcast([P, 4, DK]), ALU.mult))
                y = YN[:, tau, 256 * g:256 * g + 256]
                dve.tensor_tensor(y, y, tmp[:, 0:256], ALU.add).then_inc(o_used, 1)
                dve.wait_ge(o_used, u + 1)
            rms_dve(dve, 1, stat[:, 0:2], NH * DK, rstd)
            for tau in range(T):
                dve.tensor_scalar(YN[:, tau, :], YN[:, tau, :], rstd[:, tau:tau + 1], None, ALU.mult).then_inc(nat_ready, 1)
            turn_dve(dve, 1, XT, 1)

            dve.wait_ge(res_loaded, 32)
            for ch in range(OUT_CH):
                dve.wait_ge(piece_used, OUT_PIECE + PP * (ch + 1))
                for tau in range(T):
                    r = X2[:, tau, ch * NCH:(ch + 1) * NCH]
                    dve.tensor_tensor(r, r, bank[2 * (ch % 2) + tau][:, :], ALU.add).then_inc(out_saved, 1)
            dve.wait_ge(out_saved, 2 * OUT_CH)
            rms_dve(dve, 2, stat[:, 0:2], D, rstd)
            for tau in range(T):
                dve.tensor_scalar(XS[:, tau, :], X2[:, tau, :], rstd[:, tau:tau + 1], None, ALU.mult).then_inc(nat_ready, 1)
            run(dve.memset(ones, 1.0))
            turn_dve(dve, 2, XT, 2)

            dve.wait_ge(route_loaded, 64)
            dve.wait_ge(logit_done, 1)
            run(dve.tensor_tensor(LG, bank[4][:, 0:72].rearrange("p (t n) -> p t n", t=T),
                                  rbias.unsqueeze(1).to_broadcast([P, T, 36]), ALU.add))
            w = r8
            lg, le = LG[:, :, 0:4], LG[:, :, 4:36]
            m1 = w[:, 10:12]
            col = [w[:, 10 + 2 * n:12 + 2 * n] for n in range(14)]
            m1, gw, mxi, v1, v2, ex, p1, p2 = col[:8]

            def wide(a, n):
                return a.unsqueeze(2).to_broadcast([P, T, n])

            ohg = w[:, 40:48].rearrange("p (t n) -> p t n", t=T)
            ohb = w[:, 48:56].rearrange("p (t n) -> p t n", t=T)
            eg = w[:, 0:8].rearrange("p (t n) -> p t n", t=T)
            oh1, oh2 = (scr[:, 512 + 64 * n:576 + 64 * n].rearrange("p (t n) -> p t n", t=T) for n in range(2))

            def first_max(dst, src, m, n, rev):
                run(dve.tensor_reduce(m, src, AX, ALU.max))
                run(dve.tensor_tensor(dst, src, wide(m, n), ALU.is_ge))
                run(dve.tensor_tensor(dst, dst, rev.unsqueeze(1).to_broadcast([P, T, n]), ALU.mult))
                run(dve.tensor_reduce(mxi, dst, AX, ALU.max))
                run(dve.tensor_tensor(dst, dst, wide(mxi, n), ALU.is_equal))

            first_max(ohg, lg, m1, 4, cst[:, C_REV:C_REV + 4])
            dve.tensor_tensor(eg, lg, wide(m1, 4), ALU.subtract).then_inc(r_in, 1)
            dve.wait_ge(r_exp, 1)
            run(dve.tensor_reduce(gw, eg, AX, ALU.add))
            run(dve.reciprocal(gw, gw))
            run(dve.tensor_scalar(ohb, ohg, NEG, -NEG, ALU.mult, ALU.add))
            for tau in range(T):
                e4 = LG[:, tau, 4:36].rearrange("p (g e) -> p g e", g=4)
                run(dve.tensor_tensor(e4, e4, ohg[:, tau, :].unsqueeze(2).to_broadcast([P, 4, 8]), ALU.mult))
                run(dve.tensor_tensor(e4, e4, ohb[:, tau, :].unsqueeze(2).to_broadcast([P, 4, 8]), ALU.add))
            first_max(oh1, le, v1, 32, cst[:, C_REV + 4:C_REV + 36])
            run(dve.scalar_tensor_tensor(le, oh1, -3.0 * NEG, le, ALU.mult, ALU.add))
            first_max(oh2, le, v2, 32, cst[:, C_REV + 4:C_REV + 36])
            ed = w[:, 8:10]
            dve.tensor_tensor(ed, v2, v1, ALU.subtract).then_inc(r_in, 1)
            dve.wait_ge(r_exp, 2)
            run(dve.tensor_scalar(p1, ed, 1.0, None, ALU.add))
            run(dve.reciprocal(p1, p1))
            run(dve.tensor_tensor(p1, p1, gw, ALU.mult))
            run(dve.tensor_tensor(p2, p1, ed, ALU.mult))
            run(dve.memset(wt, 0.0))
            run(dve.memset(posm, 0.0))
            wt_, posm_ = wt[:, :, 0:NE], posm[:, :, 0:NE]
            run(dve.tensor_tensor(wt_, oh1, wide(p1, 32), ALU.mult))
            run(dve.tensor_tensor(posm_, oh2, wide(p2, 32), ALU.mult))
            run(dve.tensor_tensor(wt_, wt_, posm_, ALU.add))
            dve.tensor_tensor(sel, oh1, oh2, ALU.add).then_inc(sel_ready, 1)
            dve.wait_ge(sel_ready, 1)
            dve.wait_ge(pos_done, 1)
            run(dve.scalar_tensor_tensor(posm_, bank[5][:, 0:64].rearrange("p (t n) -> p t n", t=T), 1.0, sel, ALU.add, ALU.mult))
            run(dve.tensor_reduce(mxi[:, 0:1], bank[5][:, 64:96], AX, ALU.max))
            run(dve.tensor_copy(cnt_i[:, 0:1], mxi[:, 0:1]))
            dve.tensor_scalar(posm, posm, -1.0, None, ALU.add).then_inc(pos_ready, 2)
            dve.wait_ge(pos_ready, 2)
            dve.memset(yb, 0.0).then_inc(scat_used, 8)

            def dispatch(e, nth):
                dve.tensor_tensor(disp, cst[:, C_IOTA:C_IOTA + SLOTS].unsqueeze(1).to_broadcast([P, T, SLOTS]),
                                  posm[:, :, bass.ds(e, 1)].to_broadcast([P, T, SLOTS]),
                                  ALU.is_equal).then_inc(disp_hot, 1)
                dve.wait_ge(disp_hot, nth + 1)
                for u in range(2):
                    dve.tensor_tensor(dispw[:, :, u, :], disp, wt[:, :, bass.ds(e, 1)].to_broadcast([P, T, SLOTS]),
                                      ALU.mult).then_inc(disp_ready, 1)

            def expert(e, done, r):
                dve.wait_ge(scat_used, done * 8 + 8)
                for half in range(2):
                    dve.wait_ge(gath_done, done * 2 + (half + 1))
                    dve.tensor_tensor(xg[:, 8 * half:8 * half + 8, :], bank[half][:, :].rearrange("p (c s) -> p c s", c=8),
                                      gain[:, 2 * KC + 8 * half:2 * KC + 8 * half + 8].unsqueeze(2).to_broadcast([P, 8, SLOTS]),
                                      ALU.mult).then_inc(gath_saved, 1)
                dve.wait_ge(silu_done, done + 1)
                dve.tensor_tensor(hv[64:128, :], bank[3][64:128, :], hs[64:128, :], ALU.mult).then_inc(h_ready, 1)
                dve.wait_ge(dT_done, done + 1)
                dispatch(e + 1, done + (1 + r))
                dve.wait_ge(piece_used, done * EP + (MOE_PIECE + EP))
                dve.tensor_copy(yb[:, 1, :], bank[5][:, :]).then_inc(y_saved_d, 1)
                for tau in range(T):
                    for n in range(4):
                        dve.wait_ge(scat_done, done * 8 + (4 * tau + n + 1))
                        r = X2[:, tau, n * NCH:(n + 1) * NCH]
                        dve.tensor_tensor(r, r, bank[(6, 7, 0, 1)[n]][:, :], ALU.add).then_inc(scat_used, 1)

            dispatch(0, 0)
            with dve.Fori(0, NE) as e:
                expert(e, e, 0)
            most = dve.value_load(cnt_i[0:1, 0:1], min_val=0, max_val=SEQ)
            with dve.If(most > SLOTS):
                for r in range(1, ROUNDS):
                    dve.tensor_scalar(posm, posm, -1.0 * SLOTS, None, ALU.add).then_inc(pos_ready, 1)
                    dve.wait_ge(pos_ready, 2 + r)
                    dispatch(0, (NE + 1) * r)
                    with dve.Fori(0, NE) as e:
                        expert(e, e + r * NE, r)
            dve.wait_ge(scat_used, 8 * NE + 8)
            dve.memset(cnt_i[:, 1:2], 0).then_inc(experts_done, 1)
            rms_dve(dve, 3, stat[:, 0:2], D, rstd)
            dve.wait_ge(fin_loaded, 16)
            for tau in range(T):
                dve.scalar_tensor_tensor(XS[:, tau, :], X2[:, tau, :], rstd[:, tau:tau + 1], fgain, ALU.mult,
                                         ALU.mult).then_inc(final_ready, 1)


_INS = ["x", "attn_norm", "w_in", "hg_lb_logits", "hg_out_norm", "cmp_pos_k", "cmp_w1_k", "cmp_w2_k", "cmp_pos_v",
        "cmp_w1_v", "cmp_w2_v", "nsa_out_norm", "w_out", "ffn_norm", "moe_w_group", "moe_b_group", "moe_w_router",
        "moe_b_router", "moe_w_gate", "moe_w_up", "moe_w_down", "final_norm"]


def kernel(**inputs):
    import ml_dtypes as _ml
    import concourse.bacc as _bacc
    from concourse.bass_utils import run_bass_kernel_spmd as _run

    nc = _bacc.Bacc("TRN2", target_bir_lowering=False, num_devices=1)
    arrays, args = {}, []
    c, b = tables()
    for name, a in [(n, inputs[n]) for n in _INS] + [("consts", c), ("consts_bf", b.astype(_ml.bfloat16))]:
        a = np.ascontiguousarray(a)
        arrays[f"in_{name}"] = a
        args.append(nc.dram_tensor(f"in_{name}", a.shape, mybir.dt.from_np(a.dtype), kind="ExternalInput").ap())
    args.append(nc.dram_tensor("out_0", (1, SEQ, D), F32, kind="ExternalOutput").ap())
    hybrid_block(nc, *args)
    r = _run(nc, [arrays], core_ids=[0])
    return r.results[0]["out_0"]
```

```python
from contextlib import ExitStack

import concourse.bass as bass
from concourse import mybir
import numpy as np

F32 = mybir.dt.float32
BF16 = mybir.dt.bfloat16
I32 = mybir.dt.int32
ALU = mybir.AluOpType
ACT = mybir.ActivationFunctionType
AX = mybir.AxisListType.X

P = 128
SEQ = 256
D = 2048
T = SEQ // P
KC = D // P
HG = 1024
HH = 8
NH, NG, DK = 16, 4, 64
NCMP = 15
IN_COLS = 4 * HG + NH * DK + 6 * NG * DK + 3 * NH
HQ0, HF0, HI0, HG0, NQ0 = 0, HG, 2 * HG, 3 * HG, 4 * HG
KC0 = NQ0 + NH * DK
VC0, KS0, VS0, KW0, VW0, GR0 = (KC0 + n * NG * DK for n in range(1, 7))
NCH = 512
IN_CH = GR0 // NCH
GATE_CH = IN_CH
ORDER = [2, 3, 0, 1, 4, 5, 8, 9, 10, 11, 12, 6, 7, GATE_CH]
EARLY = 6
OUT_CH = D // NCH
PIECE = 2048
FRONT_SLOTS = 8
PP = D * NCH // (P * PIECE)
NE, FF = 32, 512
SLOTS = 64
ROUNDS = SEQ // SLOTS
EP = 12
LEVELS = [64, 32, 16, 8, 4, 2, 1]
NL = len(LEVELS)
EPS = 1e-6
NEG = 1e30

C_ID = 0
C_LT = C_ID + 128
C_M = C_LT + 128
C_COS = C_M + (NL + 2) * 128
C_SIN = C_COS + T * 32
C_CM = C_SIN + T * 32
C_CN = C_CM + T * 16
C_NV = C_CN + T * 16
C_BD = C_NV + T
C_IOTA = C_BD + 8
C_REV = C_IOTA + SLOTS
C_N = C_REV + 36
B_ID = 0
B_CAUSAL = 128
B_GM = B_CAUSAL + 512
B_N = B_GM + (NL + 1) * 128


def tables():
    c = np.zeros((P, C_N), np.float32)
    b = np.zeros((P, B_N), np.float32)
    s, t = np.arange(P)[:, None], np.arange(P)[None, :]
    c[:, C_ID:C_ID + 128] = s == t
    c[:, C_LT:C_LT + 128] = s < t
    for n, h in enumerate(LEVELS):
        start = t // (2 * h) * (2 * h)
        right = t % (2 * h) >= h
        c[:, C_M + n * 128:C_M + n * 128 + 128] = np.where(
            right, (s >= start + h) & (s <= t), (s > t) & (s < start + h))
        b[:, B_GM + n * 128:B_GM + n * 128 + 128] = (s // (2 * h) == t // (2 * h)) & (s % (2 * h) < h) & right
    c[:, C_M + NL * 128:C_M + NL * 128 + 128] = s <= t
    c[:, C_M + (NL + 1) * 128:C_M + (NL + 2) * 128] = s > t
    b[:, B_GM + NL * 128:] = s == t
    b[:, B_ID:B_ID + 128] = s == t
    b[:, B_CAUSAL:B_CAUSAL + 512] = np.concatenate([np.zeros((P, 128)), np.where(t <= s, 0, -NEG)] * 2, 1)
    inv = (1.0 / (np.float32(10000.0) ** (np.arange(0, DK, 2, dtype=np.float32) / np.float32(DK)))).astype(np.float32)
    ang = np.arange(SEQ, dtype=np.float32)[:, None] * inv[None, :]
    for tau in range(T):
        rows = np.arange(P) + tau * P
        c[:, C_COS + tau * 32:C_COS + tau * 32 + 32] = np.cos(ang[rows])
        c[:, C_SIN + tau * 32:C_SIN + tau * 32 + 32] = np.sin(ang[rows])
        m = (np.arange(16)[None, :] * 16 + 31 <= rows[:, None]) & (np.arange(16)[None, :] < NCMP)
        c[:, C_CM + tau * 16:C_CM + tau * 16 + 16] = m
        c[:, C_CN + tau * 16:C_CN + tau * 16 + 16] = (m - 1.0) * NEG
        c[:, C_NV + tau] = ~m.any(1)
    c[:, C_BD:C_BD + 8] = s // 16 == np.arange(8)[None, :]
    c[:, C_IOTA:C_IOTA + SLOTS] = np.arange(SLOTS)
    c[:, C_REV:C_REV + 4] = 4 - np.arange(4)
    c[:, C_REV + 4:C_REV + 36] = 32 - np.arange(32)
    return c, b


def hybrid_block(nc, x, attn_norm, w_in, hg_lb_logits, hg_out_norm, cmp_pos_k, cmp_w1_k, cmp_w2_k,
                 cmp_pos_v, cmp_w1_v, cmp_w2_v, nsa_out_norm, w_out, ffn_norm, moe_w_group, moe_b_group,
                 moe_w_router, moe_b_router, moe_w_gate, moe_w_up, moe_w_down, final_norm, consts, consts_bf, out):
    with ExitStack() as ctx:
        def sb(name, cols, dt=F32):
            return ctx.enter_context(nc.sbuf_tensor(name, [P, cols], dt))

        def sem(name):
            return ctx.enter_context(nc.semaphore(name))

        ctx.enter_context(nc.allow_non_contiguous_dma(reason="small transposed gains and position tables"))

        ring = sb("ring", EP * PIECE)
        proj = sb("proj", T * IN_COLS)
        xt = sb("xt", KC * SEQ)
        scr = sb("scr", 8192)
        cst = sb("cst", C_N)
        cbf = sb("cbf", B_N, BF16)
        stat = sb("stat", 128)
        gain = sb("gain", 3 * KC)
        cnt_i = sb("cnt_i", 2, I32)
        bank = [ctx.enter_context(nc.psum_tensor(f"bank{n}", [P, 512], F32)) for n in range(8)]

        PJ = proj[:, :].rearrange("p (t c) -> p t c", t=T)
        XT = xt[:, :].rearrange("p (c t) -> p c t", c=KC)
        ident = cst[:, C_ID:C_ID + 128]

        def slot(n, inner):
            n = n % FRONT_SLOTS
            return ring[:, n * PIECE:(n + 1) * PIECE].rearrange("p (a b) -> p a b", b=inner)

        work = ring[:, FRONT_SLOTS * PIECE:EP * PIECE]
        XN = scr[:, 0:T * D].rearrange("p (t c) -> p t c", t=T)
        WGATE = work[:, 6144:6144 + KC * 48].rearrange("p (c n) -> p c n", c=KC)

        cst_loaded = sem("cst_loaded")
        x_loaded = sem("x_loaded")
        slot_loaded = [sem(f"slot_loaded{n}") for n in range(EP)]
        piece_used = sem("piece_used")
        small_loaded = sem("small_loaded")
        lb_loaded = sem("lb_loaded")
        w2_loaded = sem("w2_loaded")
        route_loaded = sem("route_loaded")
        fin_loaded = sem("fin_loaded")
        stored = sem("stored")
        sq_ready = sem("sq_ready")
        ms_ready = sem("ms_ready")
        root_ready = sem("root_ready")
        nat_ready = sem("nat_ready")
        turned = sem("turned")
        turned_used = sem("turned_used")
        gate_cols_done = sem("gate_cols_done")
        proj_saved = sem("proj_saved")
        dve_chain = sem("dve_chain")
        act_chain = sem("act_chain")
        pool_chain = sem("pool_chain")

        chain_value = {"dve": 0, "act": 0, "pool": 0}
        chain_sem = {"dve": dve_chain, "act": act_chain, "pool": pool_chain}

        def link(eng, name, ins):
            chain_value[name] += 1
            ins.then_inc(chain_sem[name], 1)
            eng.wait_ge(chain_sem[name], chain_value[name])

        lb_exp = sem("lb_exp")
        lb_in = sem("lb_in")
        sig_ready = sem("sig_ready")
        f_ready = sem("f_ready")
        lf_ready = sem("lf_ready")
        qk_turned = sem("qk_turned")
        q_copied = sem("q_copied")
        k_copied = sem("k_copied")
        expo_done = sem("expo_done")
        decay_ready = sem("decay_ready")
        pair_ready = sem("pair_ready")
        gram_done = sem("gram_done")
        gram_used = sem("gram_used")
        part_added = sem("part_added")
        hg_out = sem("hg_out")
        hg_saved = sem("hg_saved")
        hg_sq = sem("hg_sq")
        hg_copied = sem("hg_copied")
        hg_ms = sem("hg_ms")
        hg_root = sem("hg_root")
        silu_ready = sem("silu_ready")
        hg_final = sem("hg_final")
        zeros_ready = sem("zeros_ready")

        def rms_dve(dve, n, ss, width, rstd):
            dve.wait_ge(sq_ready, n + 1)
            dve.tensor_scalar(rstd, ss, 1.0 / width, EPS, ALU.mult, ALU.add).then_inc(ms_ready, 1)
            dve.wait_ge(root_ready, n + 1)
            link(dve, "dve", dve.reciprocal(rstd, rstd))

        def rms_act(act, n, rstd):
            act.wait_ge(ms_ready, n + 1)
            act.activation(rstd, rstd, ACT.Sqrt).then_inc(root_ready, 1)

        def turn_pe(pe, first, src, banks):
            n = src.shape[2] // P
            for k in range(T * n // 4):
                tau, cg = k // (n // 4), k % (n // 4)
                if k >= len(banks):
                    pe.wait_ge(turned_used, first + k - len(banks) + 1)
                for j in range(4):
                    c = 4 * cg + j
                    last = pe.transpose(banks[k % len(banks)][:, j * 128:(j + 1) * 128],
                                        src[:, tau, c:c + 127 * n + 1:n], ident)
                last.then_inc(turned, 1)

        def turn_dve(dve, first, width, chunk0, g, banks):
            n = width // P
            for k in range(T * n // 4):
                tau, c = k // (n // 4), chunk0 + 4 * (k % (n // 4))
                dve.wait_ge(turned, first + k + 1)
                dve.tensor_tensor(XT[:, c:c + 4, tau * P:(tau + 1) * P],
                                  banks[k % len(banks)][:, :].rearrange("p (c t) -> p c t", c=4),
                                  gain[:, g * KC + c:g * KC + c + 4].unsqueeze(2).to_broadcast([P, 4, P]),
                                  ALU.mult).then_inc(turned_used, 1)

        def proj_bank(q, tau):
            return bank[2 * (q % 2) + tau] if q < EARLY else bank[tau]

        qT = work[:, 0:1024].rearrange("p (h t) -> p h t", h=4)
        kT = work[:, 1024:2048].rearrange("p (h t) -> p h t", h=4)
        att = [work[:, 2048 + 512 * n:2560 + 512 * n] for n in range(3)]
        lbl = work[:, 4096:6144].rearrange("p (a c) -> p a c", a=2)
        LF = scr[:, 0:2048].rearrange("p (t c) -> p t c", t=T)
        decay = [scr[:, 2048 + 512 * n:2560 + 512 * n] for n in range(2)]
        pair = [scr[:, 3072 + 512 * n:3584 + 512 * n] for n in range(2)]
        part = [scr[:, 4096 + 512 * n:4608 + 512 * n] for n in range(2)]
        sqt = scr[:, 7168:7680]
        LB = scr[:, 5120:6144]
        OMLB = scr[:, 6144:7168]
        rst = stat[:, 16:32]
        STEPS = [("level", tau, n) for tau in range(T) for n in range(NL)] + [("diag", 0, 0), ("diag", 1, 0), ("cross", 0, 0)]
        ADDS = T * NL
        ktmp = sb("ktmp", 128)
        sums = sb("sums", 16)
        nmx = sb("nmx", 8)


        def decays_upto(hg, n):
            return hg * (T * NL + 2) + sum({"level": 1, "diag": 0, "cross": 2}[s[0]] for s in STEPS[:n + 1])

        def pairs_upto(hg, n):
            return hg * (2 * T * NL + 2) + sum({"level": 2, "diag": 0, "cross": 2}[s[0]] for s in STEPS[:n + 1])

        qUT = work[:, 4096:6144].rearrange("p (a t) -> p a t", a=8)
        qRT = work[:, 6144:8192].rearrange("p (a t) -> p a t", a=8)
        kRT = [PJ[:, :, c:c + HG].rearrange("p z (g t) -> p z g t", g=4) for c in (NQ0, HG0)]
        kcz = scr[:, 0:128].rearrange("p (z x) -> p z x", z=2)
        kvT = [scr[:, 2048 + 1024 * n:3072 + 1024 * n].rearrange("p (g t) -> p g t", g=4) for n in range(2)]
        prob = scr[:, 2048:3072].rearrange("p (h s) -> p h s", h=4)
        probT = scr[:, 3072:4096].rearrange("p (h s) -> p h s", s=128)
        flat = scr[:, 4096:5056].rearrange("p (m g n) -> p m g n", m=16, g=4)
        hid = scr[:, 5056:5312]
        hidT = [scr[:, 5312 + 128 * n:5440 + 128 * n].rearrange("p (f m) -> p f m", f=2) for n in range(2)]
        hrep = scr[:, 5568:6080].rearrange("p (o f g r n) -> p o f g r n", o=2, f=2, g=2, r=4)
        vbd = scr[:, 6144:7168].rearrange("p (o h d) -> p o h d", o=2, h=8)
        sc = scr[:, 7168:7680].rearrange("p (t h n) -> p t h n", t=T, h=NH)
        pcT = scr[:, 5056:5568].rearrange("p (t o q) -> p t o q", t=T, o=2)
        tmp = scr[:, 7680:8192]
        QR = PJ[:, :, HF0:HF0 + HG]
        KR = PJ[:, :, HI0:HI0 + HG].rearrange("p t (b g u d) -> p t b g u d", b=2, g=4, u=2)
        YN = PJ[:, :, HF0:HF0 + HG]
        w2k = cst[:, C_M:C_M + 256].rearrange("p (f u d) -> p f u d", f=2, u=2)
        w2v = cst[:, C_M + 256:C_M + 384].rearrange("p (f d) -> p f d", f=2)
        posn = cst[0:16, C_M + 384:C_M + 640].rearrange("p (n x) -> p n x", n=2)
        posT = cst[:, C_M + 640:C_M + 672].rearrange("p (n m) -> p n m", n=2)

        q_turned = sem("q_turned")
        q_saved = sem("q_saved")
        rope_done = sem("rope_done")
        kv_turned = sem("kv_turned")
        kv_saved = sem("kv_saved")
        flat_ready = sem("flat_ready")
        hid_done = sem("hid_done")
        hid_ready = sem("hid_ready")
        hidT_done = sem("hidT_done")
        hidT_ready = sem("hidT_ready")
        cmp_done = sem("cmp_done")
        cmp_ready = sem("cmp_ready")
        sc_done = sem("sc_done")
        sc_in = sem("sc_in")
        sc_exp = sem("sc_exp")
        pc_ready = sem("pc_ready")
        pcT_done = sem("pcT_done")
        pcT_ready = sem("pcT_ready")
        oc_done = sem("oc_done")
        oc_used = sem("oc_used")
        gates_ready = sem("gates_ready")
        s_done = sem("s_done")
        s_max = sem("s_max")
        p_ready = sem("p_ready")
        pT_done = sem("pT_done")
        pT_ready = sem("pT_ready")
        o_done = sem("o_done")
        o_used = sem("o_used")
        XR = work[:, 0:T * D].rearrange("p (t c) -> p t c", t=T)
        pT_ready_b = sem("pT_ready_b")
        UNITS = [(br, g, tau) for br in range(2) for g in range(NG) for tau in range(T)]
        gates = stat[:, 32:128].rearrange("p (t h b) -> p t h b", t=T, h=NH)

        X2 = proj[:, 0:T * D].rearrange("p (t c) -> p t c", t=T)
        XS = proj[:, T * D:2 * T * D].rearrange("p (t c) -> p t c", t=T)
        mo = 2 * T * D
        WR = proj[:, mo:mo + KC * 36].rearrange("p (c n) -> p c n", c=KC)
        rbias = proj[:, mo + 576:mo + 612]
        fgain = proj[:, mo + 640:mo + 640 + D]
        LG = scr[:, 0:72].rearrange("p (t n) -> p t n", t=T)
        sel = scr[:, 72:136].rearrange("p (t n) -> p t n", t=T)
        wt = scr[:, 640:640 + T * (NE + 1)].rearrange("p (t n) -> p t n", t=T)
        posm = scr[:, 720:720 + T * (NE + 1)].rearrange("p (t n) -> p t n", t=T)
        ones = scr[:, 264:392]
        r8 = scr[:, 392:512]
        disp = scr[:, 1024:1152].rearrange("p (t s) -> p t s", t=T)
        dispw = scr[:, 1152:1408].rearrange("p (t u s) -> p t u s", t=T, u=2)
        dispT = scr[:, 1408:1664].rearrange("p (t q) -> p t q", t=T)
        xg = scr[:, 2048:3072].rearrange("p (c s) -> p c s", c=KC)
        hs = scr[:, 3072:3584]
        hv = scr[:, 3584:4096]
        hT = scr[:, 4096:4352].rearrange("p (c s) -> p c s", c=4)
        yb = scr[:, 4608:4608 + D]

        out_done = sem("out_done")
        out_saved = sem("out_saved")
        out0_done = sem("out0_done")
        out0_saved = sem("out0_saved")
        res_loaded = sem("res_loaded")
        logit_done = sem("logit_done")
        r_in = sem("r_in")
        r_exp = sem("r_exp")
        sel_ready = sem("sel_ready")
        pos_done = sem("pos_done")
        pos_ready = sem("pos_ready")
        disp_ready = sem("disp_ready")
        dispw_ready = sem("dispw_ready")
        gath_done = sem("gath_done")
        gath_saved = sem("gath_saved")
        dT_done = sem("dT_done")
        dT_saved = sem("dT_saved")
        gu_done = sem("gu_done")
        silu_done = sem("silu_done")
        h_ready = sem("h_ready")
        hT_done = sem("hT_done")
        hT_saved = sem("hT_saved")
        down_done = sem("down_done")
        y_saved_a = sem("y_saved_a")
        y_saved_d = sem("y_saved_d")
        scat_done = sem("scat_done")
        scat_used = sem("scat_used")
        final_ready = sem("final_ready")
        experts_done = sem("experts_done")

        x_v = x.rearrange("b (t p) d -> (b p) t d", p=P)
        out_v = out.rearrange("b (t p) d -> (b p) t d", p=P)
        win_v = w_in[0].rearrange("(p c) n -> p c n", p=P)
        wout_v = w_out[0].rearrange("(h p c) n -> h p c n", h=2, p=P)
        gate_v = moe_w_gate[0].rearrange("e (p c) n -> e p (c n)", p=P)
        up_v = moe_w_up[0].rearrange("e (p c) n -> e p (c n)", p=P)
        down_v = moe_w_down[0].rearrange("e (p c) n -> e p (c n)", p=P)

        CST_LOADS = 16 * 13
        CMP_PIECE = IN_CH * PP
        OUT_PIECE = CMP_PIECE + 4
        MOE_PIECE = OUT_PIECE + OUT_CH * PP
        assert MOE_PIECE % FRONT_SLOTS == 0

        def piece_ready(eng, n):
            eng.wait_ge(slot_loaded[n % FRONT_SLOTS], 16 * (n // FRONT_SLOTS + 1))

        def expert_piece(eng, k, done):
            before = MOE_PIECE // FRONT_SLOTS if k < FRONT_SLOTS else 0
            eng.wait_ge(slot_loaded[k], 16 * done + 16 * (before + 1))

        LATE = [(q, i) for q in range(EARLY, IN_CH) for i in range(PP)] + [(IN_CH, 0)]
        PLACES = 2 * (len(STEPS) + 1)

        def late_pieces(place):
            return LATE[place * len(LATE) // PLACES:(place + 1) * len(LATE) // PLACES]

        OUT0 = [(ch, tau) for ch in range(OUT_CH) for tau in range(T)]
        OUT0_AFTER = [2, 4, 6, 8, 10, 12, 13, 14]

        block = ctx.enter_context(nc.Block())

        @block.sync
        def _(sp):
            for tau in range(T):
                sp.dma_start(XN[:, tau, :], x_v[:, tau, :]).then_inc(x_loaded, 16)

            def load(n, src, inner):
                if n >= FRONT_SLOTS:
                    sp.wait_ge(piece_used, n - FRONT_SLOTS + 1)
                sp.dma_start(slot(n, inner), src).then_inc(slot_loaded[n % FRONT_SLOTS], 16)

            sp.wait_ge(cst_loaded, CST_LOADS)
            for q, ch in enumerate(ORDER[:IN_CH]):
                for i in range(PP):
                    load(q * PP + i, win_v[:, 4 * i:4 * i + 4, ch * NCH:(ch + 1) * NCH], NCH)
            for n, w in enumerate((cmp_w1_k, cmp_w1_v)):
                v = w[0].rearrange("(m p) n -> p m n", p=P)
                for i in range(2):
                    load(CMP_PIECE + 2 * n + i, v[:, 8 * i:8 * i + 8, :], 256)
            for half in range(2):
                for ch in range(OUT_CH):
                    for i in range(2):
                        load(OUT_PIECE + half * 8 + ch * 2 + i,
                             wout_v[half, :, 4 * i:4 * i + 4, ch * NCH:(ch + 1) * NCH], NCH)

            def expert_loads(e, done):
                for k in range(EP):
                    if isinstance(done, int) and done == 0:
                        if k < FRONT_SLOTS:
                            sp.wait_ge(piece_used, MOE_PIECE - FRONT_SLOTS + k + 1)
                        elif k == FRONT_SLOTS:
                            sp.wait_ge(out_saved, 2 * OUT_CH)
                    else:
                        sp.wait_ge(piece_used, done * EP + (MOE_PIECE - EP + k + 1))
                    w, j = ((gate_v, up_v)[k % 2], k // 2) if k < 8 else (down_v, k - 8)
                    sp.dma_start(ring[:, k * PIECE:(k + 1) * PIECE],
                                 w[bass.ds(e, 1), :, j * PIECE:(j + 1) * PIECE].rearrange("e p n -> (e p) n")
                                 ).then_inc(slot_loaded[k], 16)

            expert_loads(0, 0)
            with sp.Fori(1, NE) as e:
                expert_loads(e, e)
            sp.wait_ge(pos_ready, 2)
            most = sp.value_load(cnt_i[0:1, 0:1], min_val=0, max_val=SEQ)
            with sp.If(most > SLOTS):
                for r in range(1, ROUNDS):
                    with sp.Fori(0, NE) as e:
                        expert_loads(e, e + r * NE)
            sp.wait_ge(final_ready, 2)
            sp.dma_start(out_v, XS).then_inc(stored, 16)
            sp.wait_ge(stored, 16)

        @block.gpsimd
        def _(pool):

            pool.dma_start(WGATE, win_v[:, :, GR0:IN_COLS]).then_inc(small_loaded, 16)

            pool.dma_start(lbl, hg_lb_logits.rearrange("(o a) c -> o a c", o=1).to_broadcast([P, 2, HG])
                           ).then_inc(lb_loaded, 16)
            k = 0
            for hg in range(2):
                for n, (kind, tau, lv) in enumerate(STEPS):
                    if kind == "cross" or (kind == "level" and lv == 0):
                        continue
                    pool.wait_ge(gram_used, hg * len(STEPS) + n + 1)
                    if k:
                        pool.wait_ge(part_added, k)
                    pool.tensor_tensor(att[tau], att[tau], part[n % 2], ALU.add).then_inc(part_added, 1)
                    k += 1

            pool.wait_ge(hg_saved, 4)
            for tau in range(T):
                pool.dma_start(XR[:, tau, :], x_v[:, tau, :]).then_inc(res_loaded, 16)
            pool.wait_ge(expo_done, 2 * (T * NL + 2))
            pool.dma_start(w2v[:, :, :], cmp_w2_v[0].rearrange("(f p) d -> p f d", p=P)).then_inc(w2_loaded, 16)
            for u in range(2):
                pool.dma_start(w2k[:, :, u, :], cmp_w2_k[0].rearrange("(f p) d -> p f d", p=P)).then_inc(w2_loaded, 16)
            for n, w in enumerate((cmp_pos_k, cmp_pos_v)):
                pool.dma_start(posn[:, n, :], w[0].rearrange("(m a) d -> m (a d)", a=2)).then_inc(w2_loaded, 16)
            pool.wait_ge(hg_out, 4)
            for tau in range(T):
                cos = cst[:, C_COS + tau * 32:C_COS + tau * 32 + 32].unsqueeze(1).to_broadcast([P, NG, 32])
                sin = cst[:, C_SIN + tau * 32:C_SIN + tau * 32 + 32].unsqueeze(1).to_broadcast([P, NG, 32])
                kt = ktmp[:, :].rearrange("p (g d) -> p g d", g=NG)
                for br, col in enumerate((KS0, KW0)):
                    src = PJ[:, tau, col:col + 256].rearrange("p (g a d) -> p g a d", g=NG, a=2)
                    for half, op in ((0, ALU.subtract), (1, ALU.add)):
                        dst = KR[:, tau, br, :, 0, 32 * half:32 * half + 32]
                        link(pool, "pool", pool.tensor_tensor(dst, src[:, :, half, :], cos, ALU.mult))
                        link(pool, "pool", pool.tensor_tensor(kt, src[:, :, 1 - half, :], sin, ALU.mult))
                        link(pool, "pool", pool.tensor_tensor(dst, dst, kt, op))
                    last = pool.tensor_copy(KR[:, tau, br, :, 1, :], KR[:, tau, br, :, 0, :])
                    if tau == T - 1 and br == 1:
                        last.then_inc(rope_done, 1)
                    else:
                        link(pool, "pool", last)

            pool.wait_ge(q_turned, 4)
            pool.wait_ge(rope_done, 2)
            pool.wait_ge(hg_final, 2)
            for c in (NQ0, HG0):
                pool.memset(PJ[64:128, 0, c:c + HG], 0.0).then_inc(zeros_ready, 1)
                pool.memset(PJ[0:64, 1, c:c + HG], 0.0).then_inc(zeros_ready, 1)

            pool.wait_ge(turned, 16)
            pool.dma_start(WR[:, :, 0:4], moe_w_group[0].rearrange("(p c) n -> p c n", p=P)).then_inc(route_loaded, 16)
            pool.dma_start(WR[:, :, 4:36], moe_w_router[0].rearrange("(p c) n -> p c n", p=P)).then_inc(route_loaded, 16)
            pool.dma_start(rbias[:, 0:4], moe_b_group.to_broadcast([P, 4])).then_inc(route_loaded, 16)
            pool.dma_start(rbias[:, 4:36], moe_b_router.to_broadcast([P, NE])).then_inc(route_loaded, 16)
            pool.dma_start(fgain, final_norm.rearrange("(o d) -> o d", o=1).to_broadcast([P, D])).then_inc(fin_loaded, 16)

        @block.tensor
        def _(pe):
            pe.wait_ge(cst_loaded, CST_LOADS)
            front = [bank[n] for n in range(4)]
            pe.wait_ge(nat_ready, 2)
            turn_pe(pe, 0, XN, front)
            pe.wait_ge(turned_used, 8)

            def project(q, i):
                ch = ORDER[q]
                if i == 0:
                    if q == EARLY:
                        pe.wait_ge(proj_saved, q - 1)
                    elif q >= 2:
                        pe.wait_ge(proj_saved, q if q > EARLY else q - 1)
                width, steps = (48, range(KC)) if ch == GATE_CH else (NCH, range(4 * i, 4 * i + 4))
                if ch == GATE_CH:
                    pe.wait_ge(small_loaded, 16)
                else:
                    piece_ready(pe, q * PP + i)
                for tau in range(T):
                    for c in steps:
                        rhs = WGATE[:, c, :] if ch == GATE_CH else slot(q * PP + i, NCH)[:, c % 4, :]
                        last = pe.matmul(proj_bank(q, tau)[:, 0:width], XT[:, c, tau * P:(tau + 1) * P], rhs,
                                         start=c == 0, stop=c == KC - 1)
                last.then_inc(gate_cols_done if ch == GATE_CH else piece_used, 1)

            for q in range(EARLY):
                for i in range(PP):
                    project(q, i)

            pe.wait_ge(lf_ready, 2)
            pe.wait_ge(proj_saved, EARLY)
            place = 0
            for hg in range(2):
                for n in range(4):
                    what, tau = n // 2, n % 2
                    if n >= 2:
                        pe.wait_ge(q_copied, 2 * hg + n - 1)
                    elif hg:
                        pe.wait_ge(hg_copied, n + 1)
                    for j in range(4):
                        h = 4 * hg + j
                        col = (HQ0, HF0)[what] + h * 128
                        last = pe.transpose(bank[2 + n % 2][:, j * 128:(j + 1) * 128], PJ[:, tau, col:col + 128], ident)
                    last.then_inc(qk_turned, 1)
                for q, i in late_pieces(place):
                    project(q, i)
                place += 1
                pe.wait_ge(q_copied, 2 * (hg + 1))
                pe.wait_ge(k_copied, 2 * (hg + 1))

                def exponents(n):
                    kind, tau, lv = STEPS[n]
                    g = hg * len(STEPS) + n
                    if kind == "diag":
                        return
                    b = bank[4 + n % 2]
                    if kind == "level":
                        if n >= 2:
                            pe.wait_ge(decay_ready, decays_upto(hg, n - 2))
                        for j in range(4):
                            h = 4 * hg + j
                            last = pe.matmul(b[:, j * 128:(j + 1) * 128], LF[:, tau, h * 128:(h + 1) * 128],
                                             cst[:, C_M + lv * 128:C_M + lv * 128 + 128], start=True, stop=True)
                        last.then_inc(expo_done, 1)
                    else:
                        pe.wait_ge(decay_ready, decays_upto(hg, n - 1))
                        for u in range(2):
                            for j in range(4):
                                h = 4 * hg + j
                                m = C_M + (NL + u) * 128
                                last = pe.matmul(bank[4 + u][:, j * 128:(j + 1) * 128],
                                                 LF[:, 1 - u, h * 128:(h + 1) * 128],
                                                 cst[:, m:m + 128], start=True, stop=True)
                            last.then_inc(expo_done, 1)

                def products(n):
                    kind, tau, lv = STEPS[n]
                    g = hg * len(STEPS) + n
                    if g >= 2:
                        pe.wait_ge(gram_used, g - 1)
                    if kind != "diag":
                        pe.wait_ge(pair_ready, pairs_upto(hg, n))
                    b = bank[6 + g % 2]
                    for j in range(4):
                        sl = slice(j * 128, (j + 1) * 128)
                        if kind == "level":
                            l = r = pair[n % 2][:, sl]
                        elif kind == "diag":
                            l, r = kT[:, j, tau * P:(tau + 1) * P], qT[:, j, tau * P:(tau + 1) * P]
                        else:
                            l, r = pair[1][:, sl], pair[0][:, sl]
                        last = pe.matmul(b[:, sl], l, r, start=True, stop=True)
                    last.then_inc(gram_done, 1)

                exponents(0)
                for n in range(len(STEPS)):
                    if n + 1 < len(STEPS):
                        exponents(n + 1)
                    products(n)
                    for q, i in late_pieces(place):
                        project(q, i)
                    place += 1
                pe.wait_ge(gram_used, len(STEPS) * (hg + 1))
                pe.wait_ge(part_added, ADDS * (hg + 1))
                for tau in range(T):
                    for j in range(4):
                        h = 4 * hg + j
                        sl = slice(j * 128, (j + 1) * 128)
                        v = [PJ[:, t, HI0 + h * 128:HI0 + h * 128 + 128] for t in range(T)]
                        if tau == 0:
                            last = pe.matmul(bank[2][:, sl], att[0][:, sl], v[0], start=True, stop=True)
                        else:
                            pe.matmul(bank[3][:, sl], att[2][:, sl], v[0], start=True, stop=False)
                            last = pe.matmul(bank[3][:, sl], att[1][:, sl], v[1], start=False, stop=True)
                    last.then_inc(hg_out, 1)

            pe.wait_ge(hg_copied, 4)
            pe.wait_ge(proj_saved, IN_CH + 1)
            pe.wait_ge(w2_loaded, 80)
            for n in range(2):
                last = pe.transpose(bank[0][:, n * 16:(n + 1) * 16], posn[:, n, :], ident[0:16, 0:16])
            last.then_inc(kv_turned, 1)
            for n in range(4):
                if n >= 2:
                    pe.wait_ge(q_saved, n - 1)
                for j in range(4):
                    i = 4 * n + j
                    tau, a = i // 8, i % 8
                    last = pe.transpose(bank[1 + n % 2][:, j * 128:(j + 1) * 128],
                                        PJ[:, tau, NQ0 + a * 128:NQ0 + a * 128 + 128], ident)
                last.then_inc(q_turned, 1)
            for n in range(2):
                for j in range(4):
                    a, tau = j // 2, j % 2
                    col = (KC0, VC0)[n] + a * 128
                    last = pe.transpose(bank[3 + n][:, j * 128:(j + 1) * 128], PJ[:, tau, col:col + 128], ident)
                last.then_inc(kv_turned, 1)
            pe.wait_ge(rope_done, 2)
            for n in range(4):
                pe.wait_ge(q_saved, 3 + n)
                for j in range(4):
                    i = 4 * n + j
                    tau, a = i // 8, i % 8
                    last = pe.transpose(bank[1 + n % 2][:, j * 128:(j + 1) * 128], QR[:, tau, a * 128:(a + 1) * 128], ident)
                last.then_inc(q_turned, 1)
            for n in range(4):
                br, tau = n // 2, n % 2
                if n >= 2:
                    pe.wait_ge(q_saved, 8 + 2 * (n - 1))
                for g in range(NG):
                    last = pe.transpose(bank[5 + n % 2][:, g * 128:(g + 1) * 128],
                                        PJ[:, tau, HI0 + (br * 4 + g) * 128:HI0 + (br * 4 + g + 1) * 128], ident)
                last.then_inc(q_turned, 1)
            pe.wait_ge(hg_final, 2)
            pe.wait_ge(q_saved, 8)
            turn_pe(pe, 8, PJ[:, :, 0:HG], [bank[2], bank[7]])
            pe.wait_ge(turned_used, 12)

            def out_first(j):
                ch, tau = OUT0[j]
                if j:
                    pe.wait_ge(out0_saved, j)
                for i in range(2):
                    n = OUT_PIECE + 2 * ch + i
                    piece_ready(pe, n)
                    for cc in range(4):
                        c = 4 * i + cc
                        last = pe.matmul(bank[6][:, :], XT[:, c, tau * P:(tau + 1) * P], slot(n, NCH)[:, cc, :],
                                         start=c == 0, stop=c == 7)
                    if tau:
                        last.then_inc(piece_used, 1)
                if not tau:
                    last.then_inc(out0_done, 1)

            for n in range(2):
                pe.wait_ge(flat_ready, n + 1)
                for i in range(2):
                    piece_ready(pe, CMP_PIECE + 2 * n + i)
                    for mm in range(8):
                        m = 8 * i + mm
                        last = pe.matmul(bank[7][0:60, 0:256], flat[:, m, :, :].rearrange("p g n -> p (g n)"),
                                         slot(CMP_PIECE + 2 * n + i, 256)[:, mm, :], start=m == 0, stop=m == 15)
                    last.then_inc(piece_used, 1)
                pe.wait_ge(hid_ready, n + 1)
                for f in range(2):
                    last = pe.transpose(bank[0][:, 64 * f:64 * f + 60], hid[0:60, f * 128:(f + 1) * 128], ident[0:60, 0:60])
                last.then_inc(hidT_done, 1)
                pe.wait_ge(hidT_ready, n + 1)
                if n == 0:
                    for f in range(2):
                        last = pe.matmul(bank[0][:, 256:316], w2k[:, f, :, :].rearrange("p u d -> p (u d)"),
                                         hidT[0][:, f, 0:60], start=f == 0, stop=f == 1)
                    last.then_inc(cmp_done, 1)
                else:
                    for o in range(2):
                        for f in range(2):
                            last = pe.matmul(bank[7][:, o * 64:o * 64 + 64],
                                             hrep[:, o, f, :, :, :].rearrange("p g r n -> p (g r n)"),
                                             w2v[:, f, :], start=f == 0, stop=f == 1)
                    last.then_inc(cmp_done, 1)
            pe.wait_ge(cmp_ready, 1)
            pe.wait_ge(q_saved, 16)
            for tau in range(T):
                for a in range(NH // 2):
                    o = bank[1][:, tau * 256 + a * 32:tau * 256 + a * 32 + 32].rearrange("p (z n) -> p z n", z=2)
                    g = a // 2
                    last = pe.matmul(o[:, :, 0:NCMP], qUT[:, a, tau * P:(tau + 1) * P],
                                     kcz[:, :, g * NCMP:(g + 1) * NCMP], start=True, stop=True)
            last.then_inc(sc_done, 1)
            pe.wait_ge(pc_ready, 1)
            for tau in range(T):
                for o in range(2):
                    last = pe.transpose(bank[3][:, (2 * tau + o) * 128:(2 * tau + o + 1) * 128],
                                        sc[:, tau, 8 * o:8 * o + 8, :].rearrange("p h n -> p (h n)"), ident)
            last.then_inc(pcT_done, 1)
            pe.wait_ge(pcT_ready, 1)
            pe.wait_ge(cmp_ready, 2)
            for tau in range(T):
                for o in range(2):
                    if 2 * tau + o >= 2:
                        pe.wait_ge(oc_used, 2 * tau + o - 1)
                    last = pe.matmul(bank[4 + o][:, :], pcT[:, tau, o, :], vbd[:, o, :, :].rearrange("p h d -> p (h d)"),
                                     start=True, stop=True)
                    last.then_inc(oc_done, 1)
            pe.wait_ge(oc_used, 4)

            def scores(u):
                br, g, tau = UNITS[u]
                if u >= 2:
                    pe.wait_ge(p_ready, 4 * (u - 1))
                n = 128 * (tau + 1)
                for i in range(2):
                    b = bank[2 * (u % 2) + i][:, 0:2 * n].rearrange("p (z s) -> p z s", z=2)
                    mask = cbf[:, B_CAUSAL:B_CAUSAL + 512].rearrange("p (z s) -> p z s", z=2)[:, :, 256 - n:256]
                    pe.matmul(b, cbf[:, B_ID:B_ID + 128], mask, start=True, stop=False, skip_group_check=True)
                    last = pe.matmul(b, qRT[:, 2 * g + i, tau * P:(tau + 1) * P], kRT[br][:, :, g, 0:n],
                                     start=False, stop=True, skip_group_check=True)
                last.then_inc(s_done, 1)

            def values(u):
                br, g, tau = UNITS[u]
                pe.wait_ge(p_ready, 4 * (u + 1))
                for sb_ in range(tau + 1):
                    for h in range(4):
                        last = pe.transpose(bank[4 + sb_][:, h * 128:(h + 1) * 128],
                                            prob[:, h, sb_ * 128:(sb_ + 1) * 128], ident)
                last.then_inc(pT_done, 1)
                pe.wait_ge(pT_ready, u + 1)
                if tau:
                    pe.wait_ge(pT_ready_b, u // 2 + 1)
                if u:
                    pe.wait_ge(o_used, u)
                v0 = (VS0, VW0)[br] + g * DK
                for h in range(4):
                    for sb_ in range(tau + 1):
                        last = pe.matmul(bank[7][:, h * DK:(h + 1) * DK], probT[:, 4 * sb_ + h, :],
                                         PJ[:, sb_, v0:v0 + DK], start=sb_ == 0, stop=sb_ == tau)
                last.then_inc(o_done, 1)

            scores(0)
            for u in range(len(UNITS)):
                if u + 1 < len(UNITS):
                    scores(u + 1)
                for j, at in enumerate(OUT0_AFTER):
                    if at == u:
                        out_first(j)
                values(u)

            pe.wait_ge(nat_ready, 4)
            turn_pe(pe, 12, YN, front)
            pe.wait_ge(turned_used, 16)
            for ch in range(OUT_CH):
                if ch >= 2:
                    pe.wait_ge(out_saved, 2 * (ch - 1))
                for i in range(2):
                    n = OUT_PIECE + 8 + 2 * ch + i
                    piece_ready(pe, n)
                    for tau in range(T):
                        for cc in range(4):
                            c = 4 * i + cc
                            last = pe.matmul(bank[2 * (ch % 2) + tau][:, :], XT[:, 8 + c, tau * P:(tau + 1) * P],
                                             slot(n, NCH)[:, cc, :], start=c == 0, stop=c == 7)
                    last.then_inc(piece_used, 1)

            pe.wait_ge(nat_ready, 6)
            pe.wait_ge(out_saved, 2 * OUT_CH)
            turn_pe(pe, 16, XS, front)
            pe.wait_ge(turned_used, 24)
            pe.wait_ge(route_loaded, 64)
            for tau in range(T):
                for c in range(KC):
                    last = pe.matmul(bank[4][:, tau * 36:tau * 36 + 36], XT[:, c, tau * P:(tau + 1) * P], WR[:, c, :],
                                     start=c == 0, stop=c == KC - 1)
            last.then_inc(logit_done, 1)
            pe.wait_ge(sel_ready, 1)
            lt = cst[:, C_LT:C_LT + 128]
            pe.matmul(bank[5][:, 0:32], lt, sel[:, 0, :], start=True, stop=True)
            pe.matmul(bank[5][:, 32:64], ones, sel[:, 0, :], start=True, stop=False)
            pe.matmul(bank[5][:, 32:64], lt, sel[:, 1, :], start=False, stop=True)
            pe.matmul(bank[5][:, 64:96], ones, sel[:, 0, :], start=True, stop=False)
            pe.matmul(bank[5][:, 64:96], ones, sel[:, 1, :], start=False, stop=True).then_inc(pos_done, 1)

            def gather(nth):
                pe.wait_ge(disp_ready, nth + 1)
                for half in range(2):
                    for cc in range(8):
                        c = 8 * half + cc
                        for tau in range(T):
                            last = pe.matmul(bank[half][:, cc * SLOTS:(cc + 1) * SLOTS], XS[:, tau, c:c + 127 * KC + 1:KC],
                                             disp[:, tau, :], start=tau == 0, stop=tau == T - 1)
                    last.then_inc(gath_done, 1)

            def gate_up(done, nth):
                for j in range(4):
                    expert_piece(pe, 2 * j, done)
                    expert_piece(pe, 2 * j + 1, done)
                    if j % 2 == 0:
                        pe.wait_ge(gath_saved, 2 * nth + (j // 2 + 1))
                    for cc in range(4):
                        c = 4 * j + cc
                        for u in range(2):
                            last = pe.matmul(bank[3][64 * u:64 * u + 64, :], xg[:, c, :],
                                             ring[:, (2 * j + u) * PIECE + cc * NCH:(2 * j + u) * PIECE + (cc + 1) * NCH],
                                             start=c == 0, stop=c == KC - 1)
                            if cc == 3:
                                last.then_inc(piece_used, 1)

            def turn_hidden(done):
                pe.wait_ge(h_ready, done + 1)
                for c in range(4):
                    last = pe.matmul(bank[2][:, 256 + c * 64:256 + c * 64 + 64], hv[64:128, c:c + 127 * 4 + 1:4],
                                     ident[64:128, 64:128], start=True, stop=True)
                last.then_inc(hT_done, 1)

            def scatter(pair, k):
                if k == 0:
                    pe.wait_ge(dT_saved, pair + 1)
                    pe.wait_ge(y_saved_a, 4 * pair + 4)
                    pe.wait_ge(y_saved_d, 4 * pair + 6)
                pe.wait_ge(scat_used, 8 * pair + (k + 1))
                pe.matmul(bank[6 + k % 2][:, :], dispT[:, k // 4, :], yb[:, (k % 4) * NCH:(k % 4 + 1) * NCH],
                          start=True, stop=True).then_inc(scat_done, 1)

            def down(done, pair=None):
                pe.wait_ge(hT_saved, done + 1)
                for c in range(4):
                    expert_piece(pe, 8 + c, done)
                    if c == 0:
                        pe.wait_ge(y_saved_d, 2 * done + 2)
                        if not (isinstance(done, int) and done == 0):
                            pe.wait_ge(y_saved_a, 2 * done)
                    for n in range(4):
                        last = pe.matmul(bank[4 + n // 2][64 * (n % 2):64 * (n % 2) + 64, :], hT[:, c, :],
                                         ring[:, (8 + c) * PIECE + n * NCH:(8 + c) * PIECE + (n + 1) * NCH],
                                         start=c == 0, stop=c == 3)
                    last.then_inc(piece_used, 1)
                    if pair is not None:
                        scatter(pair, 2 * c)
                        scatter(pair, 2 * c + 1)

            def pair_of_experts(pair, r, first):
                done, nth = 2 * pair, 2 * pair + r
                gate_up(done, nth)
                pe.wait_ge(dispw_ready, 2 * pair + (2 + r))
                for tau in range(T):
                    last = pe.transpose(bank[2][:, tau * 128:(tau + 1) * 128],
                                        dispw[:, tau, :, :].rearrange("p u s -> p (u s)"), ident)
                last.then_inc(dT_done, 1)
                gather(nth + 1)
                turn_hidden(done)
                down(done, None if first else pair - 1)
                gate_up(done + 1, nth + 1)
                gather(nth + 2)
                turn_hidden(done + 1)
                down(done + 1)

            def one_round(r):
                gather(r * (NE + 1))
                pair_of_experts(r * NE // 2, r, True)
                with pe.Fori(1, NE // 2) as i:
                    pair_of_experts(i + r * NE // 2, r, False)
                for k in range(8):
                    scatter((r + 1) * NE // 2 - 1, k)

            one_round(0)
            pe.wait_ge(pos_ready, 2)
            most = pe.value_load(cnt_i[0:1, 0:1], min_val=0, max_val=SEQ)
            with pe.If(most > SLOTS):
                for r in range(1, ROUNDS):
                    one_round(r)

        @block.scalar
        def _(act):
            act.dma_start(cst[:, :], consts).then_inc(cst_loaded, 16)
            act.dma_start(cbf[:, :], consts_bf).then_inc(cst_loaded, 16)
            act.dma_start(gain[:, 0:KC], attn_norm[0].rearrange("(p c) -> p c", p=P)).then_inc(cst_loaded, 16)
            for h in range(8):
                act.dma_start(gain[16 * h:16 * h + 16, KC:KC + 8], hg_out_norm[0].rearrange("(p c) -> p c", c=8)
                              ).then_inc(cst_loaded, 16)
            act.dma_start(gain[:, KC + 8:2 * KC], nsa_out_norm[0].rearrange("(p c) -> p c", p=P)).then_inc(cst_loaded, 16)
            act.dma_start(gain[:, 2 * KC:3 * KC], ffn_norm[0].rearrange("(p c) -> p c", p=P)).then_inc(cst_loaded, 16)

            def squares(src, n, junk):
                link(act, "act", act.activation(junk, src[:, 0, :], ACT.Square, accum_out=stat[:, 0:1]))
                act.activation(junk, src[:, 1, :], ACT.Square, accum_out=stat[:, 1:2]).then_inc(sq_ready, 1)

            act.wait_ge(x_loaded, 32)
            squares(XN, 0, xt[:, 0:D])
            rms_act(act, 0, stat[:, 0:2])

            def save(q):
                ch = ORDER[q]
                if ch == GATE_CH:
                    act.wait_ge(gate_cols_done, 1)
                else:
                    act.wait_ge(piece_used, PP * (q + 1))
                width = 48 if ch == GATE_CH else NCH
                link(act, "act", act.activation(PJ[:, 0, ch * NCH:ch * NCH + width], proj_bank(q, 0)[:, 0:width], ACT.Copy))
                act.activation(PJ[:, 1, ch * NCH:ch * NCH + width], proj_bank(q, 1)[:, 0:width],
                               ACT.Copy).then_inc(proj_saved, 1)

            act.wait_ge(lb_in, 1)
            act.activation(lbl, lbl, ACT.Exp).then_inc(lb_exp, 1)
            save(0)
            save(1)
            act.wait_ge(proj_saved, 2)
            for tau in range(T):
                act.activation(PJ[:, tau, HF0:HF0 + HG], PJ[:, tau, HF0:HF0 + HG], ACT.Sigmoid).then_inc(sig_ready, 1)
            save(2)
            for tau in range(T):
                act.wait_ge(f_ready, tau + 1)
                act.activation(LF[:, tau, :], LF[:, tau, :], ACT.Ln).then_inc(lf_ready, 1)
            for q in range(3, EARLY):
                save(q)

            def save_late(place):
                for q, i in late_pieces(place):
                    if i == PP - 1 or ORDER[q] == GATE_CH:
                        save(q)

            place = 0
            for hg in range(2):
                for tau in range(T):
                    act.wait_ge(qk_turned, 4 * hg + tau + 1)
                    if hg:
                        act.wait_ge(gram_done, len(STEPS))
                        act.wait_ge(pair_ready, pairs_upto(0, len(STEPS) - 1))
                    act.activation(qT[:, :, tau * P:(tau + 1) * P], bank[2 + tau][:, :].rearrange("p (h t) -> p h t", h=4),
                                   ACT.Copy, scale=128.0 ** -0.5).then_inc(q_copied, 1)

                def decays(n):
                    kind, tau, lv = STEPS[n]
                    if kind == "diag":
                        return
                    for u in range(2 if kind == "cross" else 1):
                        act.wait_ge(expo_done, decays_upto(hg, n) - (1 - u if kind == "cross" else 0))
                        b = u if kind == "cross" else n % 2
                        if hg or n >= 2:
                            act.wait_ge(pair_ready, pairs_upto(hg, n - 1) if kind == "cross" or n < 2 else pairs_upto(hg, n - 2))
                        act.activation(decay[b], bank[4 + b][:, :], ACT.Exp).then_inc(decay_ready, 1)

                save_late(place)
                place += 1
                decays(0)
                for n in range(len(STEPS)):
                    if n + 1 < len(STEPS):
                        decays(n + 1)
                    save_late(place)
                    place += 1
                for tau in range(T):
                    act.wait_ge(hg_copied, 2 * hg + tau + 1)
                    if 2 * hg + tau:
                        act.wait_ge(hg_saved, 2 * hg + tau)
                    act.activation(sqt, PJ[:, tau, HQ0 + 512 * hg:HQ0 + 512 * hg + 512], ACT.Square).then_inc(hg_sq, 1)
            act.wait_ge(proj_saved, IN_CH + 1)
            for tau in range(T):
                act.activation(PJ[:, tau, HG0:HG0 + HG], PJ[:, tau, HG0:HG0 + HG], ACT.Silu).then_inc(silu_ready, 1)
            act.activation(gates[:, :, :, :].rearrange("p t h b -> p t (h b)"), PJ[:, :, GR0:GR0 + 48],
                           ACT.Sigmoid).then_inc(gates_ready, 1)
            act.wait_ge(hg_ms, 1)
            act.activation(rst, rst, ACT.Sqrt).then_inc(hg_root, 1)

            for n in range(12):
                act.wait_ge(q_turned, n + 1)
                if n < 8:
                    i = 4 * (n % 4)
                    tau, a = i // 8, i % 8
                    act.activation((qUT, qRT)[n // 4][:, a:a + 4, tau * P:(tau + 1) * P],
                                   bank[1 + n % 2][:, :].rearrange("p (a t) -> p a t", a=4),
                                   ACT.Copy, scale=DK ** -0.5).then_inc(q_saved, 1)
                else:
                    br, tau = (n - 8) // 2, n % 2
                    act.wait_ge(zeros_ready, 4)
                    b = bank[5 + n % 2][:, :].rearrange("p (g t) -> p g t", g=4)
                    for z in range(2):
                        rows = slice(64 * z, 64 * z + 64)
                        act.activation(kRT[br][rows, z, :, tau * P:(tau + 1) * P], b[rows, :, :],
                                       ACT.Copy).then_inc(q_saved, 1)
            for n in range(2):
                act.wait_ge(piece_used, CMP_PIECE + 2 * (n + 1))
                if n:
                    act.wait_ge(hidT_done, n)
                act.activation(hid[0:60, :], bank[7][0:60, 0:256], ACT.Gelu_apprx_tanh).then_inc(hid_ready, 1)
            act.wait_ge(sc_in, 1)
            act.activation(sc, sc, ACT.Exp).then_inc(sc_exp, 1)
            for u, (br, g, tau) in enumerate(UNITS):
                act.wait_ge(s_max, u + 1)
                if u:
                    act.wait_ge(pT_done, u)
                if u >= 2:
                    act.wait_ge(o_used, u - 1)
                n = 128 * (tau + 1)
                for i in range(2):
                    for half in range(2):
                        h = 2 * i + half
                        act.activation(prob[:, h, 0:n], bank[2 * (u % 2) + i][:, half * n:(half + 1) * n], ACT.Exp,
                                       bias=nmx[:, 4 * (u % 2) + h:4 * (u % 2) + h + 1],
                                       accum_out=sums[:, 4 * (u % 2) + h:4 * (u % 2) + h + 1]).then_inc(p_ready, 1)
                if tau:
                    act.wait_ge(pT_done, u + 1)
                    act.wait_ge(o_done, u)
                    act.activation(probT[:, 4:8, :], bank[5][:, :].rearrange("p (h s) -> p h s", h=4),
                                   ACT.Copy).then_inc(pT_ready_b, 1)
            act.wait_ge(o_used, len(UNITS))
            squares(YN, 1, scr[:, 0:HG])
            rms_act(act, 1, stat[:, 0:2])
            act.wait_ge(out_saved, 2 * OUT_CH)
            squares(X2, 2, xt[:, 0:D])
            rms_act(act, 2, stat[:, 0:2])
            act.wait_ge(r_in, 1)
            act.activation(r8[:, 0:8], r8[:, 0:8], ACT.Exp).then_inc(r_exp, 1)
            act.wait_ge(r_in, 2)
            act.activation(r8[:, 8:10], r8[:, 8:10], ACT.Exp).then_inc(r_exp, 1)

            def hidden(done):
                act.wait_ge(piece_used, done * EP + (MOE_PIECE + 8))
                act.activation(hs[64:128, :], bank[3][0:64, :], ACT.Silu).then_inc(silu_done, 1)
                act.wait_ge(hT_done, done + 1)
                act.activation(hT.rearrange("p c s -> p (c s)"), bank[2][:, 256:512], ACT.Copy).then_inc(hT_saved, 1)

            def outputs(done, u):
                act.wait_ge(piece_used, done * EP + (MOE_PIECE + EP))
                for n in range(2):
                    act.activation(yb[64 * u:64 * u + 64, n * NCH:(n + 1) * NCH], bank[4][64 * n:64 * n + 64, :],
                                   ACT.Copy).then_inc(y_saved_a, 1)

            def pair_of_experts(pair, first):
                hidden(2 * pair)
                if not first:
                    act.wait_ge(scat_done, 8 * pair)
                act.wait_ge(dT_done, pair + 1)
                act.activation(dispT.rearrange("p t q -> p (t q)"), bank[2][:, 0:256], ACT.Copy).then_inc(dT_saved, 1)
                outputs(2 * pair, 0)
                hidden(2 * pair + 1)
                outputs(2 * pair + 1, 1)

            def one_round(r):
                if r:
                    act.wait_ge(scat_done, 4 * NE * r)
                pair_of_experts(r * NE // 2, True)
                with act.Fori(1, NE // 2) as i:
                    pair_of_experts(i + r * NE // 2, False)

            one_round(0)
            act.wait_ge(pos_ready, 2)
            most = act.value_load(cnt_i[0:1, 0:1], min_val=0, max_val=SEQ)
            with act.If(most > SLOTS):
                for r in range(1, ROUNDS):
                    one_round(r)
            act.wait_ge(experts_done, 1)
            squares(X2, 3, xt[:, 0:D])
            rms_act(act, 3, stat[:, 0:2])

        @block.vector
        def _(dve):
            def run(ins):
                link(dve, "dve", ins)

            rstd = stat[:, 0:2]
            rms_dve(dve, 0, stat[:, 0:2], D, rstd)
            for tau in range(T):
                dve.tensor_scalar(XN[:, tau, :], XN[:, tau, :], rstd[:, tau:tau + 1], None, ALU.mult).then_inc(nat_ready, 1)
            dve.wait_ge(cst_loaded, CST_LOADS)
            front = [bank[n] for n in range(4)]
            turn_dve(dve, 0, D, 0, 0, front)

            dve.wait_ge(lb_loaded, 16)
            run(dve.tensor_tensor(LB, lbl[:, 0, :], lbl[:, 1, :], ALU.max))
            dve.tensor_tensor(lbl[:, 0, :], lbl[:, 0, :], LB, ALU.subtract).then_inc(dve_chain, 1)
            chain_value["dve"] += 1
            dve.tensor_tensor(lbl[:, 1, :], lbl[:, 1, :], LB, ALU.subtract).then_inc(lb_in, 1)
            dve.wait_ge(lb_exp, 1)
            run(dve.tensor_tensor(OMLB, lbl[:, 0, :], lbl[:, 1, :], ALU.add))
            run(dve.reciprocal(OMLB, OMLB))
            run(dve.tensor_tensor(LB, lbl[:, 0, :], OMLB, ALU.mult))
            run(dve.tensor_tensor(OMLB, lbl[:, 1, :], OMLB, ALU.mult))
            for tau in range(T):
                f = PJ[:, tau, HF0:HF0 + HG]
                dve.wait_ge(sig_ready, tau + 1)
                run(dve.tensor_tensor(LF[:, tau, :], f, OMLB, ALU.mult))
                run(dve.tensor_tensor(LF[:, tau, :], LF[:, tau, :], LB, ALU.add))
                dve.tensor_scalar(f, LF[:, tau, :], -1.0, 1.0, ALU.mult, ALU.add).then_inc(f_ready, 1)
            for hg in range(2):
                for tau in range(T):
                    dve.wait_ge(qk_turned, 4 * hg + 2 + tau + 1)
                    dve.tensor_copy(kT[:, :, tau * P:(tau + 1) * P],
                                    bank[2 + tau][:, :].rearrange("p (h t) -> p h t", h=4)).then_inc(k_copied, 1)
                dve.wait_ge(k_copied, 2 * (hg + 1))
                dve.wait_ge(q_copied, 2 * (hg + 1))

                def decayed(n):
                    kind, tau, lv = STEPS[n]
                    if kind == "diag":
                        return
                    dve.wait_ge(decay_ready, decays_upto(hg, n))
                    if hg or n >= 2:
                        dve.wait_ge(gram_done, hg * len(STEPS) + max(n - 1, 0))
                    if kind == "cross":
                        v = [pair[i].rearrange("p (h t) -> p h t", h=4) for i in range(2)]
                        d = [decay[i].rearrange("p (h t) -> p h t", h=4) for i in range(2)]
                        dve.tensor_tensor(v[0], d[0], qT[:, :, P:2 * P], ALU.mult).then_inc(pair_ready, 1)
                        dve.tensor_tensor(v[1], d[1], kT[:, :, 0:P], ALU.mult).then_inc(pair_ready, 1)
                        return
                    w = LEVELS[lv]

                    def halves(a, side):
                        return a.rearrange("p (b two w) -> p b two w", two=2, w=w)[:, :, side, :]

                    for side, src in ((1, qT), (0, kT)):
                        if w == 64:
                            s_ = src[:, :, tau * P + 64 * side:tau * P + 64 * side + 64]
                            dve.tensor_tensor(halves(pair[n % 2], side), halves(decay[n % 2], side), s_,
                                              ALU.mult).then_inc(pair_ready, 1)
                        else:
                            s_ = src[:, :, tau * P:(tau + 1) * P].rearrange("p h (b two w) -> p h b two w", two=2, w=w)[:, :, :, side, :]
                            v, d = (a.rearrange("p (h b two w) -> p h b two w", h=4, two=2, w=w)[:, :, :, side, :]
                                    for a in (pair[n % 2], decay[n % 2]))
                            dve.tensor_tensor(v, d, s_, ALU.mult).then_inc(pair_ready, 1)

                def masked(n):
                    kind, tau, lv = STEPS[n]
                    g = hg * len(STEPS) + n
                    dve.wait_ge(gram_done, g + 1)
                    b = bank[6 + g % 2][:, :].rearrange("p (h t) -> p h t", h=4)
                    if kind == "cross":
                        dve.tensor_copy(att[2], bank[6 + g % 2][:, :]).then_inc(gram_used, 1)
                        return
                    m = B_GM + (lv if kind == "level" else NL) * 128
                    first = kind == "level" and lv == 0
                    if first and hg:
                        dve.wait_ge(hg_out, 2)
                    if not first:
                        adds = sum(1 for s in STEPS[:max(n - 1, 0)] if not (s[0] == "cross" or (s[0] == "level" and s[2] == 0)))
                        if hg * ADDS + adds:
                            dve.wait_ge(part_added, hg * ADDS + adds)
                    elif hg:
                        dve.wait_ge(part_added, hg * ADDS)
                    dst = (att[tau] if first else part[n % 2]).rearrange("p (h t) -> p h t", h=4)
                    dve.tensor_tensor(dst, b, cbf[:, m:m + 128].unsqueeze(1).to_broadcast([P, 4, P]),
                                      ALU.mult).then_inc(gram_used, 1)

                decayed(0)
                for n in range(len(STEPS)):
                    if n + 1 < len(STEPS):
                        decayed(n + 1)
                    masked(n)
                for tau in range(T):
                    dve.wait_ge(hg_out, 2 * hg + tau + 1)
                    dve.tensor_copy(PJ[:, tau, HQ0 + 512 * hg:HQ0 + 512 * hg + 512], bank[2 + tau][:, :]).then_inc(hg_copied, 1)
                    dve.wait_ge(hg_sq, 2 * hg + tau + 1)
                    dve.tensor_reduce(rst[:, tau * 8 + 4 * hg:tau * 8 + 4 * hg + 4],
                                      sqt.rearrange("p (h v) -> p h v", h=4), AX, ALU.add).then_inc(hg_saved, 1)
            dve.wait_ge(hg_saved, 4)
            dve.tensor_scalar(rst, rst, 1.0 / 128, EPS, ALU.mult, ALU.add).then_inc(hg_ms, 1)
            for tau in range(T):
                cos = cst[:, C_COS + tau * 32:C_COS + tau * 32 + 32].unsqueeze(1).to_broadcast([P, NH, 32])
                sin = cst[:, C_SIN + tau * 32:C_SIN + tau * 32 + 32].unsqueeze(1).to_broadcast([P, NH, 32])
                src = PJ[:, tau, NQ0:NQ0 + NH * DK].rearrange("p (h a d) -> p h a d", h=NH, a=2)
                dq = QR[:, tau, :].rearrange("p (h a d) -> p h a d", h=NH, a=2)
                qt = tmp.rearrange("p (h d) -> p h d", h=NH)
                for half, op in ((0, ALU.subtract), (1, ALU.add)):
                    run(dve.tensor_tensor(dq[:, :, half, :], src[:, :, half, :], cos, ALU.mult))
                    run(dve.tensor_tensor(qt, src[:, :, 1 - half, :], sin, ALU.mult))
                    last = dve.tensor_tensor(dq[:, :, half, :], dq[:, :, half, :], qt, op)
                    if tau == T - 1 and half == 1:
                        last.then_inc(rope_done, 1)
                    else:
                        run(last)
            dve.wait_ge(hg_root, 1)
            run(dve.reciprocal(rst, rst))
            dve.wait_ge(silu_ready, 2)
            for tau in range(T):
                o = PJ[:, tau, 0:HG].rearrange("p (h v) -> p h v", h=HH)
                run(dve.tensor_tensor(o, o, rst[:, tau * 8:tau * 8 + 8].unsqueeze(2).to_broadcast([P, HH, 128]), ALU.mult))
                dve.wait_ge(dve_chain, chain_value["dve"])
                dve.tensor_tensor(PJ[:, tau, 0:HG], PJ[:, tau, 0:HG], PJ[:, tau, HG0:HG0 + HG],
                                  ALU.mult).then_inc(hg_final, 1)

            turn_dve(dve, 8, HG, 0, 1, [bank[2], bank[7]])

            dve.wait_ge(kv_turned, 1)
            run(dve.tensor_copy(posT[:, :, :].rearrange("p n m -> p (n m)"), bank[0][:, 0:32]))
            run(dve.memset(hrep, 0.0))
            run(dve.memset(sc, 0.0))
            for n in range(2):
                dve.wait_ge(kv_turned, n + 2)
                b = bank[3 + n][:, :].rearrange("p (a t) -> p a t", a=2)
                v = kvT[n].rearrange("p (a two) t -> p a two t", two=2)
                for two in range(2):
                    rows = slice(64 * two, 64 * two + 64)
                    run(dve.tensor_copy(v[0:64, :, two, :], b[rows, :, :]))
                    run(dve.tensor_copy(v[64:128, :, two, 0:SEQ - 1], b[rows, :, 1:SEQ]))
            for n in range(2):
                if n:
                    dve.wait_ge(piece_used, CMP_PIECE + 2)
                for i in range(2):
                    src = kvT[n].rearrange("p g (b m two) -> p m g b two", m=8, two=2)[:, :, :, i:i + NCMP, 0]
                    pos = posT[:, n, 8 * i:8 * i + 8].unsqueeze(2).unsqueeze(3).to_broadcast([P, 8, NG, NCMP])
                    for g in range(NG):
                        ins = dve.tensor_tensor(flat[:, 8 * i:8 * i + 8, g, :], src[:, :, g, :], pos[:, :, g, :], ALU.add)
                        if i == 1 and g == NG - 1:
                            ins.then_inc(flat_ready, 1)
                        else:
                            run(ins)
                dve.wait_ge(hidT_done, n + 1)
                hb = bank[0][:, 0:128].rearrange("p (f x) -> p f x", f=2)
                if n == 0:
                    dve.tensor_copy(hidT[0][:, :, 0:60], hb[:, :, 0:60]).then_inc(hidT_ready, 1)
                    dve.wait_ge(cmp_done, 1)
                    run(dve.memset(kcz, 0.0))
                    run(dve.tensor_copy(kcz[0:64, 0, 0:60], bank[0][0:64, 256:316]))
                    dve.tensor_copy(kcz[64:128, 1, 0:60], bank[0][64:128, 256:316]).then_inc(cmp_ready, 1)
                else:
                    for o in range(2):
                        for f in range(2):
                            src = hb[:, f, 0:60].rearrange("p (g n) -> p g n", g=4)[:, 2 * o:2 * o + 2, :]
                            ins = dve.tensor_copy(hrep[:, o, f, :, :, 0:NCMP],
                                                  src.unsqueeze(2).to_broadcast([P, 2, 4, NCMP]))
                            if o and f:
                                ins.then_inc(hidT_ready, 1)
                            else:
                                run(ins)
                    dve.wait_ge(cmp_done, 2)
                    for o in range(2):
                        ins = dve.tensor_tensor(vbd[:, o, :, :],
                                                bank[7][:, o * 64:o * 64 + 64].unsqueeze(1).to_broadcast([P, 8, DK]),
                                                cst[:, C_BD:C_BD + 8].unsqueeze(2).to_broadcast([P, 8, DK]), ALU.mult)
                        if o:
                            ins.then_inc(cmp_ready, 1)
                        else:
                            run(ins)
            cm = cst[:, C_CM:C_CM + 32].rearrange("p (t n) -> p t n", t=T)
            cn = cst[:, C_CN:C_CN + 32].rearrange("p (t n) -> p t n", t=T)
            dve.wait_ge(sc_done, 1)
            for tau in range(T):
                b = bank[1][:, tau * 256:tau * 256 + 256].rearrange("p (h n) -> p h n", h=NH)[:, :, 0:NCMP]
                run(dve.tensor_tensor(sc[:, tau, :, 0:NCMP], b,
                                      cm[:, tau, 0:NCMP].unsqueeze(1).to_broadcast([P, NH, NCMP]), ALU.mult))
                run(dve.tensor_tensor(sc[:, tau, :, 0:NCMP], sc[:, tau, :, 0:NCMP],
                                      cn[:, tau, 0:NCMP].unsqueeze(1).to_broadcast([P, NH, NCMP]), ALU.add))
            mx = tmp[:, 0:32].rearrange("p (t h) -> p t h", t=T)
            sm = tmp[:, 32:64].rearrange("p (t h) -> p t h", t=T)
            run(dve.tensor_reduce(mx, sc[:, :, :, 0:NCMP], AX, ALU.max))
            for tau in range(T):
                ins = dve.tensor_tensor(sc[:, tau, :, 0:NCMP], sc[:, tau, :, 0:NCMP],
                                        mx[:, tau, :].unsqueeze(2).to_broadcast([P, NH, NCMP]), ALU.subtract)
                if tau:
                    ins.then_inc(sc_in, 1)
                else:
                    run(ins)
            dve.wait_ge(sc_exp, 1)
            for tau in range(T):
                run(dve.tensor_tensor(sc[:, tau, :, :], sc[:, tau, :, :], cm[:, tau, :].unsqueeze(1).to_broadcast([P, NH, 16]), ALU.mult))
            run(dve.tensor_reduce(sm, sc, AX, ALU.add))
            for tau in range(T):
                run(dve.tensor_scalar(sm[:, tau, :], sm[:, tau, :], cst[:, C_NV + tau:C_NV + tau + 1], None, ALU.add))
            run(dve.reciprocal(sm, sm))
            for tau in range(T):
                ins = dve.tensor_tensor(sc[:, tau, :, :], sc[:, tau, :, :], sm[:, tau, :].unsqueeze(2).to_broadcast([P, NH, 16]), ALU.mult)
                if tau:
                    ins.then_inc(pc_ready, 1)
                else:
                    run(ins)
            dve.wait_ge(pcT_done, 1)
            dve.tensor_copy(pcT.rearrange("p t o q -> p (t o q)"), bank[3][:, :]).then_inc(pcT_ready, 1)
            dve.wait_ge(gates_ready, 1)
            dve.wait_ge(q_turned, 8)
            for tau in range(T):
                for o in range(2):
                    dve.wait_ge(oc_done, 2 * tau + o + 1)
                    dve.tensor_tensor(YN[:, tau, 512 * o:512 * o + 512].rearrange("p (h d) -> p h d", h=8),
                                      bank[4 + o][:, :].rearrange("p (h d) -> p h d", h=8),
                                      gates[:, tau, 8 * o:8 * o + 8, 0].unsqueeze(2).to_broadcast([P, 8, DK]),
                                      ALU.mult).then_inc(oc_used, 1)
            dve.wait_ge(oc_used, 4)

            def maxima(u):
                br, g, tau = UNITS[u]
                n = 128 * (tau + 1)
                dve.wait_ge(s_done, u + 1)
                if u >= 2:
                    dve.wait_ge(p_ready, 4 * (u - 1))
                m = nmx[:, 4 * (u % 2):4 * (u % 2) + 4].rearrange("p (i half) -> p i half", half=2)
                for i in range(2):
                    run(dve.tensor_reduce(m[:, i, :], bank[2 * (u % 2) + i][:, 0:2 * n].rearrange("p (z s) -> p z s", z=2),
                                          AX, ALU.max))
                dve.tensor_scalar(nmx[:, 4 * (u % 2):4 * (u % 2) + 4], nmx[:, 4 * (u % 2):4 * (u % 2) + 4], -1.0, None,
                                  ALU.mult).then_inc(s_max, 1)

            maxima(0)
            for u, (br, g, tau) in enumerate(UNITS):
                if u + 1 < len(UNITS):
                    maxima(u + 1)
                dve.wait_ge(pT_done, u + 1)
                if u:
                    dve.wait_ge(o_done, u)
                dve.tensor_copy(probT[:, 0:4, :], bank[4][:, :].rearrange("p (h s) -> p h s", h=4)).then_inc(pT_ready, 1)
                dve.wait_ge(p_ready, 4 * (u + 1))
                su = sums[:, 4 * (u % 2):4 * (u % 2) + 4]
                sg = sums[:, 8 + 4 * (u % 2):12 + 4 * (u % 2)]
                run(dve.reciprocal(sg, su))
                run(dve.tensor_tensor(sg, sg, gates[:, tau, 4 * g:4 * g + 4, 1 + br], ALU.mult))
                dve.wait_ge(o_done, u + 1)
                t4 = tmp[:, 0:256].rearrange("p (h d) -> p h d", h=4)
                run(dve.tensor_tensor(t4, bank[7][:, 0:256].rearrange("p (h d) -> p h d", h=4),
                                      sg.unsqueeze(2).to_broadcast([P, 4, DK]), ALU.mult))
                y = YN[:, tau, 256 * g:256 * g + 256]
                dve.tensor_tensor(y, y, tmp[:, 0:256], ALU.add).then_inc(o_used, 1)
                dve.wait_ge(o_used, u + 1)
                for j, at in enumerate(OUT0_AFTER):
                    if at == u:
                        dve.wait_ge(res_loaded, 32)
                        ch, tt = OUT0[j]
                        if tt:
                            dve.wait_ge(piece_used, OUT_PIECE + 2 * (ch + 1))
                        else:
                            dve.wait_ge(out0_done, ch + 1)
                        r = XR[:, tt, ch * NCH:(ch + 1) * NCH]
                        dve.tensor_tensor(r, r, bank[6][:, :], ALU.add).then_inc(out0_saved, 1)
            rms_dve(dve, 1, stat[:, 0:2], NH * DK, rstd)
            for tau in range(T):
                dve.tensor_scalar(YN[:, tau, :], YN[:, tau, :], rstd[:, tau:tau + 1], None, ALU.mult).then_inc(nat_ready, 1)
            turn_dve(dve, 12, NH * DK, 8, 1, front)

            dve.wait_ge(turned, 16)
            for ch in range(OUT_CH):
                dve.wait_ge(piece_used, OUT_PIECE + 8 + 2 * (ch + 1))
                for tau in range(T):
                    c = slice(ch * NCH, (ch + 1) * NCH)
                    dve.tensor_tensor(X2[:, tau, c], XR[:, tau, c], bank[2 * (ch % 2) + tau][:, :],
                                      ALU.add).then_inc(out_saved, 1)
            dve.wait_ge(out_saved, 2 * OUT_CH)
            rms_dve(dve, 2, stat[:, 0:2], D, rstd)
            for tau in range(T):
                dve.tensor_scalar(XS[:, tau, :], X2[:, tau, :], rstd[:, tau:tau + 1], None, ALU.mult).then_inc(nat_ready, 1)
            run(dve.memset(ones, 1.0))
            turn_dve(dve, 16, D, 0, 2, front)

            dve.wait_ge(route_loaded, 64)
            dve.wait_ge(logit_done, 1)
            run(dve.tensor_tensor(LG, bank[4][:, 0:72].rearrange("p (t n) -> p t n", t=T),
                                  rbias.unsqueeze(1).to_broadcast([P, T, 36]), ALU.add))
            w = r8
            lg, le = LG[:, :, 0:4], LG[:, :, 4:36]
            m1 = w[:, 10:12]
            col = [w[:, 10 + 2 * n:12 + 2 * n] for n in range(14)]
            m1, gw, mxi, v1, v2, ex, p1, p2 = col[:8]

            def wide(a, n):
                return a.unsqueeze(2).to_broadcast([P, T, n])

            ohg = w[:, 40:48].rearrange("p (t n) -> p t n", t=T)
            ohb = w[:, 48:56].rearrange("p (t n) -> p t n", t=T)
            eg = w[:, 0:8].rearrange("p (t n) -> p t n", t=T)
            oh1, oh2 = (scr[:, 512 + 64 * n:576 + 64 * n].rearrange("p (t n) -> p t n", t=T) for n in range(2))

            def first_max(dst, src, m, n, rev):
                run(dve.tensor_reduce(m, src, AX, ALU.max))
                run(dve.tensor_tensor(dst, src, wide(m, n), ALU.is_ge))
                run(dve.tensor_tensor(dst, dst, rev.unsqueeze(1).to_broadcast([P, T, n]), ALU.mult))
                run(dve.tensor_reduce(mxi, dst, AX, ALU.max))
                run(dve.tensor_tensor(dst, dst, wide(mxi, n), ALU.is_equal))

            first_max(ohg, lg, m1, 4, cst[:, C_REV:C_REV + 4])
            dve.tensor_tensor(eg, lg, wide(m1, 4), ALU.subtract).then_inc(r_in, 1)
            dve.wait_ge(r_exp, 1)
            run(dve.tensor_reduce(gw, eg, AX, ALU.add))
            run(dve.reciprocal(gw, gw))
            run(dve.tensor_scalar(ohb, ohg, NEG, -NEG, ALU.mult, ALU.add))
            for tau in range(T):
                e4 = LG[:, tau, 4:36].rearrange("p (g e) -> p g e", g=4)
                run(dve.tensor_tensor(e4, e4, ohg[:, tau, :].unsqueeze(2).to_broadcast([P, 4, 8]), ALU.mult))
                run(dve.tensor_tensor(e4, e4, ohb[:, tau, :].unsqueeze(2).to_broadcast([P, 4, 8]), ALU.add))
            first_max(oh1, le, v1, 32, cst[:, C_REV + 4:C_REV + 36])
            run(dve.scalar_tensor_tensor(le, oh1, -3.0 * NEG, le, ALU.mult, ALU.add))
            first_max(oh2, le, v2, 32, cst[:, C_REV + 4:C_REV + 36])
            ed = w[:, 8:10]
            dve.tensor_tensor(ed, v2, v1, ALU.subtract).then_inc(r_in, 1)
            dve.wait_ge(r_exp, 2)
            run(dve.tensor_scalar(p1, ed, 1.0, None, ALU.add))
            run(dve.reciprocal(p1, p1))
            run(dve.tensor_tensor(p1, p1, gw, ALU.mult))
            run(dve.tensor_tensor(p2, p1, ed, ALU.mult))
            run(dve.memset(wt, 0.0))
            run(dve.memset(posm, 0.0))
            wt_, posm_ = wt[:, :, 0:NE], posm[:, :, 0:NE]
            run(dve.tensor_tensor(wt_, oh1, wide(p1, 32), ALU.mult))
            run(dve.tensor_tensor(posm_, oh2, wide(p2, 32), ALU.mult))
            run(dve.tensor_tensor(wt_, wt_, posm_, ALU.add))
            dve.tensor_tensor(sel, oh1, oh2, ALU.add).then_inc(sel_ready, 1)
            dve.wait_ge(sel_ready, 1)
            dve.wait_ge(pos_done, 1)
            run(dve.scalar_tensor_tensor(posm_, bank[5][:, 0:64].rearrange("p (t n) -> p t n", t=T), 1.0, sel, ALU.add, ALU.mult))
            run(dve.tensor_reduce(mxi[:, 0:1], bank[5][:, 64:96], AX, ALU.max))
            run(dve.tensor_copy(cnt_i[:, 0:1], mxi[:, 0:1]))
            dve.tensor_scalar(posm, posm, -1.0, None, ALU.add).then_inc(pos_ready, 2)
            dve.wait_ge(pos_ready, 2)
            dve.memset(mxi, 0.0).then_inc(scat_used, 2)
            dve.memset(v1, 0.0).then_inc(y_saved_d, 2)

            def dispatch(e, nth, u):
                if not (isinstance(nth, int) and nth == 0):
                    dve.wait_ge(dispw_ready, nth)
                dve.tensor_tensor(disp, cst[:, C_IOTA:C_IOTA + SLOTS].unsqueeze(1).to_broadcast([P, T, SLOTS]),
                                  posm[:, :, bass.ds(e, 1)].to_broadcast([P, T, SLOTS]),
                                  ALU.is_equal).then_inc(disp_ready, 1)
                dve.wait_ge(disp_ready, nth + 1)
                dve.tensor_tensor(dispw[:, :, u, :], disp, wt[:, :, bass.ds(e, 1)].to_broadcast([P, T, SLOTS]),
                                  ALU.mult).then_inc(dispw_ready, 1)

            def save_gather(nth):
                for half in range(2):
                    dve.wait_ge(gath_done, 2 * nth + (half + 1))
                    dve.tensor_tensor(xg[:, 8 * half:8 * half + 8, :], bank[half][:, :].rearrange("p (c s) -> p c s", c=8),
                                      gain[:, 2 * KC + 8 * half:2 * KC + 8 * half + 8].unsqueeze(2).to_broadcast([P, 8, SLOTS]),
                                      ALU.mult).then_inc(gath_saved, 1)

            def hidden(done):
                dve.wait_ge(silu_done, done + 1)
                dve.tensor_tensor(hv[64:128, :], bank[3][64:128, :], hs[64:128, :], ALU.mult).then_inc(h_ready, 1)

            def outputs(done, u):
                dve.wait_ge(piece_used, done * EP + (MOE_PIECE + EP))
                for n in range(2):
                    dve.tensor_copy(yb[64 * u:64 * u + 64, (2 + n) * NCH:(3 + n) * NCH],
                                    bank[5][64 * n:64 * n + 64, :]).then_inc(y_saved_d, 1)

            def add_scatter(pair):
                dve.wait_ge(scat_used, 8 * pair + 2)
                for k in range(8):
                    dve.wait_ge(scat_done, 8 * pair + (k + 1))
                    r = X2[:, k // 4, (k % 4) * NCH:(k % 4 + 1) * NCH]
                    dve.tensor_tensor(r, r, bank[6 + k % 2][:, :], ALU.add).then_inc(scat_used, 1)

            def pair_of_experts(e, pair, r, first):
                done, nth = 2 * pair, 2 * pair + r
                dve.wait_ge(gath_done, 2 * nth + 2)
                dispatch(e + 1, nth + 1, 1)
                hidden(done)
                save_gather(nth + 1)
                if not first:
                    add_scatter(pair - 1)
                outputs(done, 0)
                dve.wait_ge(dT_done, pair + 1)
                dispatch(e + 2, nth + 2, 0)
                hidden(done + 1)
                save_gather(nth + 2)
                outputs(done + 1, 1)

            def one_round(r):
                dispatch(0, r * (NE + 1), 0)
                save_gather(r * (NE + 1))
                pair_of_experts(0, r * NE // 2, r, True)
                with dve.Fori(1, NE // 2) as i:
                    pair_of_experts(2 * i, i + r * NE // 2, r, False)
                add_scatter((r + 1) * NE // 2 - 1)

            one_round(0)
            most = dve.value_load(cnt_i[0:1, 0:1], min_val=0, max_val=SEQ)
            with dve.If(most > SLOTS):
                for r in range(1, ROUNDS):
                    dve.tensor_scalar(posm, posm, -1.0 * SLOTS, None, ALU.add).then_inc(pos_ready, 1)
                    dve.wait_ge(pos_ready, 2 + r)
                    one_round(r)
            dve.wait_ge(scat_used, 4 * NE + 2)
            dve.memset(cnt_i[:, 1:2], 0).then_inc(experts_done, 1)
            rms_dve(dve, 3, stat[:, 0:2], D, rstd)
            dve.wait_ge(fin_loaded, 16)
            for tau in range(T):
                dve.scalar_tensor_tensor(XS[:, tau, :], X2[:, tau, :], rstd[:, tau:tau + 1], fgain, ALU.mult,
                                         ALU.mult).then_inc(final_ready, 1)


_INS = ["x", "attn_norm", "w_in", "hg_lb_logits", "hg_out_norm", "cmp_pos_k", "cmp_w1_k", "cmp_w2_k", "cmp_pos_v",
        "cmp_w1_v", "cmp_w2_v", "nsa_out_norm", "w_out", "ffn_norm", "moe_w_group", "moe_b_group", "moe_w_router",
        "moe_b_router", "moe_w_gate", "moe_w_up", "moe_w_down", "final_norm"]


def kernel(**inputs):
    import ml_dtypes as _ml
    import concourse.bacc as _bacc
    from concourse.bass_utils import run_bass_kernel_spmd as _run

    nc = _bacc.Bacc("TRN2", target_bir_lowering=False, num_devices=1)
    arrays, args = {}, []
    c, b = tables()
    for name, a in [(n, inputs[n]) for n in _INS] + [("consts", c), ("consts_bf", b.astype(_ml.bfloat16))]:
        a = np.ascontiguousarray(a)
        arrays[f"in_{name}"] = a
        args.append(nc.dram_tensor(f"in_{name}", a.shape, mybir.dt.from_np(a.dtype), kind="ExternalInput").ap())
    args.append(nc.dram_tensor("out_0", (1, SEQ, D), F32, kind="ExternalOutput").ap())
    hybrid_block(nc, *args)
    r = _run(nc, [arrays], core_ids=[0])
    return r.results[0]["out_0"]
```

```python
from contextlib import ExitStack

import concourse.bass as bass
from concourse import mybir
import numpy as np

F32 = mybir.dt.float32
F32R = mybir.dt.float32r
BF16 = mybir.dt.bfloat16
I32 = mybir.dt.int32
ALU = mybir.AluOpType
ACT = mybir.ActivationFunctionType
AX = mybir.AxisListType.X

P = 128
SEQ = 256
D = 2048
T = SEQ // P
KC = D // P
HG = 1024
HH = 8
NH, NG, DK = 16, 4, 64
NCMP = 15
IN_COLS = 4 * HG + NH * DK + 6 * NG * DK + 3 * NH
HQ0, HF0, HI0, HG0, NQ0 = 0, HG, 2 * HG, 3 * HG, 4 * HG
KC0 = NQ0 + NH * DK
VC0, KS0, VS0, KW0, VW0, GR0 = (KC0 + n * NG * DK for n in range(1, 7))
NCH = 512
IN_CH = GR0 // NCH
GATE_CH = IN_CH
ORDER = [2, 3, 0, 1, 4, 5, 10, 11, 12, 8, 9, 6, 7, GATE_CH]
CMP_AT = 11
EARLY = 6
OUT_CH = D // NCH
PIECE = 2048
FRONT_SLOTS = 4
PP = D * NCH // (P * PIECE)
NE = 32
SLOTS = 64
ROUNDS = SEQ // SLOTS
EP = 12
LEVELS = [64, 32, 16, 8, 4, 2, 1]
NL = len(LEVELS)
EPS = 1e-6
NEG = 1e30

C_ID = 0
C_LT = C_ID + 128
C_M = C_LT + 128
C_COS = C_M + (NL + 2) * 128
C_SIN = C_COS + T * 32
C_CM = C_SIN + T * 32
C_CN = C_CM + T * 16
C_NV = C_CN + T * 16
C_BD = C_NV + T
C_IOTA = C_BD + 8
C_REV = C_IOTA + SLOTS
C_N = C_REV + 36
B_ID = 0
B_CAUSAL = 128
B_GM = B_CAUSAL + 512
B_N = B_GM + (NL + 1) * 128


def tables():
    c = np.zeros((P, C_N), np.float32)
    b = np.zeros((P, B_N), np.float32)
    s, t = np.arange(P)[:, None], np.arange(P)[None, :]
    c[:, C_ID:C_ID + 128] = s == t
    c[:, C_LT:C_LT + 128] = s < t
    for n, h in enumerate(LEVELS):
        start = t // (2 * h) * (2 * h)
        right = t % (2 * h) >= h
        c[:, C_M + n * 128:C_M + n * 128 + 128] = np.where(
            right, (s >= start + h) & (s <= t), (s > t) & (s < start + h))
        b[:, B_GM + n * 128:B_GM + n * 128 + 128] = (s // (2 * h) == t // (2 * h)) & (s % (2 * h) < h) & right
    c[:, C_M + NL * 128:C_M + NL * 128 + 128] = s <= t
    c[:, C_M + (NL + 1) * 128:C_M + (NL + 2) * 128] = s > t
    b[:, B_GM + NL * 128:] = s == t
    b[:, B_ID:B_ID + 128] = s == t
    b[:, B_CAUSAL:B_CAUSAL + 512] = np.concatenate([np.zeros((P, 128)), np.where(t <= s, 0, -NEG)] * 2, 1)
    inv = (1.0 / (np.float32(10000.0) ** (np.arange(0, DK, 2, dtype=np.float32) / np.float32(DK)))).astype(np.float32)
    ang = np.arange(SEQ, dtype=np.float32)[:, None] * inv[None, :]
    for tau in range(T):
        rows = np.arange(P) + tau * P
        c[:, C_COS + tau * 32:C_COS + tau * 32 + 32] = np.cos(ang[rows])
        c[:, C_SIN + tau * 32:C_SIN + tau * 32 + 32] = np.sin(ang[rows])
        m = (np.arange(16)[None, :] * 16 + 31 <= rows[:, None]) & (np.arange(16)[None, :] < NCMP)
        c[:, C_CM + tau * 16:C_CM + tau * 16 + 16] = m
        c[:, C_CN + tau * 16:C_CN + tau * 16 + 16] = (m - 1.0) * NEG
        c[:, C_NV + tau] = ~m.any(1)
    c[:, C_BD:C_BD + 8] = s // 16 == np.arange(8)[None, :]
    c[:, C_IOTA:C_IOTA + SLOTS] = np.arange(SLOTS)
    c[:, C_REV:C_REV + 4] = 4 - np.arange(4)
    c[:, C_REV + 4:C_REV + 36] = 32 - np.arange(32)
    return c, b


def hybrid_block(nc, x, attn_norm, w_in, hg_lb_logits, hg_out_norm, cmp_pos_k, cmp_w1_k, cmp_w2_k,
                 cmp_pos_v, cmp_w1_v, cmp_w2_v, nsa_out_norm, w_out, ffn_norm, moe_w_group, moe_b_group,
                 moe_w_router, moe_b_router, moe_w_gate, moe_w_up, moe_w_down, final_norm, consts, consts_bf, out):
    with ExitStack() as ctx:
        def sb(name, cols, dt=F32):
            return ctx.enter_context(nc.sbuf_tensor(name, [P, cols], dt))

        def sem(name):
            return ctx.enter_context(nc.semaphore(name))

        ctx.enter_context(nc.allow_non_contiguous_dma(reason="small transposed gains and position tables"))

        ring_at = -(-nc.sbuf_base // 32) * 32
        ring = sb("ring", EP * PIECE)
        proj_at = nc.sbuf_base
        proj = sb("proj", T * IN_COLS)
        xt = sb("xt", KC * SEQ)
        scr_at = nc.sbuf_base
        scr = sb("scr", 8192)
        cst = sb("cst", C_N)
        cbf = sb("cbf", B_N, BF16)
        stat = sb("stat", 128)
        gain = sb("gain", 3 * KC)
        rgain = sb("rgain", KC)
        cnt_i = sb("cnt_i", 2, I32)
        bank = [ctx.enter_context(nc.psum_tensor(f"bank{n}", [P, 512], F32)) for n in range(8)]

        PJ = proj[:, :].rearrange("p (t c) -> p t c", t=T)
        XT = xt[:, :].rearrange("p (c t) -> p c t", c=KC)
        ident = cst[:, C_ID:C_ID + 128]

        def slot(n, inner):
            n = n % FRONT_SLOTS
            return ring[:, n * PIECE:(n + 1) * PIECE].rearrange("p (a b) -> p a b", b=inner)

        def slot_flat(n):
            n = n % FRONT_SLOTS
            return ring[:, n * PIECE:(n + 1) * PIECE]

        work = ring[:, FRONT_SLOTS * PIECE:EP * PIECE]
        XN = scr[:, 0:T * D].rearrange("p (t c) -> p t c", t=T)
        WGATE = work[:, 14336:14336 + KC * 48].rearrange("p (c n) -> p c n", c=KC)

        def over(name, at, cols):
            return nc.alloc_sbuf_tensor_at(name, [P, cols], F32R, offset=at)[:, :]

        work_at = ring_at + 4 * FRONT_SLOTS * PIECE
        XH, XL = (over(name, work_at + 4 * (6144 + KC * SEQ * n), KC * SEQ).rearrange("p (c t) -> p c t", c=KC)
                  for n, name in enumerate(("x_hi", "x_lo")))
        WH = [over(f"w_hi{n}", at, PIECE) for n, at in
              enumerate((proj_at + 4 * NQ0, proj_at + 4 * (IN_COLS + NQ0), work_at))]
        YH, YL = (over(name, work_at + 4 * (9216 + 8 * SEQ * n), 8 * SEQ).rearrange("p (c t) -> p c t", c=8)
                  for n, name in enumerate(("y_hi", "y_lo")))
        OH = [over(f"o_hi{n}", at, PIECE) for n, at in
              enumerate((work_at + 4 * 13312, scr_at + 4 * 5120, work_at + 4 * 4096, work_at + 4 * 6144))]
        WL = [over(f"w_lo{n}", ring_at + 4 * PIECE * n, PIECE) for n in range(FRONT_SLOTS)]

        ident_loaded = sem("ident_loaded")
        cst_loaded = sem("cst_loaded")
        x_loaded = sem("x_loaded")
        slot_loaded = [sem(f"slot_loaded{n}") for n in range(EP)]
        piece_used = sem("piece_used")
        small_loaded = sem("small_loaded")
        lb_loaded = sem("lb_loaded")
        w2_loaded = sem("w2_loaded")
        route_loaded = sem("route_loaded")
        fin_loaded = sem("fin_loaded")
        rgain_loaded = sem("rgain_loaded")
        stored = sem("stored")
        sq_ready = sem("sq_ready")
        ms_ready = sem("ms_ready")
        root_ready = sem("root_ready")
        nat_ready = sem("nat_ready")
        turned = sem("turned")
        turned_used = sem("turned_used")
        xh_ready = sem("xh_ready")
        xl_ready = sem("xl_ready")
        wh_ready = sem("wh_ready")
        wl_ready = sem("wl_ready")
        gate_cols_done = sem("gate_cols_done")
        proj_saved = sem("proj_saved")
        dve_chain = sem("dve_chain")
        act_chain = sem("act_chain")
        pool_chain = sem("pool_chain")

        chain_value = {"dve": 0, "act": 0, "pool": 0}
        chain_sem = {"dve": dve_chain, "act": act_chain, "pool": pool_chain}

        def link(eng, name, ins):
            chain_value[name] += 1
            ins.then_inc(chain_sem[name], 1)
            eng.wait_ge(chain_sem[name], chain_value[name])

        lb_exp = sem("lb_exp")
        lb_in = sem("lb_in")
        sig_ready = sem("sig_ready")
        f_ready = sem("f_ready")
        lf_ready = sem("lf_ready")
        qk_turned = sem("qk_turned")
        q_copied = sem("q_copied")
        k_copied = sem("k_copied")
        expo_done = sem("expo_done")
        decay_ready = sem("decay_ready")
        pair_ready = sem("pair_ready")
        gram_done = sem("gram_done")
        gram_used = sem("gram_used")
        part_added = sem("part_added")
        hg_out = sem("hg_out")
        hg_saved = sem("hg_saved")
        hg_sq = sem("hg_sq")
        hg_copied = sem("hg_copied")
        hg_ms = sem("hg_ms")
        hg_root = sem("hg_root")
        silu_ready = sem("silu_ready")
        hg_final = sem("hg_final")
        zeros_ready = sem("zeros_ready")

        def rms_dve(dve, n, ss, width, rstd):
            dve.wait_ge(sq_ready, n + 1)
            dve.tensor_scalar(rstd, ss, 1.0 / width, EPS, ALU.mult, ALU.add).then_inc(ms_ready, 1)
            dve.wait_ge(root_ready, n + 1)
            link(dve, "dve", dve.reciprocal(rstd, rstd))

        def rms_act(act, n, rstd):
            act.wait_ge(ms_ready, n + 1)
            act.activation(rstd, rstd, ACT.Sqrt).then_inc(root_ready, 1)

        def turn_pe(pe, first, src, banks):
            n = src.shape[2] // P
            for k in range(T * n // 4):
                tau, cg = k // (n // 4), k % (n // 4)
                if k >= len(banks):
                    pe.wait_ge(turned_used, first + k - len(banks) + 1)
                for j in range(4):
                    c = 4 * cg + j
                    last = pe.transpose(banks[k % len(banks)][:, j * 128:(j + 1) * 128],
                                        src[:, tau, c:c + 127 * n + 1:n], ident)
                last.then_inc(turned, 1)

        def turn_dve(dve, first, width, chunk0, g, banks):
            n = width // P
            for k in range(T * n // 4):
                tau, c = k // (n // 4), chunk0 + 4 * (k % (n // 4))
                dve.wait_ge(turned, first + k + 1)
                dve.tensor_tensor(XT[:, c:c + 4, tau * P:(tau + 1) * P],
                                  banks[k % len(banks)][:, :].rearrange("p (c t) -> p c t", c=4),
                                  gain[:, g * KC + c:g * KC + c + 4].unsqueeze(2).to_broadcast([P, 4, P]),
                                  ALU.mult).then_inc(turned_used, 1)

        def x_block(n):
            tau, c = n // 4, 4 * (n % 4)
            return slice(c, c + 4), slice(tau * P, (tau + 1) * P)

        def y_block(n):
            tau, c = n // 2, 4 * (n % 2)
            return slice(c, c + 4), slice(tau * P, (tau + 1) * P)

        def split_piece(n):
            if n < EARLY * PP:
                return n, WH[n % 3], n - 2 if n >= 3 else 0
            k = n - EARLY * PP
            if k < 8:
                return OUT_PIECE + k, OH[k % 2], OUT_PIECE + k - 1 if k >= 2 else 0
            return OUT_PIECE + k, OH[k % 4], OUT_PIECE + (8 if k < 12 else k - 3)

        def split_act(act, n):
            piece, hi, free_at = split_piece(n)
            piece_ready(act, piece)
            if free_at:
                act.wait_ge(piece_used, free_at)
            act.activation(hi, slot_flat(piece), ACT.Copy).then_inc(wh_ready, 1)

        def split_dve(dve, n):
            piece, hi, _ = split_piece(n)
            dve.wait_ge(wh_ready, n + 1)
            dve.tensor_tensor(WL[piece % FRONT_SLOTS], slot_flat(piece), hi.bitcast(F32), ALU.subtract).then_inc(wl_ready, 1)

        def split_y_act(act, half):
            for n in range(4):
                act.wait_ge(turned_used, 8 + 4 * half + n + 1)
                c, t = y_block(n)
                act.activation(YH[:, c, t], XT[:, 8 * half + c.start:8 * half + c.stop, t], ACT.Copy).then_inc(xh_ready, 1)

        def split_y_pool(pool, half):
            for n in range(4):
                pool.wait_ge(xh_ready, 8 + 4 * half + n + 1)
                c, t = y_block(n)
                pool.tensor_tensor(YL[:, c, t], XT[:, 8 * half + c.start:8 * half + c.stop, t],
                                   YH[:, c, t].bitcast(F32), ALU.subtract).then_inc(xl_ready, 1)

        def proj_bank(q, tau):
            return bank[2 * (q % 2) + tau] if q < EARLY else bank[tau]

        qT = work[:, 0:1024].rearrange("p (h t) -> p h t", h=4)
        kT = work[:, 1024:2048].rearrange("p (h t) -> p h t", h=4)
        att = [work[:, 2048 + 512 * n:2560 + 512 * n] for n in range(3)]
        lbl = work[:, 4096:6144].rearrange("p (a c) -> p a c", a=2)
        LF = scr[:, 0:2048].rearrange("p (t c) -> p t c", t=T)
        decay = [scr[:, 2048 + 512 * n:2560 + 512 * n] for n in range(2)]
        pair = [scr[:, 3072 + 512 * n:3584 + 512 * n] for n in range(2)]
        part = [scr[:, 4096 + 512 * n:4608 + 512 * n] for n in range(2)]
        sqt = scr[:, 7680:8192]
        LB = scr[:, 5120:6144]
        OMLB = scr[:, 6144:7168]
        rst = stat[:, 16:32]
        STEPS = [("level", tau, n) for tau in range(T) for n in range(NL)] + [("diag", 0, 0), ("diag", 1, 0), ("cross", 0, 0)]
        ADDS = T * NL
        ktmp = sb("ktmp", 128)
        sums = sb("sums", 16)
        nmx = sb("nmx", 8)


        def decays_upto(hg, n):
            return hg * (T * NL + 2) + sum({"level": 1, "diag": 0, "cross": 2}[s[0]] for s in STEPS[:n + 1])

        def pairs_upto(hg, n):
            return hg * (2 * T * NL + 2) + sum({"level": 2, "diag": 0, "cross": 2}[s[0]] for s in STEPS[:n + 1])

        qUT = work[:, 4096:6144].rearrange("p (a t) -> p a t", a=8)
        qRT = work[:, 6144:8192].rearrange("p (a t) -> p a t", a=8)
        kRT = [PJ[:, :, c:c + HG].rearrange("p z (g t) -> p z g t", g=4) for c in (NQ0, HF0)]
        kcz = work[:, 15104:15232].rearrange("p (z x) -> p z x", z=2)
        kvT = [work[:, 12288 + 1024 * n:13312 + 1024 * n].rearrange("p (g t) -> p g t", g=4) for n in range(2)]
        prob = [a.rearrange("p (h s) -> p h s", h=4) for a in (scr[:, 2048:3072], work[:, 8192:9216])]
        probT = [scr[:, 3072 + 1024 * n:4096 + 1024 * n].rearrange("p (h s) -> p h s", s=128) for n in range(2)]
        flat = [work[:, c:c + 960].rearrange("p (m g n) -> p m g n", m=16, g=4) for c in (15104, 12288)]
        hid = [scr[:, 5120 + 256 * n:5376 + 256 * n] for n in range(2)]
        hidT = work[:, 16064:16192].rearrange("p (f m) -> p f m", f=2)
        hrep = scr[:, 5632:6144].rearrange("p (o f g r n) -> p o f g r n", o=2, f=2, g=2, r=4)
        vbd = scr[:, 6144:7168].rearrange("p (o h d) -> p o h d", o=2, h=8)
        sc = scr[:, 7168:7680].rearrange("p (t h n) -> p t h n", t=T, h=NH)
        pcT = scr[:, 5120:5632].rearrange("p (t o q) -> p t o q", t=T, o=2)
        tmp = scr[:, 7680:8192]
        QR = work[:, 8192:10240].rearrange("p (t c) -> p t c", t=T)
        KR = work[:, 10240:12288].rearrange("p (t b g u d) -> p t b g u d", t=T, b=2, g=4, u=2)
        YN = PJ[:, :, HI0:HI0 + HG]
        w2k = work[:, 3584:3840].rearrange("p (f u d) -> p f u d", f=2, u=2)
        w2v = work[:, 16192:16320].rearrange("p (f d) -> p f d", f=2)
        posn = work[0:16, 3840:4096].rearrange("p (n x) -> p n x", n=2)
        posT = work[:, 16320:16352].rearrange("p (n m) -> p n m", n=2)

        side_done = sem("side_done")
        side_saved = sem("side_saved")
        q_roped = sem("q_roped")
        k_roped = sem("k_roped")
        cmp_zeroed = sem("cmp_zeroed")
        flat_ready = sem("flat_ready")
        hid_ready = sem("hid_ready")
        cmp_ready = sem("cmp_ready")
        sc_done = sem("sc_done")
        sc_in = sem("sc_in")
        sc_exp = sem("sc_exp")
        pc_ready = sem("pc_ready")
        pcT_done = sem("pcT_done")
        pcT_ready = sem("pcT_ready")
        oc_done = sem("oc_done")
        oc_used = sem("oc_used")
        gates_ready = sem("gates_ready")
        s_done = sem("s_done")
        s_max = sem("s_max")
        p_ready = sem("p_ready")
        pT_done = sem("pT_done")
        pT_ready = sem("pT_ready")
        o_done = sem("o_done")
        o_used = sem("o_used")
        XR = work[:, 0:T * D].rearrange("p (t c) -> p t c", t=T)
        pT_ready_b = sem("pT_ready_b")
        UNITS = [(br, g, tau) for br in range(2) for g in range(NG) for tau in range(T)]
        y_stat = stat[:, 6:8]
        gates = stat[:, 32:128].rearrange("p (t h b) -> p t h b", t=T, h=NH)

        X2 = proj[:, 0:T * D].rearrange("p (t c) -> p t c", t=T)
        XS = proj[:, T * D:2 * T * D].rearrange("p (t c) -> p t c", t=T)
        RT = scr[:, 4096:8192].rearrange("p (c t) -> p c t", c=KC)
        mo = 2 * T * D
        WR = proj[:, mo:mo + KC * 36].rearrange("p (c n) -> p c n", c=KC)
        rbias = proj[:, mo + 576:mo + 612]
        fgain = proj[:, mo + 640:mo + 640 + D]
        LG = scr[:, 0:72].rearrange("p (t n) -> p t n", t=T)
        sel = scr[:, 72:136].rearrange("p (t n) -> p t n", t=T)
        wt = scr[:, 640:640 + T * NE].rearrange("p (t n) -> p t n", t=T)
        posm = scr[:, 720:720 + T * NE].rearrange("p (t n) -> p t n", t=T)
        ones = scr[:, 264:392]
        r8 = scr[:, 392:512]
        disp = scr[:, 1024:1152].rearrange("p (t s) -> p t s", t=T)
        dispw = scr[:, 1152:1408].rearrange("p (t u s) -> p t u s", t=T, u=2)
        dispT = scr[:, 1408:1664].rearrange("p (t q) -> p t q", t=T)
        xg = scr[:, 2048:3072].rearrange("p (c s) -> p c s", c=KC)
        hs = scr[:, 3072:3584]
        hv = scr[:, 3584:4096]
        hT = scr[:, 4096:4352].rearrange("p (c s) -> p c s", c=4)
        yb = scr[:, 4608:4608 + D]

        x2_turned = sem("x2_turned")
        x2_saved = sem("x2_saved")
        rstd_ready = sem("rstd_ready")
        x_rstd = sem("x_rstd")
        out_saved = sem("out_saved")
        out0_done = sem("out0_done")
        out0_saved = sem("out0_saved")
        res_loaded = sem("res_loaded")
        logit_done = sem("logit_done")
        r_in = sem("r_in")
        r_exp = sem("r_exp")
        sel_ready = sem("sel_ready")
        pos_done = sem("pos_done")
        pos_ready = sem("pos_ready")
        disp_ready = sem("disp_ready")
        dispw_ready = sem("dispw_ready")
        gath_done = sem("gath_done")
        gath_saved = sem("gath_saved")
        dT_done = sem("dT_done")
        dT_saved = sem("dT_saved")
        silu_done = sem("silu_done")
        h_ready = sem("h_ready")
        hT_done = sem("hT_done")
        hT_saved = sem("hT_saved")
        y_saved_a = sem("y_saved_a")
        y_saved_d = sem("y_saved_d")
        scat_done = sem("scat_done")
        scat_used = sem("scat_used")
        final_ready = sem("final_ready")
        experts_done = sem("experts_done")

        x_v = x.rearrange("b (t p) d -> (b p) t d", p=P)
        out_v = out.rearrange("b (t p) d -> (b p) t d", p=P)
        win_v = w_in[0].rearrange("(p c) n -> p c n", p=P)
        wout_v = w_out[0].rearrange("(h p c) n -> h p c n", h=2, p=P)
        gate_v = moe_w_gate[0].rearrange("e (p c) n -> e p (c n)", p=P)
        up_v = moe_w_up[0].rearrange("e (p c) n -> e p (c n)", p=P)
        down_v = moe_w_down[0].rearrange("e (p c) n -> e p (c n)", p=P)

        CST_LOADS = 16 * 12
        CMP_PIECE = CMP_AT * PP
        OUT_PIECE = IN_CH * PP + 4

        def first_piece(q):
            return q * PP + (4 if q >= CMP_AT else 0)
        MOE_PIECE = OUT_PIECE + OUT_CH * PP
        assert MOE_PIECE % FRONT_SLOTS == 0

        def piece_ready(eng, n):
            eng.wait_ge(slot_loaded[n % FRONT_SLOTS], 16 * (n // FRONT_SLOTS + 1))

        def expert_piece(eng, k, done):
            before = MOE_PIECE // FRONT_SLOTS if k < FRONT_SLOTS else 0
            eng.wait_ge(slot_loaded[k], 16 * done + 16 * (before + 1))

        LATE = [("proj", q, i) for q in range(EARLY, CMP_AT) for i in range(PP)]
        LATE += [("cmp", n, i) for n in range(2) for i in range(2)]
        LATE += [("proj", CMP_AT, i) for i in range(PP)]
        TAIL = [("proj", q, i) for q in range(CMP_AT + 1, IN_CH) for i in range(PP)] + [("proj", IN_CH, 0)]
        PLACES = 2 * (len(STEPS) + 1)

        def late_pieces(place):
            dense = PLACES * 3 // 4
            n = len(LATE) - PP
            if place < dense:
                return LATE[place * n // dense:(place + 1) * n // dense]
            return LATE[n + (place - dense) // 2:][:1] if (place - dense) % 2 == 0 else []

        SIDE = [(5, "pos", 0), (6, "kv", 0), (7, "kv", 1),
                (19, "qu", (0, 0)), (20, "qu", (1, 0)), (21, "kr", (1, 0)), (22, "kr", (1, 1)),
                (23, "qu", (0, 1)), (24, "qu", (1, 1)), (25, "hid", 0), (26, "qr", (0, 0)), (27, "w2", 0),
                (27, "qr", (0, 1)), (28, "hid", 1), (29, "qr", (1, 0)), (30, "qr", (1, 1)),
                (31, "kr", (0, 0)), (32, "kr", (0, 1)), (33, "w2", 1)]
        SIDE_FIRST = sum(1 for p, _, _ in SIDE if p < len(STEPS) + 1)

        def side_of(kind, which):
            return next(j for j, (_, k_, w_) in enumerate(SIDE) if (k_, w_) == (kind, which))

        OUT0 = [(ch, tau) for ch in range(OUT_CH) for tau in range(T)]
        OUT0_AFTER = [1, 3, 5, 7, 9, 11, 13, 16]

        block = ctx.enter_context(nc.Block())

        @block.sync
        def _(sp):
            for tau in range(T):
                sp.dma_start(XN[:, tau, :], x_v[:, tau, :]).then_inc(x_loaded, 16)

            def load(n, src, inner):
                if n >= FRONT_SLOTS:
                    sp.wait_ge(piece_used, n - FRONT_SLOTS + 1)
                sp.dma_start(slot(n, inner), src).then_inc(slot_loaded[n % FRONT_SLOTS], 16)

            for q, ch in enumerate(ORDER[:IN_CH]):
                if q == 1:
                    sp.dma_start(cst[:, 128:C_N], consts[:, 128:C_N]).then_inc(cst_loaded, 16)
                    sp.dma_start(cbf[:, :], consts_bf).then_inc(cst_loaded, 16)
                    for h in range(8):
                        sp.dma_start(gain[16 * h:16 * h + 16, KC:KC + 8], hg_out_norm[0].rearrange("(p c) -> p c", c=8)
                                      ).then_inc(cst_loaded, 16)
                    sp.dma_start(gain[:, KC + 8:2 * KC], nsa_out_norm[0].rearrange("(p c) -> p c", p=P)).then_inc(cst_loaded, 16)
                    sp.dma_start(gain[:, 2 * KC:3 * KC], ffn_norm[0].rearrange("(p c) -> p c", p=P)).then_inc(cst_loaded, 16)
                if q == CMP_AT:
                    for n, w in enumerate((cmp_w1_k, cmp_w1_v)):
                        v = w[0].rearrange("(m p) n -> p m n", p=P)
                        for i in range(2):
                            load(CMP_PIECE + 2 * n + i, v[:, 8 * i:8 * i + 8, :], 256)
                for i in range(PP):
                    load(first_piece(q) + i, win_v[:, 4 * i:4 * i + 4, ch * NCH:(ch + 1) * NCH], NCH)
            for half in range(2):
                for ch in range(OUT_CH):
                    for i in range(2):
                        load(OUT_PIECE + half * 8 + ch * 2 + i,
                             wout_v[half, :, 4 * i:4 * i + 4, ch * NCH:(ch + 1) * NCH], NCH)

            def expert_loads(e, done):
                for k in range(EP):
                    if isinstance(done, int) and done == 0:
                        if k < FRONT_SLOTS:
                            sp.wait_ge(piece_used, MOE_PIECE - FRONT_SLOTS + k + 1)
                        elif k == FRONT_SLOTS:
                            sp.wait_ge(out_saved, 2 * OUT_CH)
                    else:
                        sp.wait_ge(piece_used, done * EP + (MOE_PIECE - EP + k + 1))
                    w, j = ((gate_v, up_v)[k % 2], k // 2) if k < 8 else (down_v, k - 8)
                    sp.dma_start(ring[:, k * PIECE:(k + 1) * PIECE],
                                 w[bass.ds(e, 1), :, j * PIECE:(j + 1) * PIECE].rearrange("e p n -> (e p) n")
                                 ).then_inc(slot_loaded[k], 16)

            expert_loads(0, 0)
            with sp.Fori(1, NE) as e:
                expert_loads(e, e)
            sp.wait_ge(pos_ready, 2)
            most = sp.value_load(cnt_i[0:1, 0:1], min_val=0, max_val=SEQ)
            with sp.If(most > SLOTS):
                for r in range(1, ROUNDS):
                    with sp.Fori(0, NE) as e:
                        expert_loads(e, e + r * NE)
            for tau in range(T):
                sp.wait_ge(final_ready, tau + 1)
                sp.dma_start(out_v[:, tau, :], XS[:, tau, :]).then_inc(stored, 16)
            sp.wait_ge(stored, 16 * T)

        @block.gpsimd
        def _(pool):
            for n in range(4):
                pool.wait_ge(xh_ready, n + 1)
                c, t = x_block(n)
                pool.tensor_tensor(XL[:, c, t], XT[:, c, t], XH[:, c, t].bitcast(F32), ALU.subtract).then_inc(xl_ready, 1)

            pool.wait_ge(slot_loaded[1], 16)
            pool.dma_start(WGATE, win_v[:, :, GR0:IN_COLS]).then_inc(small_loaded, 16)
            pool.dma_start(rgain[:, :], ffn_norm[0].rearrange("(c p) -> p c", p=P)).then_inc(rgain_loaded, 16)

            pool.dma_start(lbl, hg_lb_logits.rearrange("(o a) c -> o a c", o=1).to_broadcast([P, 2, HG])
                           ).then_inc(lb_loaded, 16)
            pool.dma_start(w2v[:, :, :], cmp_w2_v[0].rearrange("(f p) d -> p f d", p=P)).then_inc(w2_loaded, 16)
            for u in range(2):
                pool.dma_start(w2k[:, :, u, :], cmp_w2_k[0].rearrange("(f p) d -> p f d", p=P)).then_inc(w2_loaded, 16)
            for n, w in enumerate((cmp_pos_k, cmp_pos_v)):
                pool.dma_start(posn[:, n, :], w[0].rearrange("(m a) d -> m (a d)", a=2)).then_inc(w2_loaded, 16)

            def rotate_keys(br, tau):
                pool.wait_ge(proj_saved, ORDER.index((KS0, KW0)[br] // NCH) + 1)
                cos = cst[:, C_COS + tau * 32:C_COS + tau * 32 + 32].unsqueeze(1).to_broadcast([P, NG, 32])
                sin = cst[:, C_SIN + tau * 32:C_SIN + tau * 32 + 32].unsqueeze(1).to_broadcast([P, NG, 32])
                kt = ktmp[:, :].rearrange("p (g d) -> p g d", g=NG)
                src = PJ[:, tau, (KS0, KW0)[br]:(KS0, KW0)[br] + 256].rearrange("p (g a d) -> p g a d", g=NG, a=2)
                for half, op in ((0, ALU.subtract), (1, ALU.add)):
                    dst = KR[:, tau, br, :, 0, 32 * half:32 * half + 32]
                    link(pool, "pool", pool.tensor_tensor(dst, src[:, :, half, :], cos, ALU.mult))
                    link(pool, "pool", pool.tensor_tensor(kt, src[:, :, 1 - half, :], sin, ALU.mult))
                    link(pool, "pool", pool.tensor_tensor(dst, dst, kt, op))
                pool.tensor_copy(KR[:, tau, br, :, 1, :], KR[:, tau, br, :, 0, :]).then_inc(k_roped, 1)

            def clear_keys(br):
                if br:
                    pool.wait_ge(qk_turned, 8)
                else:
                    pool.wait_ge(side_done, side_of("qu", (1, 1)) + 1)
                    pool.wait_ge(q_roped, 1)
                pool.wait_ge(k_roped, 4)
                if k:
                    pool.wait_ge(part_added, k)
                c = (NQ0, HF0)[br]
                pool.memset(PJ[64:128, 0, c:c + HG], 0.0).then_inc(zeros_ready, 1)
                pool.memset(PJ[0:64, 1, c:c + HG], 0.0).then_inc(zeros_ready, 1)
                pool.wait_ge(zeros_ready, 2 if br else 4)

            pool.wait_ge(cst_loaded, CST_LOADS)
            k = 0
            for hg in range(2):
                for n, (kind, tau, lv) in enumerate(STEPS):
                    if not (kind == "cross" or (kind == "level" and lv == 0)):
                        pool.wait_ge(gram_used, hg * len(STEPS) + n + 1)
                        if k:
                            pool.wait_ge(part_added, k)
                        pool.tensor_tensor(att[tau], att[tau], part[n % 2], ALU.add).then_inc(part_added, 1)
                        k += 1
                    place = hg * (len(STEPS) + 1) + 1 + n
                    for at, br, tt in ((10, 0, 0), (11, 0, 1), (15, 1, 0), (16, 1, 1)):
                        if at == place:
                            rotate_keys(br, tt)
                    if place in (19, 27):
                        clear_keys(1 if place == 19 else 0)

            pool.wait_ge(hg_saved, 4)
            for tau in range(T):
                pool.dma_start(XR[:, tau, :], x_v[:, tau, :]).then_inc(res_loaded, 16)

            split_y_pool(pool, 0)
            split_y_pool(pool, 1)

            pool.wait_ge(turned, 16)
            pool.dma_start(WR[:, :, 0:4], moe_w_group[0].rearrange("(c p) n -> p c n", p=P)).then_inc(route_loaded, 16)
            pool.dma_start(WR[:, :, 4:36], moe_w_router[0].rearrange("(c p) n -> p c n", p=P)).then_inc(route_loaded, 16)
            pool.dma_start(rbias[:, 0:4], moe_b_group.to_broadcast([P, 4])).then_inc(route_loaded, 16)
            pool.dma_start(rbias[:, 4:36], moe_b_router.to_broadcast([P, NE])).then_inc(route_loaded, 16)
            pool.dma_start(fgain, final_norm.rearrange("(o d) -> o d", o=1).to_broadcast([P, D])).then_inc(fin_loaded, 16)

        @block.tensor
        def _(pe):
            pe.wait_ge(ident_loaded, 32)
            front = [bank[n] for n in range(4)]
            pe.wait_ge(x_loaded, 32)
            turn_pe(pe, 0, XN, front)
            pe.wait_ge(xl_ready, 8)

            def split_product(acc, xh, xl, w_hi, w_lo, start, stop):
                pe.matmul(acc, xh, w_hi, start=start, stop=False)
                pe.matmul(acc, xl, w_hi, start=False, stop=False)
                return pe.matmul(acc, xh, w_lo, start=False, stop=stop)

            def project_split(q, i):
                n = q * PP + i
                if i == 0 and q >= 2:
                    pe.wait_ge(proj_saved, q - 1)
                pe.wait_ge(wl_ready, n + 1)
                hi, lo = split_piece(n)[1], WL[n % FRONT_SLOTS]
                for tau in range(T):
                    t = slice(tau * P, (tau + 1) * P)
                    for cc in range(4):
                        c, w = 4 * i + cc, slice(cc * NCH, (cc + 1) * NCH)
                        last = split_product(proj_bank(q, tau)[:, :], XH[:, c, t], XL[:, c, t], hi[:, w], lo[:, w],
                                             c == 0, c == KC - 1)
                last.then_inc(piece_used, 1)

            def project(q, i):
                ch = ORDER[q]
                if i == 0:
                    if q == EARLY:
                        pe.wait_ge(proj_saved, q - 1)
                    elif q >= 2:
                        pe.wait_ge(proj_saved, q if q > EARLY else q - 1)
                    if q == CMP_AT:
                        pe.wait_ge(hid_ready, 2)
                width, steps = (48, range(KC)) if ch == GATE_CH else (NCH, range(4 * i, 4 * i + 4))
                if ch == GATE_CH:
                    pe.wait_ge(small_loaded, 16)
                else:
                    piece_ready(pe, first_piece(q) + i)
                for tau in range(T):
                    for c in steps:
                        rhs = WGATE[:, c, :] if ch == GATE_CH else slot(first_piece(q) + i, NCH)[:, c % 4, :]
                        last = pe.matmul(proj_bank(q, tau)[:, 0:width], XT[:, c, tau * P:(tau + 1) * P], rhs,
                                         start=c == 0, stop=c == KC - 1)
                last.then_inc(gate_cols_done if ch == GATE_CH else piece_used, 1)

            def compress(n, i):
                if i == 0:
                    pe.wait_ge(proj_saved, CMP_AT)
                    pe.wait_ge(flat_ready, n + 1)
                piece_ready(pe, CMP_PIECE + 2 * n + i)
                for mm in range(8):
                    m = 8 * i + mm
                    last = pe.matmul(bank[n][0:60, 0:256], flat[n][:, m, :, :].rearrange("p g n -> p (g n)"),
                                     slot(CMP_PIECE + 2 * n + i, 256)[:, mm, :], start=m == 0, stop=m == 15)
                last.then_inc(piece_used, 1)

            def between(place):
                for what, q, i in late_pieces(place):
                    (project if what == "proj" else compress)(q, i)
                for j, (at, kind, which) in enumerate(SIDE):
                    if at == place:
                        side_job(j, kind, which)

            def side_job(j, kind, which):
                b = bank[2 + j % 2]
                if j >= 2:
                    pe.wait_ge(side_saved, j - 1)
                if kind == "pos":
                    pe.wait_ge(w2_loaded, 80)
                    for n in range(2):
                        last = pe.transpose(b[:, n * 16:(n + 1) * 16], posn[:, n, :], ident[0:16, 0:16])
                elif kind == "kv":
                    pe.wait_ge(proj_saved, ORDER.index(KC0 // NCH) + 1)
                    for k in range(4):
                        col = (KC0, VC0)[which] + k // 2 * 128
                        last = pe.transpose(b[:, k * 128:(k + 1) * 128], PJ[:, k % 2, col:col + 128], ident)
                elif kind in ("qu", "qr"):
                    tau, half = which
                    if kind == "qu":
                        pe.wait_ge(proj_saved, ORDER.index(NQ0 // NCH + half) + 1)
                    else:
                        pe.wait_ge(q_roped, 1)
                    for k in range(4):
                        c = (4 * half + k) * 128
                        src = PJ[:, tau, NQ0 + c:NQ0 + c + 128] if kind == "qu" else QR[:, tau, c:c + 128]
                        last = pe.transpose(b[:, k * 128:(k + 1) * 128], src, ident)
                elif kind == "kr":
                    br, tau = which
                    pe.wait_ge(k_roped, 2 * br + tau + 1)
                    for g in range(NG):
                        last = pe.transpose(b[:, g * 128:(g + 1) * 128],
                                            KR[:, tau, br, g, :, :].rearrange("p u d -> p (u d)"), ident)
                elif kind == "hid":
                    pe.wait_ge(hid_ready, which + 1)
                    for f in range(2):
                        last = pe.transpose(b[:, 64 * f:64 * f + 60], hid[which][0:60, f * 128:(f + 1) * 128],
                                            ident[0:60, 0:60])
                elif which == 0:
                    pe.wait_ge(side_saved, side_of("hid", 0) + 1)
                    for f in range(2):
                        last = pe.matmul(b[:, 0:60], w2k[:, f, :, :].rearrange("p u d -> p (u d)"),
                                         hidT[:, f, 0:60], start=f == 0, stop=f == 1)
                else:
                    pe.wait_ge(side_saved, side_of("hid", 1) + 1)
                    for o in range(2):
                        for f in range(2):
                            last = pe.matmul(b[:, o * 64:o * 64 + 64],
                                             hrep[:, o, f, :, :, :].rearrange("p g r n -> p (g r n)"),
                                             w2v[:, f, :], start=f == 0, stop=f == 1)
                last.then_inc(side_done, 1)

            for q in range(EARLY):
                for i in range(PP):
                    project_split(q, i)

            pe.wait_ge(cst_loaded, CST_LOADS)
            pe.wait_ge(lf_ready, 2)
            pe.wait_ge(proj_saved, EARLY)
            place = 0
            for hg in range(2):
                for n in range(4):
                    what, tau = n // 2, n % 2
                    if n >= 2:
                        pe.wait_ge(q_copied, 2 * hg + n - 1)
                    elif hg:
                        pe.wait_ge(hg_copied, n + 1)
                    for j in range(4):
                        h = 4 * hg + j
                        col = (HQ0, HF0)[what] + h * 128
                        last = pe.transpose(bank[2 + n % 2][:, j * 128:(j + 1) * 128], PJ[:, tau, col:col + 128], ident)
                    last.then_inc(qk_turned, 1)
                between(place)
                place += 1
                pe.wait_ge(q_copied, 2 * (hg + 1))
                pe.wait_ge(k_copied, 2 * (hg + 1))

                def exponents(n):
                    kind, tau, lv = STEPS[n]
                    g = hg * len(STEPS) + n
                    if kind == "diag":
                        return
                    b = bank[4 + n % 2]
                    if kind == "level":
                        if n >= 2:
                            pe.wait_ge(decay_ready, decays_upto(hg, n - 2))
                        for j in range(4):
                            h = 4 * hg + j
                            last = pe.matmul(b[:, j * 128:(j + 1) * 128], LF[:, tau, h * 128:(h + 1) * 128],
                                             cst[:, C_M + lv * 128:C_M + lv * 128 + 128], start=True, stop=True)
                        last.then_inc(expo_done, 1)
                    else:
                        pe.wait_ge(decay_ready, decays_upto(hg, n - 1))
                        for u in range(2):
                            for j in range(4):
                                h = 4 * hg + j
                                m = C_M + (NL + u) * 128
                                last = pe.matmul(bank[4 + u][:, j * 128:(j + 1) * 128],
                                                 LF[:, 1 - u, h * 128:(h + 1) * 128],
                                                 cst[:, m:m + 128], start=True, stop=True)
                            last.then_inc(expo_done, 1)

                def products(n):
                    kind, tau, lv = STEPS[n]
                    g = hg * len(STEPS) + n
                    if g >= 2:
                        pe.wait_ge(gram_used, g - 1)
                    if kind != "diag":
                        pe.wait_ge(pair_ready, pairs_upto(hg, n))
                    b = bank[6 + g % 2]
                    for j in range(4):
                        sl = slice(j * 128, (j + 1) * 128)
                        if kind == "level":
                            l = r = pair[n % 2][:, sl]
                        elif kind == "diag":
                            l, r = kT[:, j, tau * P:(tau + 1) * P], qT[:, j, tau * P:(tau + 1) * P]
                        else:
                            l, r = pair[1][:, sl], pair[0][:, sl]
                        last = pe.matmul(b[:, sl], l, r, start=True, stop=True)
                    last.then_inc(gram_done, 1)

                exponents(0)
                for n in range(len(STEPS)):
                    if n + 1 < len(STEPS):
                        exponents(n + 1)
                    products(n)
                    between(place)
                    place += 1
                pe.wait_ge(gram_used, len(STEPS) * (hg + 1))
                pe.wait_ge(part_added, ADDS * (hg + 1))
                pe.wait_ge(side_saved, SIDE_FIRST if hg == 0 else len(SIDE) - 1)
                if hg:
                    pe.wait_ge(cmp_ready, 1)
                for tau in range(T):
                    for j in range(4):
                        h = 4 * hg + j
                        sl = slice(j * 128, (j + 1) * 128)
                        v = [PJ[:, t, HI0 + h * 128:HI0 + h * 128 + 128] for t in range(T)]
                        if tau == 0:
                            last = pe.matmul(bank[2][:, sl], att[0][:, sl], v[0], start=True, stop=True)
                        else:
                            pe.matmul(bank[3][:, sl], att[2][:, sl], v[0], start=True, stop=False)
                            last = pe.matmul(bank[3][:, sl], att[1][:, sl], v[1], start=False, stop=True)
                    last.then_inc(hg_out, 1)

            for tau in range(T):
                for a in range(NH // 2):
                    o = bank[4][:, tau * 256 + a * 32:tau * 256 + a * 32 + 32].rearrange("p (z n) -> p z n", z=2)
                    g = a // 2
                    last = pe.matmul(o[:, :, 0:NCMP], qUT[:, a, tau * P:(tau + 1) * P],
                                     kcz[:, :, g * NCMP:(g + 1) * NCMP], start=True, stop=True)
            last.then_inc(sc_done, 1)
            for what, q, i in TAIL[:2]:
                project(q, i)
            pe.wait_ge(pc_ready, 1)
            for tau in range(T):
                for o in range(2):
                    last = pe.transpose(bank[5][:, (2 * tau + o) * 128:(2 * tau + o + 1) * 128],
                                        sc[:, tau, 8 * o:8 * o + 8, :].rearrange("p h n -> p (h n)"), ident)
            last.then_inc(pcT_done, 1)
            for what, q, i in TAIL[2:]:
                project(q, i)
            pe.wait_ge(pcT_ready, 1)
            for tau in range(T):
                for o in range(2):
                    if 2 * tau + o >= 2:
                        pe.wait_ge(oc_used, 2 * tau + o - 1)
                    last = pe.matmul(bank[4 + o][:, :], pcT[:, tau, o, :], vbd[:, o, :, :].rearrange("p h d -> p (h d)"),
                                     start=True, stop=True)
                    last.then_inc(oc_done, 1)

            def out_piece(k, tau, b, i):
                n = EARLY * PP + k
                pe.wait_ge(wl_ready, n + 1)
                piece, hi, _ = split_piece(n)
                lo, t = WL[piece % FRONT_SLOTS], slice(tau * P, (tau + 1) * P)
                for cc in range(4):
                    c, w = 4 * i + cc, slice(cc * NCH, (cc + 1) * NCH)
                    last = split_product(b[:, :], YH[:, c, t], YL[:, c, t], hi[:, w], lo[:, w], c == 0, c == 7)
                return last

            def out_first(j):
                ch, tau = OUT0[j]
                if j:
                    pe.wait_ge(out0_saved, j)
                pe.wait_ge(xl_ready, 12)
                for i in range(2):
                    last = out_piece(2 * ch + i, tau, bank[6], i)
                    if tau:
                        last.then_inc(piece_used, 1)
                if not tau:
                    last.then_inc(out0_done, 1)

            def scores(u):
                br, g, tau = UNITS[u]
                if u >= 2:
                    pe.wait_ge(p_ready, 4 * (u - 1))
                n = 128 * (tau + 1)
                for i in range(2):
                    b = bank[2 * (u % 2) + i][:, 0:2 * n].rearrange("p (z s) -> p z s", z=2)
                    mask = cbf[:, B_CAUSAL:B_CAUSAL + 512].rearrange("p (z s) -> p z s", z=2)[:, :, 256 - n:256]
                    pe.matmul(b, cbf[:, B_ID:B_ID + 128], mask, start=True, stop=False, skip_group_check=True)
                    last = pe.matmul(b, qRT[:, 2 * g + i, tau * P:(tau + 1) * P], kRT[br][:, :, g, 0:n],
                                     start=False, stop=True, skip_group_check=True)
                last.then_inc(s_done, 1)

            def turn_probs(u):
                br, g, tau = UNITS[u]
                pe.wait_ge(p_ready, 4 * (u + 1))
                if u:
                    pe.wait_ge(pT_ready, u)
                if u // 2:
                    pe.wait_ge(pT_ready_b, u // 2)
                for sb_ in range(tau + 1):
                    for h in range(4):
                        last = pe.transpose(bank[4 + sb_][:, h * 128:(h + 1) * 128],
                                            prob[u % 2][:, h, sb_ * 128:(sb_ + 1) * 128], ident)
                last.then_inc(pT_done, 1)

            def values(u):
                br, g, tau = UNITS[u]
                pe.wait_ge(pT_ready, u + 1)
                if tau:
                    pe.wait_ge(pT_ready_b, u // 2 + 1)
                if u:
                    pe.wait_ge(o_used, u)
                v0 = (VS0, VW0)[br] + g * DK
                for h in range(4):
                    for sb_ in range(tau + 1):
                        last = pe.matmul(bank[7][:, h * DK:(h + 1) * DK], probT[u % 2][:, 4 * sb_ + h, :],
                                         PJ[:, sb_, v0:v0 + DK], start=sb_ == 0, stop=sb_ == tau)
                last.then_inc(o_done, 1)

            pe.wait_ge(proj_saved, IN_CH + 1)
            scores(0)
            scores(1)
            pe.wait_ge(hg_final, 2)
            turn_pe(pe, 8, PJ[:, :, 0:HG], [bank[6], bank[7]])
            pe.wait_ge(turned_used, 12)
            pe.wait_ge(oc_used, 4)
            for u in range(len(UNITS) + 1):
                if u < len(UNITS):
                    turn_probs(u)
                if u + 2 < len(UNITS):
                    scores(u + 2)
                if u:
                    values(u - 1)
                for j, at in enumerate(OUT0_AFTER):
                    if at == u:
                        out_first(j)

            pe.wait_ge(o_used, len(UNITS))
            turn_pe(pe, 12, YN, front)
            pe.wait_ge(xl_ready, 16)

            def turn_x2(ch):
                for tau in range(T):
                    pe.wait_ge(out_saved, 2 * ch + tau + 1)
                    if ch:
                        pe.wait_ge(x2_saved, 2 * (ch - 1) + tau + 1)
                    for j in range(4):
                        last = pe.transpose(bank[4 + tau][:, j * 128:(j + 1) * 128],
                                            X2[:, tau, ch * NCH + j * 128:ch * NCH + (j + 1) * 128], ident)
                    last.then_inc(x2_turned, 1)

            def route(ch):
                for tau in range(T):
                    pe.wait_ge(x2_saved, 2 * ch + tau + 1)
                    for c in range(4 * ch, 4 * ch + 4):
                        last = pe.matmul(bank[6 + tau][:, 0:36], RT[:, c, tau * P:(tau + 1) * P], WR[:, c, :],
                                         start=c == 0, stop=c == KC - 1)
                return last

            for ch in range(OUT_CH):
                if ch >= 2:
                    pe.wait_ge(out_saved, 2 * (ch - 1))
                for i in range(2):
                    for tau in range(T):
                        last = out_piece(8 + 2 * ch + i, tau, bank[2 * (ch % 2) + tau], i)
                    last.then_inc(piece_used, 1)
                if ch:
                    turn_x2(ch - 1)
            pe.wait_ge(route_loaded, 64)
            for ch in range(OUT_CH - 1):
                route(ch)
            turn_x2(OUT_CH - 1)
            route(OUT_CH - 1).then_inc(logit_done, 1)
            pe.wait_ge(sel_ready, 1)
            lt = cst[:, C_LT:C_LT + 128]
            pe.matmul(bank[5][:, 0:32], lt, sel[:, 0, :], start=True, stop=True)
            pe.matmul(bank[5][:, 32:64], ones, sel[:, 0, :], start=True, stop=False)
            pe.matmul(bank[5][:, 32:64], lt, sel[:, 1, :], start=False, stop=True)
            pe.matmul(bank[5][:, 64:96], ones, sel[:, 0, :], start=True, stop=False)
            pe.matmul(bank[5][:, 64:96], ones, sel[:, 1, :], start=False, stop=True).then_inc(pos_done, 1)

            def gather(nth):
                if isinstance(nth, int) and nth == 0:
                    pe.wait_ge(nat_ready, 2)
                pe.wait_ge(disp_ready, nth + 1)
                for half in range(2):
                    for cc in range(8):
                        c = 8 * half + cc
                        for tau in range(T):
                            last = pe.matmul(bank[half][:, cc * SLOTS:(cc + 1) * SLOTS], XS[:, tau, c:c + 127 * KC + 1:KC],
                                             disp[:, tau, :], start=tau == 0, stop=tau == T - 1)
                    last.then_inc(gath_done, 1)

            def gate_up(done):
                for j in range(4):
                    expert_piece(pe, 2 * j, done)
                    expert_piece(pe, 2 * j + 1, done)
                    if j % 2 == 0:
                        pe.wait_ge(gath_saved, 2 * done + (j // 2 + 1))
                    for cc in range(4):
                        c = 4 * j + cc
                        for u in range(2):
                            last = pe.matmul(bank[3][64 * u:64 * u + 64, :], xg[:, c, :],
                                             ring[:, (2 * j + u) * PIECE + cc * NCH:(2 * j + u) * PIECE + (cc + 1) * NCH],
                                             start=c == 0, stop=c == KC - 1)
                            if cc == 3:
                                last.then_inc(piece_used, 1)

            def turn_hidden(done):
                pe.wait_ge(h_ready, done + 1)
                for c in range(4):
                    last = pe.matmul(bank[2][:, 256 + c * 64:256 + c * 64 + 64], hv[64:128, c:c + 127 * 4 + 1:4],
                                     ident[64:128, 64:128], start=True, stop=True)
                last.then_inc(hT_done, 1)

            def scatter(pair, k):
                if k == 0:
                    pe.wait_ge(dT_saved, pair + 1)
                    pe.wait_ge(y_saved_a, 4 * pair + 4)
                    pe.wait_ge(y_saved_d, 4 * pair + 6)
                pe.wait_ge(scat_used, 8 * pair + (k + 1))
                pe.matmul(bank[6 + k % 2][:, :], dispT[:, k // 4, :], yb[:, (k % 4) * NCH:(k % 4 + 1) * NCH],
                          start=True, stop=True).then_inc(scat_done, 1)

            def down(done, pair=None):
                pe.wait_ge(hT_saved, done + 1)
                for c in range(4):
                    expert_piece(pe, 8 + c, done)
                    if c == 0:
                        pe.wait_ge(y_saved_d, 2 * done + 2)
                        if not (isinstance(done, int) and done == 0):
                            pe.wait_ge(y_saved_a, 2 * done)
                    for n in range(4):
                        last = pe.matmul(bank[4 + n // 2][64 * (n % 2):64 * (n % 2) + 64, :], hT[:, c, :],
                                         ring[:, (8 + c) * PIECE + n * NCH:(8 + c) * PIECE + (n + 1) * NCH],
                                         start=c == 0, stop=c == 3)
                    last.then_inc(piece_used, 1)
                    if pair is not None:
                        scatter(pair, 2 * c)
                        scatter(pair, 2 * c + 1)

            def pair_of_experts(pair, first=False, last_of_round=False):
                done = 2 * pair
                gate_up(done)
                pe.wait_ge(dispw_ready, 2 * pair + 2)
                for tau in range(T):
                    last = pe.transpose(bank[2][:, tau * 128:(tau + 1) * 128],
                                        dispw[:, tau, :, :].rearrange("p u s -> p (u s)"), ident)
                last.then_inc(dT_done, 1)
                gather(done + 1)
                turn_hidden(done)
                down(done, None if first else pair - 1)
                gate_up(done + 1)
                if not last_of_round:
                    gather(done + 2)
                turn_hidden(done + 1)
                down(done + 1)

            def one_round(r):
                gather(r * NE)
                pair_of_experts(r * NE // 2, first=True)
                with pe.Fori(1, NE // 2 - 1) as i:
                    pair_of_experts(i + r * NE // 2)
                pair_of_experts((r + 1) * NE // 2 - 1, last_of_round=True)
                for k in range(8):
                    scatter((r + 1) * NE // 2 - 1, k)

            one_round(0)
            pe.wait_ge(pos_ready, 2)
            most = pe.value_load(cnt_i[0:1, 0:1], min_val=0, max_val=SEQ)
            with pe.If(most > SLOTS):
                for r in range(1, ROUNDS):
                    one_round(r)

        @block.scalar
        def _(act):
            act.dma_start(cst[:, 0:128], consts[:, 0:128]).then_inc(ident_loaded, 16)
            act.dma_start(gain[:, 0:KC], attn_norm[0].rearrange("(p c) -> p c", p=P)).then_inc(ident_loaded, 16)
            act.wait_ge(ident_loaded, 32)
            link(act, "act", act.activation(stat[:, 5:6], ident[:, 0:1], ACT.Copy))

            def squares(src, n, junk):
                link(act, "act", act.activation(junk, src[:, 0, :], ACT.Square, accum_out=stat[:, 0:1]))
                act.activation(junk, src[:, 1, :], ACT.Square, accum_out=stat[:, 1:2]).then_inc(sq_ready, 1)

            for n in range(8):
                act.wait_ge(turned_used, n + 1)
                c, t = x_block(n)
                act.activation(XH[:, c, t], XT[:, c, t], ACT.Copy).then_inc(xh_ready, 1)
            for n in range(3):
                split_act(act, n)
            link(act, "act", act.activation(proj[:, 0:D], XN[:, 0, :], ACT.Square, accum_out=stat[:, 2:3]))
            act.activation(proj[:, 0:D], XN[:, 1, :], ACT.Square, accum_out=stat[:, 3:4]).then_inc(sq_ready, 1)
            rms_act(act, 0, stat[:, 2:4])

            def save(q):
                ch = ORDER[q]
                if ch == GATE_CH:
                    act.wait_ge(gate_cols_done, 1)
                else:
                    act.wait_ge(piece_used, first_piece(q) + PP)
                width = 48 if ch == GATE_CH else NCH
                link(act, "act", act.activation(PJ[:, 0, ch * NCH:ch * NCH + width], proj_bank(q, 0)[:, 0:width], ACT.Copy,
                                          scale=stat[:, 2:3]))
                act.activation(PJ[:, 1, ch * NCH:ch * NCH + width], proj_bank(q, 1)[:, 0:width],
                               ACT.Copy, scale=stat[:, 3:4]).then_inc(proj_saved, 1)

            for n in range(EARLY * PP):
                if n + 3 < EARLY * PP:
                    split_act(act, n + 3)
                q, i = divmod(n, PP)
                if i < PP - 1:
                    continue
                if q == 0:
                    act.wait_ge(x_rstd, 1)
                save(q)
                if q == 0:
                    act.wait_ge(lb_in, 1)
                    act.activation(lbl, lbl, ACT.Exp).then_inc(lb_exp, 1)
                elif q == 1:
                    act.wait_ge(proj_saved, 2)
                    for tau in range(T):
                        act.activation(PJ[:, tau, HF0:HF0 + HG], PJ[:, tau, HF0:HF0 + HG], ACT.Sigmoid).then_inc(sig_ready, 1)
                elif q == 2:
                    for tau in range(T):
                        act.wait_ge(f_ready, tau + 1)
                        act.activation(LF[:, tau, :], LF[:, tau, :], ACT.Ln).then_inc(lf_ready, 1)

            def save_late(place):
                for what, q, i in late_pieces(place):
                    if what == "cmp":
                        if i == 1:
                            act.wait_ge(piece_used, CMP_PIECE + 2 * (q + 1))
                            act.activation(hid[q][0:60, :], bank[q][0:60, 0:256], ACT.Gelu_apprx_tanh).then_inc(hid_ready, 1)
                    elif i == PP - 1 or ORDER[q] == GATE_CH:
                        save(q)
                for j, (at, kind, which) in enumerate(SIDE):
                    if at == place and (kind, which) != ("w2", 1):
                        side_save(j, kind, which)

            def side_save(j, kind, which):
                act.wait_ge(side_done, j + 1)
                b = bank[2 + j % 2]
                pairs = []
                scale = 1.0
                if kind == "pos":
                    pairs.append((posT[:, :, :].rearrange("p n m -> p (n m)"), b[:, 0:32]))
                elif kind == "kv":
                    bv = b[:, :].rearrange("p (a t) -> p a t", a=2)
                    v = kvT[which].rearrange("p (a two) t -> p a two t", two=2)
                    for two in range(2):
                        rows = slice(64 * two, 64 * two + 64)
                        pairs.append((v[0:64, :, two, :], bv[rows, :, :]))
                        pairs.append((v[64:128, :, two, 0:SEQ - 1], bv[rows, :, 1:SEQ]))
                elif kind in ("qu", "qr"):
                    tau, half = which
                    scale = DK ** -0.5
                    pairs.append(((qUT if kind == "qu" else qRT)[:, 4 * half:4 * half + 4, tau * P:(tau + 1) * P],
                                  b[:, :].rearrange("p (a t) -> p a t", a=4)))
                elif kind == "kr":
                    br, tau = which
                    act.wait_ge(zeros_ready, 2 if br else 4)
                    bv = b[:, :].rearrange("p (g t) -> p g t", g=4)
                    for z in range(2):
                        rows = slice(64 * z, 64 * z + 64)
                        pairs.append((kRT[br][rows, z, :, tau * P:(tau + 1) * P], bv[rows, :, :]))
                elif kind == "hid":
                    act.wait_ge(cmp_zeroed, 1)
                    hb = b[:, 0:128].rearrange("p (f x) -> p f x", f=2)
                    if which == 0:
                        pairs.append((hidT[:, :, 0:60], hb[:, :, 0:60]))
                    else:
                        for o in range(2):
                            for f in range(2):
                                src = hb[:, f, 0:60].rearrange("p (g n) -> p g n", g=4)[:, 2 * o:2 * o + 2, :]
                                pairs.append((hrep[:, o, f, :, :, 0:NCMP], src.unsqueeze(2).to_broadcast([P, 2, 4, NCMP])))
                else:
                    act.wait_ge(cmp_zeroed, 2)
                    for z in range(2):
                        rows = slice(64 * z, 64 * z + 64)
                        pairs.append((kcz[rows, z, 0:60], b[rows, 0:60]))
                for dst, src in pairs[:-1]:
                    link(act, "act", act.activation(dst, src, ACT.Copy, scale=scale))
                act.activation(pairs[-1][0], pairs[-1][1], ACT.Copy, scale=scale).then_inc(side_saved, 1)

            place = 0
            for hg in range(2):
                for tau in range(T):
                    act.wait_ge(qk_turned, 4 * hg + tau + 1)
                    if hg:
                        act.wait_ge(gram_done, len(STEPS))
                        act.wait_ge(pair_ready, pairs_upto(0, len(STEPS) - 1))
                    act.activation(qT[:, :, tau * P:(tau + 1) * P], bank[2 + tau][:, :].rearrange("p (h t) -> p h t", h=4),
                                   ACT.Copy, scale=128.0 ** -0.5).then_inc(q_copied, 1)

                def decays(n):
                    kind, tau, lv = STEPS[n]
                    if kind == "diag":
                        return
                    for u in range(2 if kind == "cross" else 1):
                        act.wait_ge(expo_done, decays_upto(hg, n) - (1 - u if kind == "cross" else 0))
                        b = u if kind == "cross" else n % 2
                        if hg or n >= 2:
                            act.wait_ge(pair_ready, pairs_upto(hg, n - 1) if kind == "cross" or n < 2 else pairs_upto(hg, n - 2))
                        act.activation(decay[b], bank[4 + b][:, :], ACT.Exp).then_inc(decay_ready, 1)

                save_late(place)
                place += 1
                decays(0)
                for n in range(len(STEPS)):
                    if n + 1 < len(STEPS):
                        decays(n + 1)
                    save_late(place)
                    place += 1
                for tau in range(T):
                    act.wait_ge(hg_copied, 2 * hg + tau + 1)
                    if 2 * hg + tau:
                        act.wait_ge(hg_saved, 2 * hg + tau)
                    act.activation(sqt, PJ[:, tau, HQ0 + 512 * hg:HQ0 + 512 * hg + 512], ACT.Square).then_inc(hg_sq, 1)
            act.wait_ge(hg_ms, 1)
            act.activation(rst, rst, ACT.Sqrt).then_inc(hg_root, 1)
            act.wait_ge(sc_in, 1)
            act.activation(sc, sc, ACT.Exp).then_inc(sc_exp, 1)
            for what, q, i in TAIL:
                if i == PP - 1 or ORDER[q] == GATE_CH:
                    save(q)
            act.wait_ge(proj_saved, IN_CH + 1)
            act.activation(gates[:, :, :, :].rearrange("p t h b -> p t (h b)"), PJ[:, :, GR0:GR0 + 48],
                           ACT.Sigmoid).then_inc(gates_ready, 1)
            for tau in range(T):
                act.activation(PJ[:, tau, HG0:HG0 + HG], PJ[:, tau, HG0:HG0 + HG], ACT.Silu).then_inc(silu_ready, 1)

            def exponentials(u):
                br, g, tau = UNITS[u]
                act.wait_ge(s_max, u + 1)
                if u >= 2:
                    act.wait_ge(pT_done, u - 1)
                n = 128 * (tau + 1)
                for i in range(2):
                    for half in range(2):
                        h = 2 * i + half
                        act.activation(prob[u % 2][:, h, 0:n], bank[2 * (u % 2) + i][:, half * n:(half + 1) * n], ACT.Exp,
                                       bias=nmx[:, 4 * (u % 2) + h:4 * (u % 2) + h + 1],
                                       accum_out=sums[:, 4 * (u % 2) + h:4 * (u % 2) + h + 1]).then_inc(p_ready, 1)

            exponentials(0)
            split_y_act(act, 0)
            for u, (br, g, tau) in enumerate(UNITS):
                if u + 1 < len(UNITS):
                    exponentials(u + 1)
                if tau:
                    act.wait_ge(pT_done, u + 1)
                    if u >= 2:
                        act.wait_ge(o_done, u - 1)
                    act.activation(probT[u % 2][:, 4:8, :], bank[5][:, :].rearrange("p (h s) -> p h s", h=4),
                                   ACT.Copy).then_inc(pT_ready_b, 1)
                if u % 4 == 0:
                    for k in range(2):
                        split_act(act, EARLY * PP + u // 2 + k)
            act.wait_ge(o_used, len(UNITS))
            link(act, "act", act.activation(scr[:, 0:HG], YN[:, 0, :], ACT.Square, accum_out=y_stat[:, 0:1]))
            act.activation(scr[:, 0:HG], YN[:, 1, :], ACT.Square, accum_out=y_stat[:, 1:2]).then_inc(sq_ready, 1)
            split_act(act, EARLY * PP + 8)
            split_y_act(act, 1)
            rms_act(act, 1, y_stat)
            for k in range(9, 16):
                split_act(act, EARLY * PP + k)
            most_cols = D - NCH
            for first, c, k in ((0, slice(0, most_cols), 0), (most_cols, slice(most_cols, D), 2)):
                act.wait_ge(out_saved, 2 * OUT_CH if first else 2 * (OUT_CH - 1))
                for tau in range(T):
                    ins = act.activation(xt[:, c], X2[:, tau, c], ACT.Square, accum_out=stat[:, k + tau:k + tau + 1])
                    if first and tau:
                        ins.then_inc(sq_ready, 1)
                    else:
                        link(act, "act", ins)
            rms_act(act, 2, stat[:, 0:2])
            act.wait_ge(r_in, 1)
            act.activation(r8[:, 0:8], r8[:, 0:8], ACT.Exp).then_inc(r_exp, 1)
            act.wait_ge(rstd_ready, 1)
            for tau in range(T):
                act.activation(XS[:, tau, :], X2[:, tau, :], ACT.Copy, scale=stat[:, tau:tau + 1]).then_inc(nat_ready, 1)
            act.wait_ge(r_in, 2)
            act.activation(r8[:, 8:10], r8[:, 8:10], ACT.Exp).then_inc(r_exp, 1)

            def hidden(done):
                act.wait_ge(piece_used, done * EP + (MOE_PIECE + 8))
                act.activation(hs[64:128, :], bank[3][0:64, :], ACT.Silu).then_inc(silu_done, 1)
                act.wait_ge(hT_done, done + 1)
                act.activation(hT.rearrange("p c s -> p (c s)"), bank[2][:, 256:512], ACT.Copy).then_inc(hT_saved, 1)

            def outputs(done, u):
                act.wait_ge(piece_used, done * EP + (MOE_PIECE + EP))
                for n in range(2):
                    act.activation(yb[64 * u:64 * u + 64, n * NCH:(n + 1) * NCH], bank[4][64 * n:64 * n + 64, :],
                                   ACT.Copy).then_inc(y_saved_a, 1)

            def pair_of_experts(pair, first):
                hidden(2 * pair)
                if not first:
                    act.wait_ge(scat_done, 8 * pair)
                act.wait_ge(dT_done, pair + 1)
                act.activation(dispT.rearrange("p t q -> p (t q)"), bank[2][:, 0:256], ACT.Copy).then_inc(dT_saved, 1)
                outputs(2 * pair, 0)
                hidden(2 * pair + 1)
                outputs(2 * pair + 1, 1)

            def one_round(r):
                if r:
                    act.wait_ge(scat_done, 4 * NE * r)
                pair_of_experts(r * NE // 2, True)
                with act.Fori(1, NE // 2) as i:
                    pair_of_experts(i + r * NE // 2, False)

            one_round(0)
            act.wait_ge(pos_ready, 2)
            most = act.value_load(cnt_i[0:1, 0:1], min_val=0, max_val=SEQ)
            with act.If(most > SLOTS):
                for r in range(1, ROUNDS):
                    one_round(r)
            act.wait_ge(experts_done, 1)
            for tau in range(T):
                act.activation(xt[:, 0:D], X2[:, tau, :], ACT.Square, accum_out=stat[:, 2 * tau:2 * tau + 1]).then_inc(sq_ready, 1)
                rms_act(act, 3 + tau, stat[:, 2 * tau:2 * tau + 1])

        @block.vector
        def _(dve):
            def run(ins):
                link(dve, "dve", ins)

            rstd = stat[:, 0:2]
            dve.wait_ge(ident_loaded, 32)
            front = [bank[n] for n in range(4)]
            turn_dve(dve, 0, D, 0, 0, front)
            for n in range(4, 8):
                c, t = x_block(n)
                dve.wait_ge(xh_ready, n + 1)
                dve.tensor_tensor(XL[:, c, t], XT[:, c, t], XH[:, c, t].bitcast(F32), ALU.subtract).then_inc(xl_ready, 1)

            def lower_bound_logits():
                dve.wait_ge(lb_loaded, 16)
                run(dve.tensor_tensor(LB, lbl[:, 0, :], lbl[:, 1, :], ALU.max))
                dve.tensor_tensor(lbl[:, 0, :], lbl[:, 0, :], LB, ALU.subtract).then_inc(dve_chain, 1)
                chain_value["dve"] += 1
                dve.tensor_tensor(lbl[:, 1, :], lbl[:, 1, :], LB, ALU.subtract).then_inc(lb_in, 1)

            def lower_bound():
                dve.wait_ge(lb_exp, 1)
                run(dve.tensor_tensor(OMLB, lbl[:, 0, :], lbl[:, 1, :], ALU.add))
                run(dve.reciprocal(OMLB, OMLB))
                run(dve.tensor_tensor(LB, lbl[:, 0, :], OMLB, ALU.mult))
                run(dve.tensor_tensor(OMLB, lbl[:, 1, :], OMLB, ALU.mult))

            def forget(tau):
                f = PJ[:, tau, HF0:HF0 + HG]
                dve.wait_ge(sig_ready, tau + 1)
                run(dve.tensor_tensor(LF[:, tau, :], f, OMLB, ALU.mult))
                run(dve.tensor_tensor(LF[:, tau, :], LF[:, tau, :], LB, ALU.add))
                dve.tensor_scalar(f, LF[:, tau, :], -1.0, 1.0, ALU.mult, ALU.add).then_inc(f_ready, 1)

            for n in range(EARLY * PP):
                split_dve(dve, n)
                if n == 2:
                    rms_dve(dve, 0, stat[:, 2:4], D, stat[:, 2:4])
                    dve.memset(stat[:, 4:5], 0.0).then_inc(x_rstd, 1)
                elif n == 6:
                    lower_bound_logits()
                elif n == 8:
                    lower_bound()
                elif n in (10, 11):
                    forget(n - 10)

            def side(place):
                if place == 1:
                    run(dve.memset(hrep, 0.0))
                    dve.memset(sc, 0.0).then_inc(cmp_zeroed, 1)
                elif 8 <= place < 12:
                    n, i = divmod(place - 8, 2)
                    dve.wait_ge(side_saved, side_of("kv", n) + 1)
                    src = kvT[n].rearrange("p g (b m two) -> p m g b two", m=8, two=2)[:, :, :, i:i + NCMP, 0]
                    pos = posT[:, n, 8 * i:8 * i + 8].unsqueeze(2).unsqueeze(3).to_broadcast([P, 8, NG, NCMP])
                    for g in range(NG):
                        ins = dve.tensor_tensor(flat[n][:, 8 * i:8 * i + 8, g, :], src[:, :, g, :], pos[:, :, g, :], ALU.add)
                        if i == 1 and g == NG - 1:
                            ins.then_inc(flat_ready, 1)
                        else:
                            run(ins)
                elif 22 <= place < 26:
                    tau, half = divmod(place - 22, 2)
                    dve.wait_ge(proj_saved, CMP_AT)
                    cos = cst[:, C_COS + tau * 32:C_COS + tau * 32 + 32].unsqueeze(1).to_broadcast([P, NH, 32])
                    sin = cst[:, C_SIN + tau * 32:C_SIN + tau * 32 + 32].unsqueeze(1).to_broadcast([P, NH, 32])
                    q4 = PJ[:, tau, NQ0:NQ0 + NH * DK].rearrange("p (h a d) -> p h a d", h=NH, a=2)
                    dq = QR[:, tau, :].rearrange("p (h a d) -> p h a d", h=NH, a=2)
                    qt = tmp.rearrange("p (h d) -> p h d", h=NH)
                    run(dve.tensor_tensor(dq[:, :, half, :], q4[:, :, half, :], cos, ALU.mult))
                    run(dve.tensor_tensor(qt, q4[:, :, 1 - half, :], sin, ALU.mult))
                    last = dve.tensor_tensor(dq[:, :, half, :], dq[:, :, half, :], qt, ALU.add if half else ALU.subtract)
                    if place == 25:
                        last.then_inc(q_roped, 1)
                        dve.wait_ge(q_roped, 1)
                    else:
                        run(last)
                elif place == 26:
                    dve.wait_ge(piece_used, CMP_PIECE + 2)
                    dve.memset(kcz, 0.0).then_inc(cmp_zeroed, 1)
                elif place == 34:
                    j = side_of("w2", 1)
                    dve.wait_ge(side_done, j + 1)
                    for o in range(2):
                        ins = dve.tensor_tensor(vbd[:, o, :, :],
                                                bank[2 + j % 2][:, o * 64:o * 64 + 64].unsqueeze(1).to_broadcast([P, 8, DK]),
                                                cst[:, C_BD:C_BD + 8].unsqueeze(2).to_broadcast([P, 8, DK]), ALU.mult)
                        if o:
                            ins.then_inc(cmp_ready, 1)
                        else:
                            run(ins)

            dve.wait_ge(cst_loaded, CST_LOADS)
            for hg in range(2):
                for tau in range(T):
                    dve.wait_ge(qk_turned, 4 * hg + 2 + tau + 1)
                    dve.tensor_copy(kT[:, :, tau * P:(tau + 1) * P],
                                    bank[2 + tau][:, :].rearrange("p (h t) -> p h t", h=4)).then_inc(k_copied, 1)
                dve.wait_ge(k_copied, 2 * (hg + 1))
                dve.wait_ge(q_copied, 2 * (hg + 1))

                def decayed(n):
                    kind, tau, lv = STEPS[n]
                    if kind == "diag":
                        return
                    dve.wait_ge(decay_ready, decays_upto(hg, n))
                    if hg or n >= 2:
                        dve.wait_ge(gram_done, hg * len(STEPS) + max(n - 1, 0))
                    if kind == "cross":
                        v = [pair[i].rearrange("p (h t) -> p h t", h=4) for i in range(2)]
                        d = [decay[i].rearrange("p (h t) -> p h t", h=4) for i in range(2)]
                        dve.tensor_tensor(v[0], d[0], qT[:, :, P:2 * P], ALU.mult).then_inc(pair_ready, 1)
                        dve.tensor_tensor(v[1], d[1], kT[:, :, 0:P], ALU.mult).then_inc(pair_ready, 1)
                        return
                    w = LEVELS[lv]

                    def halves(a, side):
                        return a.rearrange("p (b two w) -> p b two w", two=2, w=w)[:, :, side, :]

                    for side, src in ((1, qT), (0, kT)):
                        if w == 64:
                            s_ = src[:, :, tau * P + 64 * side:tau * P + 64 * side + 64]
                            dve.tensor_tensor(halves(pair[n % 2], side), halves(decay[n % 2], side), s_,
                                              ALU.mult).then_inc(pair_ready, 1)
                        else:
                            s_ = src[:, :, tau * P:(tau + 1) * P].rearrange("p h (b two w) -> p h b two w", two=2, w=w)[:, :, :, side, :]
                            v, d = (a.rearrange("p (h b two w) -> p h b two w", h=4, two=2, w=w)[:, :, :, side, :]
                                    for a in (pair[n % 2], decay[n % 2]))
                            dve.tensor_tensor(v, d, s_, ALU.mult).then_inc(pair_ready, 1)

                def masked(n):
                    kind, tau, lv = STEPS[n]
                    g = hg * len(STEPS) + n
                    dve.wait_ge(gram_done, g + 1)
                    b = bank[6 + g % 2][:, :].rearrange("p (h t) -> p h t", h=4)
                    if kind == "cross":
                        dve.tensor_copy(att[2], bank[6 + g % 2][:, :]).then_inc(gram_used, 1)
                        return
                    m = B_GM + (lv if kind == "level" else NL) * 128
                    first = kind == "level" and lv == 0
                    if first and hg:
                        dve.wait_ge(hg_out, 2)
                    if not first:
                        adds = sum(1 for s in STEPS[:max(n - 1, 0)] if not (s[0] == "cross" or (s[0] == "level" and s[2] == 0)))
                        if hg * ADDS + adds:
                            dve.wait_ge(part_added, hg * ADDS + adds)
                    elif hg:
                        dve.wait_ge(part_added, hg * ADDS)
                    dst = (att[tau] if first else part[n % 2]).rearrange("p (h t) -> p h t", h=4)
                    dve.tensor_tensor(dst, b, cbf[:, m:m + 128].unsqueeze(1).to_broadcast([P, 4, P]),
                                      ALU.mult).then_inc(gram_used, 1)

                decayed(0)
                for n in range(len(STEPS)):
                    if n + 1 < len(STEPS):
                        decayed(n + 1)
                    masked(n)
                    side(hg * (len(STEPS) + 1) + 1 + n)
                for tau in range(T):
                    dve.wait_ge(hg_out, 2 * hg + tau + 1)
                    dve.tensor_copy(PJ[:, tau, HQ0 + 512 * hg:HQ0 + 512 * hg + 512], bank[2 + tau][:, :]).then_inc(hg_copied, 1)
                    dve.wait_ge(hg_sq, 2 * hg + tau + 1)
                    dve.tensor_reduce(rst[:, tau * 8 + 4 * hg:tau * 8 + 4 * hg + 4],
                                      sqt.rearrange("p (h v) -> p h v", h=4), AX, ALU.add).then_inc(hg_saved, 1)
            dve.wait_ge(hg_saved, 4)
            dve.tensor_scalar(rst, rst, 1.0 / 128, EPS, ALU.mult, ALU.add).then_inc(hg_ms, 1)
            cm = cst[:, C_CM:C_CM + 32].rearrange("p (t n) -> p t n", t=T)
            cn = cst[:, C_CN:C_CN + 32].rearrange("p (t n) -> p t n", t=T)
            dve.wait_ge(sc_done, 1)
            for tau in range(T):
                b = bank[4][:, tau * 256:tau * 256 + 256].rearrange("p (h n) -> p h n", h=NH)[:, :, 0:NCMP]
                run(dve.tensor_tensor(sc[:, tau, :, 0:NCMP], b,
                                      cm[:, tau, 0:NCMP].unsqueeze(1).to_broadcast([P, NH, NCMP]), ALU.mult))
                run(dve.tensor_tensor(sc[:, tau, :, 0:NCMP], sc[:, tau, :, 0:NCMP],
                                      cn[:, tau, 0:NCMP].unsqueeze(1).to_broadcast([P, NH, NCMP]), ALU.add))
            mx = tmp[:, 0:32].rearrange("p (t h) -> p t h", t=T)
            sm = tmp[:, 32:64].rearrange("p (t h) -> p t h", t=T)
            run(dve.tensor_reduce(mx, sc[:, :, :, 0:NCMP], AX, ALU.max))
            for tau in range(T):
                ins = dve.tensor_tensor(sc[:, tau, :, 0:NCMP], sc[:, tau, :, 0:NCMP],
                                        mx[:, tau, :].unsqueeze(2).to_broadcast([P, NH, NCMP]), ALU.subtract)
                if tau:
                    ins.then_inc(sc_in, 1)
                else:
                    run(ins)
            dve.wait_ge(sc_exp, 1)
            for tau in range(T):
                run(dve.tensor_tensor(sc[:, tau, :, :], sc[:, tau, :, :], cm[:, tau, :].unsqueeze(1).to_broadcast([P, NH, 16]), ALU.mult))
            run(dve.tensor_reduce(sm, sc, AX, ALU.add))
            for tau in range(T):
                run(dve.tensor_scalar(sm[:, tau, :], sm[:, tau, :], cst[:, C_NV + tau:C_NV + tau + 1], None, ALU.add))
            run(dve.reciprocal(sm, sm))
            for tau in range(T):
                ins = dve.tensor_tensor(sc[:, tau, :, :], sc[:, tau, :, :], sm[:, tau, :].unsqueeze(2).to_broadcast([P, NH, 16]), ALU.mult)
                if tau:
                    ins.then_inc(pc_ready, 1)
                else:
                    run(ins)
            dve.wait_ge(pcT_done, 1)
            dve.tensor_copy(pcT.rearrange("p t o q -> p (t o q)"), bank[5][:, :]).then_inc(pcT_ready, 1)
            dve.wait_ge(gates_ready, 1)
            for tau in range(T):
                for o in range(2):
                    dve.wait_ge(oc_done, 2 * tau + o + 1)
                    dve.tensor_tensor(YN[:, tau, 512 * o:512 * o + 512].rearrange("p (h d) -> p h d", h=8),
                                      bank[4 + o][:, :].rearrange("p (h d) -> p h d", h=8),
                                      gates[:, tau, 8 * o:8 * o + 8, 0].unsqueeze(2).to_broadcast([P, 8, DK]),
                                      ALU.mult).then_inc(oc_used, 1)
            dve.wait_ge(oc_used, 4)

            def save_out0(j):
                dve.wait_ge(res_loaded, 32)
                ch, tt = OUT0[j]
                if tt:
                    dve.wait_ge(piece_used, OUT_PIECE + 2 * (ch + 1))
                else:
                    dve.wait_ge(out0_done, ch + 1)
                r = XR[:, tt, ch * NCH:(ch + 1) * NCH]
                dve.tensor_tensor(r, r, bank[6][:, :], ALU.add).then_inc(out0_saved, 1)

            def maxima(u):
                br, g, tau = UNITS[u]
                n = 128 * (tau + 1)
                dve.wait_ge(s_done, u + 1)
                m = nmx[:, 4 * (u % 2):4 * (u % 2) + 4].rearrange("p (i half) -> p i half", half=2)
                for i in range(2):
                    run(dve.tensor_reduce(m[:, i, :], bank[2 * (u % 2) + i][:, 0:2 * n].rearrange("p (z s) -> p z s", z=2),
                                          AX, ALU.max))
                dve.tensor_scalar(nmx[:, 4 * (u % 2):4 * (u % 2) + 4], nmx[:, 4 * (u % 2):4 * (u % 2) + 4], -1.0, None,
                                  ALU.mult).then_inc(s_max, 1)

            dve.wait_ge(hg_root, 1)
            run(dve.reciprocal(rst, rst))
            dve.wait_ge(silu_ready, 2)
            for tau in range(T):
                o = PJ[:, tau, 0:HG].rearrange("p (h v) -> p h v", h=HH)
                run(dve.tensor_tensor(o, o, rst[:, tau * 8:tau * 8 + 8].unsqueeze(2).to_broadcast([P, HH, 128]), ALU.mult))
                dve.wait_ge(dve_chain, chain_value["dve"])
                dve.tensor_tensor(PJ[:, tau, 0:HG], PJ[:, tau, 0:HG], PJ[:, tau, HG0:HG0 + HG],
                                  ALU.mult).then_inc(hg_final, 1)

            maxima(0)
            turn_dve(dve, 8, HG, 0, 1, [bank[6], bank[7]])
            maxima(1)

            for u in range(len(UNITS) + 1):
                if u < len(UNITS):
                    br, g, tau = UNITS[u]
                    dve.wait_ge(pT_done, u + 1)
                    if u >= 2:
                        dve.wait_ge(o_done, u - 1)
                    dve.tensor_copy(probT[u % 2][:, 0:4, :], bank[4][:, :].rearrange("p (h s) -> p h s", h=4)
                                    ).then_inc(pT_ready, 1)
                    dve.wait_ge(p_ready, 4 * (u + 1))
                    su = sums[:, 4 * (u % 2):4 * (u % 2) + 4]
                    sg = sums[:, 8 + 4 * (u % 2):12 + 4 * (u % 2)]
                    run(dve.reciprocal(sg, su))
                    run(dve.tensor_tensor(sg, sg, gates[:, tau, 4 * g:4 * g + 4, 1 + br], ALU.mult))
                    if u + 2 < len(UNITS):
                        maxima(u + 2)
                if u:
                    br, g, tau = UNITS[u - 1]
                    sg = sums[:, 8 + 4 * ((u - 1) % 2):12 + 4 * ((u - 1) % 2)]
                    dve.wait_ge(o_done, u)
                    t4 = tmp[:, 0:256].rearrange("p (h d) -> p h d", h=4)
                    run(dve.tensor_tensor(t4, bank[7][:, 0:256].rearrange("p (h d) -> p h d", h=4),
                                          sg.unsqueeze(2).to_broadcast([P, 4, DK]), ALU.mult))
                    y = YN[:, tau, 256 * g:256 * g + 256]
                    dve.tensor_tensor(y, y, tmp[:, 0:256], ALU.add).then_inc(o_used, 1)
                    dve.wait_ge(o_used, u)
                if u < len(UNITS) and u % 4 == 0:
                    for k in range(2):
                        split_dve(dve, EARLY * PP + u // 2 + k)
                for j, at in enumerate(OUT0_AFTER):
                    if at == u < len(UNITS):
                        save_out0(j)
            save_out0(len(OUT0) - 1)
            dve.wait_ge(out0_saved, len(OUT0))
            turn_dve(dve, 12, NH * DK, 8, 1, front)
            split_dve(dve, EARLY * PP + 8)
            rms_dve(dve, 1, y_stat, NH * DK, y_stat)
            split_dve(dve, EARLY * PP + 9)

            dve.wait_ge(turned, 16)
            def save_turned(ch):
                for tau in range(T):
                    dve.wait_ge(x2_turned, 2 * ch + tau + 1)
                    dve.tensor_tensor(RT[:, 4 * ch:4 * ch + 4, tau * P:(tau + 1) * P],
                                      bank[4 + tau][:, :].rearrange("p (c t) -> p c t", c=4),
                                      rgain[:, 4 * ch:4 * ch + 4].unsqueeze(2).to_broadcast([P, 4, P]),
                                      ALU.mult).then_inc(x2_saved, 1)

            dve.wait_ge(rgain_loaded, 16)
            for ch in range(OUT_CH):
                for k in range(10 + 2 * ch, min(12 + 2 * ch, 16)):
                    split_dve(dve, EARLY * PP + k)
                dve.wait_ge(piece_used, OUT_PIECE + 8 + 2 * (ch + 1))
                for tau in range(T):
                    c = slice(ch * NCH, (ch + 1) * NCH)
                    dve.scalar_tensor_tensor(X2[:, tau, c], bank[2 * (ch % 2) + tau][:, :], y_stat[:, tau:tau + 1],
                                             XR[:, tau, c], ALU.mult, ALU.add).then_inc(out_saved, 1)
                if ch:
                    save_turned(ch - 1)
            save_turned(OUT_CH - 1)
            dve.wait_ge(sq_ready, 3)
            run(dve.tensor_tensor(stat[:, 0:2], stat[:, 0:2], stat[:, 2:4], ALU.add))
            rms_dve(dve, 2, stat[:, 0:2], D, rstd)
            dve.memset(ones, 1.0).then_inc(rstd_ready, 1)
            dve.wait_ge(rstd_ready, 1)

            dve.wait_ge(route_loaded, 64)
            dve.wait_ge(logit_done, 1)
            for tau in range(T):
                run(dve.scalar_tensor_tensor(LG[:, tau, :], bank[6 + tau][:, 0:36], rstd[:, tau:tau + 1], rbias,
                                             ALU.mult, ALU.add))
            w = r8
            lg, le = LG[:, :, 0:4], LG[:, :, 4:36]
            col = [w[:, 10 + 2 * n:12 + 2 * n] for n in range(14)]
            m1, gw, mxi, v1, v2, ex, p1, p2 = col[:8]

            def wide(a, n):
                return a.unsqueeze(2).to_broadcast([P, T, n])

            ohg = w[:, 40:48].rearrange("p (t n) -> p t n", t=T)
            ohb = w[:, 48:56].rearrange("p (t n) -> p t n", t=T)
            eg = w[:, 0:8].rearrange("p (t n) -> p t n", t=T)
            oh1, oh2 = (scr[:, 512 + 64 * n:576 + 64 * n].rearrange("p (t n) -> p t n", t=T) for n in range(2))

            def first_max(dst, src, m, n, rev):
                run(dve.tensor_reduce(m, src, AX, ALU.max))
                run(dve.tensor_tensor(dst, src, wide(m, n), ALU.is_ge))
                run(dve.tensor_tensor(dst, dst, rev.unsqueeze(1).to_broadcast([P, T, n]), ALU.mult))
                run(dve.tensor_reduce(mxi, dst, AX, ALU.max))
                run(dve.tensor_tensor(dst, dst, wide(mxi, n), ALU.is_equal))

            first_max(ohg, lg, m1, 4, cst[:, C_REV:C_REV + 4])
            dve.tensor_tensor(eg, lg, wide(m1, 4), ALU.subtract).then_inc(r_in, 1)
            dve.wait_ge(r_exp, 1)
            run(dve.tensor_reduce(gw, eg, AX, ALU.add))
            run(dve.reciprocal(gw, gw))
            run(dve.tensor_scalar(ohb, ohg, NEG, -NEG, ALU.mult, ALU.add))
            for tau in range(T):
                e4 = LG[:, tau, 4:36].rearrange("p (g e) -> p g e", g=4)
                run(dve.tensor_tensor(e4, e4, ohg[:, tau, :].unsqueeze(2).to_broadcast([P, 4, 8]), ALU.mult))
                run(dve.tensor_tensor(e4, e4, ohb[:, tau, :].unsqueeze(2).to_broadcast([P, 4, 8]), ALU.add))
            first_max(oh1, le, v1, 32, cst[:, C_REV + 4:C_REV + 36])
            run(dve.scalar_tensor_tensor(le, oh1, -3.0 * NEG, le, ALU.mult, ALU.add))
            first_max(oh2, le, v2, 32, cst[:, C_REV + 4:C_REV + 36])
            ed = w[:, 8:10]
            dve.tensor_tensor(ed, v2, v1, ALU.subtract).then_inc(r_in, 1)
            dve.wait_ge(r_exp, 2)
            run(dve.tensor_scalar(p1, ed, 1.0, None, ALU.add))
            run(dve.reciprocal(p1, p1))
            run(dve.tensor_tensor(p1, p1, gw, ALU.mult))
            run(dve.tensor_tensor(p2, p1, ed, ALU.mult))
            run(dve.tensor_tensor(wt, oh1, wide(p1, 32), ALU.mult))
            run(dve.tensor_tensor(posm, oh2, wide(p2, 32), ALU.mult))
            run(dve.tensor_tensor(wt, wt, posm, ALU.add))
            dve.tensor_tensor(sel, oh1, oh2, ALU.add).then_inc(sel_ready, 1)
            dve.wait_ge(sel_ready, 1)
            dve.wait_ge(pos_done, 1)
            run(dve.scalar_tensor_tensor(posm, bank[5][:, 0:64].rearrange("p (t n) -> p t n", t=T), 1.0, sel, ALU.add, ALU.mult))
            run(dve.tensor_reduce(mxi[:, 0:1], bank[5][:, 64:96], AX, ALU.max))
            run(dve.tensor_copy(cnt_i[:, 0:1], mxi[:, 0:1]))
            dve.tensor_scalar(posm, posm, -1.0, None, ALU.add).then_inc(pos_ready, 2)
            dve.wait_ge(pos_ready, 2)
            dve.memset(mxi, 0.0).then_inc(scat_used, 2)
            dve.memset(v1, 0.0).then_inc(y_saved_d, 2)

            def dispatch(e, nth, u):
                if not (isinstance(nth, int) and nth == 0):
                    dve.wait_ge(dispw_ready, nth)
                dve.tensor_tensor(disp, cst[:, C_IOTA:C_IOTA + SLOTS].unsqueeze(1).to_broadcast([P, T, SLOTS]),
                                  posm[:, :, bass.ds(e, 1)].to_broadcast([P, T, SLOTS]),
                                  ALU.is_equal).then_inc(disp_ready, 1)
                dve.wait_ge(disp_ready, nth + 1)
                dve.tensor_tensor(dispw[:, :, u, :], disp, wt[:, :, bass.ds(e, 1)].to_broadcast([P, T, SLOTS]),
                                  ALU.mult).then_inc(dispw_ready, 1)

            def save_gather(nth):
                for half in range(2):
                    dve.wait_ge(gath_done, 2 * nth + (half + 1))
                    dve.tensor_tensor(xg[:, 8 * half:8 * half + 8, :], bank[half][:, :].rearrange("p (c s) -> p c s", c=8),
                                      gain[:, 2 * KC + 8 * half:2 * KC + 8 * half + 8].unsqueeze(2).to_broadcast([P, 8, SLOTS]),
                                      ALU.mult).then_inc(gath_saved, 1)

            def hidden(done):
                dve.wait_ge(silu_done, done + 1)
                dve.tensor_tensor(hv[64:128, :], bank[3][64:128, :], hs[64:128, :], ALU.mult).then_inc(h_ready, 1)

            def outputs(done, u):
                dve.wait_ge(piece_used, done * EP + (MOE_PIECE + EP))
                for n in range(2):
                    dve.tensor_copy(yb[64 * u:64 * u + 64, (2 + n) * NCH:(3 + n) * NCH],
                                    bank[5][64 * n:64 * n + 64, :]).then_inc(y_saved_d, 1)

            def add_scatter(pair):
                dve.wait_ge(scat_used, 8 * pair + 2)
                for k in range(8):
                    dve.wait_ge(scat_done, 8 * pair + (k + 1))
                    r = X2[:, k // 4, (k % 4) * NCH:(k % 4 + 1) * NCH]
                    dve.tensor_tensor(r, r, bank[6 + k % 2][:, :], ALU.add).then_inc(scat_used, 1)

            def pair_of_experts(e, pair, first=False, last_of_round=False):
                done = 2 * pair
                dve.wait_ge(gath_done, 2 * done + 2)
                dispatch(e + 1, done + 1, 1)
                hidden(done)
                save_gather(done + 1)
                if not first:
                    add_scatter(pair - 1)
                outputs(done, 0)
                if not last_of_round:
                    dve.wait_ge(dT_done, pair + 1)
                    dispatch(e + 2, done + 2, 0)
                hidden(done + 1)
                if not last_of_round:
                    save_gather(done + 2)
                outputs(done + 1, 1)

            def one_round(r):
                if r:
                    dve.wait_ge(dT_done, r * NE // 2)
                dispatch(0, r * NE, 0)
                save_gather(r * NE)
                pair_of_experts(0, r * NE // 2, first=True)
                with dve.Fori(1, NE // 2 - 1) as i:
                    pair_of_experts(2 * i, i + r * NE // 2)
                pair_of_experts(NE - 2, (r + 1) * NE // 2 - 1, last_of_round=True)
                add_scatter((r + 1) * NE // 2 - 1)

            one_round(0)
            most = dve.value_load(cnt_i[0:1, 0:1], min_val=0, max_val=SEQ)
            with dve.If(most > SLOTS):
                for r in range(1, ROUNDS):
                    dve.tensor_scalar(posm, posm, -1.0 * SLOTS, None, ALU.add).then_inc(pos_ready, 1)
                    dve.wait_ge(pos_ready, 2 + r)
                    one_round(r)
            dve.wait_ge(scat_used, 4 * NE + 2)
            dve.memset(cnt_i[:, 1:2], 0).then_inc(experts_done, 1)
            dve.wait_ge(fin_loaded, 16)
            for tau in range(T):
                r = stat[:, 2 * tau:2 * tau + 1]
                rms_dve(dve, 3 + tau, r, D, r)
                dve.scalar_tensor_tensor(XS[:, tau, :], X2[:, tau, :], r, fgain, ALU.mult, ALU.mult).then_inc(final_ready, 1)


_INS = ["x", "attn_norm", "w_in", "hg_lb_logits", "hg_out_norm", "cmp_pos_k", "cmp_w1_k", "cmp_w2_k", "cmp_pos_v",
        "cmp_w1_v", "cmp_w2_v", "nsa_out_norm", "w_out", "ffn_norm", "moe_w_group", "moe_b_group", "moe_w_router",
        "moe_b_router", "moe_w_gate", "moe_w_up", "moe_w_down", "final_norm"]


def kernel(**inputs):
    import ml_dtypes as _ml
    import concourse.bacc as _bacc
    from concourse.bass_utils import run_bass_kernel_spmd as _run

    nc = _bacc.Bacc("TRN2", target_bir_lowering=False, num_devices=1)
    arrays, args = {}, []
    c, b = tables()
    for name, a in [(n, inputs[n]) for n in _INS] + [("consts", c), ("consts_bf", b.astype(_ml.bfloat16))]:
        a = np.ascontiguousarray(a)
        arrays[f"in_{name}"] = a
        args.append(nc.dram_tensor(f"in_{name}", a.shape, mybir.dt.from_np(a.dtype), kind="ExternalInput").ap())
    args.append(nc.dram_tensor("out_0", (1, SEQ, D), F32, kind="ExternalOutput").ap())
    hybrid_block(nc, *args)
    r = _run(nc, [arrays], core_ids=[0])
    return r.results[0]["out_0"]
```
